# Optimizing a Trainium2 kernel written in Bass

```python
import jax, jax.numpy as jnp
from jax import lax
import numpy as np

D_MODEL = 2048
BATCH = 1
SEQ = 256
DEPTH = 1

CHUNK = 64
N_META = 16
META_PAD = CHUNK - N_META
M_HEADS = 8
M_V = D_MODEL // M_HEADS
M_QK = M_V // 2
A_DH = 64
A_HEADS = D_MODEL // A_DH
A_KV = A_HEADS // 8
A_GROUP = A_HEADS // A_KV
WINDOW = 128
WIN_CHUNKS = WINDOW // CHUNK
D_FF = 256 * ((8 * D_MODEL // 3 + 255) // 256)
CONV_W = 3
EPS = 1e-6
NEG = -1e30
SECTION_SIZES = (M_HEADS * M_QK, M_HEADS * M_QK, M_HEADS * M_V, M_HEADS, M_HEADS, M_HEADS * M_V,
                 A_HEADS * A_DH, A_KV * A_DH, A_KV * A_DH, D_MODEL, D_MODEL)
D_IN = sum(SECTION_SIZES)

kernel_name = 'hybrid_mlstm_swa_sink_convffn'

def rmsnorm(x, g):
    xf = x.astype(jnp.float32)
    y = xf * lax.rsqrt(jnp.mean(xf * xf, axis=-1, keepdims=True) + EPS)
    return (y * g.astype(jnp.float32)).astype(x.dtype)

def split_sections(z):
    out, start = [], 0
    for size in SECTION_SIZES:
        out.append(z[..., start:start + size])
        start += size
    return out

def pad_front(t, value=0.0):
    pad = [(0, 0)] * t.ndim
    pad[1] = (META_PAD, 0)
    return jnp.pad(t, pad, constant_values=value)

def mlstm_chunkwise(q, k, v, i_pre, log_f):
    B, Lp, H, dk = q.shape
    dv = v.shape[-1]
    nc = Lp // CHUNK

    def chunks(t):
        t = t.reshape((B, nc, CHUNK, H) + t.shape[3:])
        return jnp.transpose(t, (1, 0, 3, 2) + tuple(range(4, t.ndim)))

    k = k * dk ** -0.5
    causal = jnp.tril(jnp.ones((CHUNK, CHUNK), dtype=bool))

    def step(carry, xs):
        C, n, m = carry
        qc, kc, vc, ic, fc = xs
        b = jnp.cumsum(fc, axis=-1)
        D = jnp.where(causal, b[..., :, None] - b[..., None, :] + ic[..., None, :], NEG)
        inter = b + m[..., None]
        m_t = jnp.maximum(inter, D.max(-1))
        w_inter = jnp.exp(inter - m_t)
        S = jnp.einsum('bhtd,bhsd->bhts', qc, kc) * jnp.exp(D - m_t[..., None])
        num = jnp.einsum('bhts,bhsv->bhtv', S, vc) + w_inter[..., None] * jnp.einsum('bhvd,bhtd->bhtv', C, qc)
        den = S.sum(-1) + w_inter * jnp.einsum('bhd,bhtd->bht', n, qc)
        h = num / jnp.maximum(jnp.abs(den), jnp.exp(-m_t))[..., None]
        b_end = b[..., -1]
        a = b_end[..., None] - b + ic
        m_new = jnp.maximum(b_end + m, a.max(-1))
        wa = jnp.exp(a - m_new[..., None])
        decay = jnp.exp(b_end + m - m_new)
        C = decay[..., None, None] * C + jnp.einsum('bhs,bhsv,bhsd->bhvd', wa, vc, kc)
        n = decay[..., None] * n + jnp.einsum('bhs,bhsd->bhd', wa, kc)
        return (C, n, m_new), h

    init = (jnp.zeros((B, H, dv, dk), q.dtype), jnp.zeros((B, H, dk), q.dtype), jnp.zeros((B, H), q.dtype))
    _, h = lax.scan(step, init, (chunks(q), chunks(k), chunks(v), chunks(i_pre), chunks(log_f)))
    return jnp.transpose(h, (1, 0, 3, 2, 4)).reshape(B, Lp, H, dv)

def swa_sink_attention(q, k, v, sinks):
    B, Lp, _, dh = q.shape
    nc = Lp // CHUNK
    qc = q.reshape(B, nc, CHUNK, A_KV, A_GROUP, dh)
    kc = k.reshape(B, nc, CHUNK, A_KV, dh)
    vc = v.reshape(B, nc, CHUNK, A_KV, dh)

    def window(t):
        meta = jnp.broadcast_to(t[:, :1, META_PAD:], (B, nc, N_META, A_KV, dh))
        parts = [meta] + [jnp.pad(t, ((0, 0), (j, 0), (0, 0), (0, 0), (0, 0)))[:, :nc]
                          for j in reversed(range(WIN_CHUNKS))]
        return jnp.concatenate(parts, axis=2)

    kw, vw = window(kc), window(vc)
    c = jnp.arange(nc)[:, None]
    off = jnp.arange(CHUNK)[None, :]
    mask_parts = [jnp.broadcast_to(c >= WIN_CHUNKS, (nc, N_META))]
    for j in reversed(range(WIN_CHUNKS)):
        src = c - j
        mask_parts.append((src >= 0) & ((src > 0) | (off >= META_PAD)))
    mask = jnp.concatenate(mask_parts, axis=1)

    s = jnp.einsum('bcqhgd,bckhd->bchgqk', qc, kw).astype(jnp.float32) * dh ** -0.5
    s = jnp.where(mask[None, :, None, None, None, :], s, NEG)
    sink = jnp.broadcast_to(sinks.astype(jnp.float32).reshape(A_KV, A_GROUP)[None, None, :, :, None, None],
                            s.shape[:-1] + (1,))
    p = jax.nn.softmax(jnp.concatenate([s, sink], axis=-1), axis=-1)[..., :-1]
    o = jnp.einsum('bchgqk,bckhd->bcqhgd', p.astype(vw.dtype), vw)
    return o.reshape(B, Lp, A_HEADS * dh)

def conv_ffn(x, w_up, conv_w, conv_b, w_down):
    L = x.shape[1]
    u = x @ w_up
    up = jnp.pad(u, ((0, 0), (CONV_W - 1, 0), (0, 0)))
    u = sum(up[:, j:j + L] * conv_w[j] for j in range(CONV_W)) + conv_b
    gate, val = u[..., :D_FF], u[..., D_FF:]
    return (jax.nn.gelu(gate, approximate=True) * val) @ w_down

def hybrid_layer(h, w_in, b_in, mh_norm, sinks, w_a, w_b, w_out, g_pre_mix, g_post_mix,
                 g_pre_ffn, g_post_ffn, w_up, conv_w, conv_b, w_down):
    B, L, _ = h.shape
    dt = h.dtype
    xn = rmsnorm(h, g_pre_mix)
    z = xn @ w_in + b_in
    mq, mk, mv, mi, mf, mo, aq, ak, av, ga, gb = split_sections(z)
    f32 = jnp.float32
    hm = mlstm_chunkwise(pad_front(mq.reshape(B, L, M_HEADS, M_QK).astype(f32)),
                         pad_front(mk.reshape(B, L, M_HEADS, M_QK).astype(f32)),
                         pad_front(mv.reshape(B, L, M_HEADS, M_V).astype(f32)),
                         pad_front(mi.astype(f32), NEG),
                         pad_front(jax.nn.log_sigmoid(mf.astype(f32)), 0.0))[:, META_PAD:]
    hm = hm * lax.rsqrt(jnp.mean(hm * hm, axis=-1, keepdims=True) + EPS) * mh_norm.astype(f32)
    ya = hm.reshape(B, L, M_HEADS * M_V).astype(dt) * jax.nn.sigmoid(mo)
    yb = swa_sink_attention(pad_front(aq.reshape(B, L, A_HEADS, A_DH)),
                            pad_front(ak.reshape(B, L, A_KV, A_DH)),
                            pad_front(av.reshape(B, L, A_KV, A_DH)), sinks)[:, META_PAD:]
    y = (jax.nn.sigmoid(ga) * (ya @ w_a) + jax.nn.sigmoid(gb) * (yb @ w_b)) @ w_out
    h = h + rmsnorm(y, g_post_mix)
    h = h + rmsnorm(conv_ffn(rmsnorm(h, g_pre_ffn), w_up, conv_w, conv_b, w_down), g_post_ffn)
    return h

def setup_inputs(seed: int = 0) -> dict:
    key = jax.random.key(seed)
    ks = jax.random.split(key, 18)
    nrm = lambda k, shape, scale: jax.random.normal(k, shape, jnp.float32) * scale
    f_start = sum(SECTION_SIZES[:4])
    b_in = nrm(ks[3], (DEPTH, D_IN), 0.02)
    b_in = b_in.at[:, f_start:f_start + M_HEADS].add(jnp.linspace(3.0, 6.0, M_HEADS))
    gain = lambda k: 1.0 + nrm(k, (DEPTH, D_MODEL), 0.02)
    return {
        'x': nrm(ks[0], (BATCH, SEQ, D_MODEL), 1.0),
        'meta': nrm(ks[1], (N_META, D_MODEL), 1.0),
        'w_in': nrm(ks[2], (DEPTH, D_MODEL, D_IN), D_MODEL ** -0.5),
        'b_in': b_in,
        'mh_norm': 1.0 + nrm(ks[4], (DEPTH, M_HEADS, M_V), 0.02),
        'sinks': nrm(ks[5], (DEPTH, A_HEADS), 0.5),
        'w_a': nrm(ks[6], (DEPTH, M_HEADS * M_V, D_MODEL), (M_HEADS * M_V) ** -0.5),
        'w_b': nrm(ks[7], (DEPTH, A_HEADS * A_DH, D_MODEL), (A_HEADS * A_DH) ** -0.5),
        'w_out': nrm(ks[8], (DEPTH, D_MODEL, D_MODEL), D_MODEL ** -0.5),
        'g_pre_mix': gain(ks[9]),
        'g_post_mix': gain(ks[10]),
        'g_pre_ffn': gain(ks[11]),
        'g_post_ffn': gain(ks[12]),
        'w_up': nrm(ks[13], (DEPTH, D_MODEL, 2 * D_FF), D_MODEL ** -0.5),
        'conv_w': nrm(ks[14], (DEPTH, CONV_W, 2 * D_FF), CONV_W ** -0.5),
        'conv_b': nrm(ks[15], (DEPTH, 2 * D_FF), 0.02),
        'w_down': nrm(ks[16], (DEPTH, D_FF, D_MODEL), D_FF ** -0.5),
    }

def reference(x, meta, w_in, b_in, mh_norm, sinks, w_a, w_b, w_out, g_pre_mix, g_post_mix,
              g_pre_ffn, g_post_ffn, w_up, conv_w, conv_b, w_down):
    B = x.shape[0]
    h = jnp.concatenate([jnp.broadcast_to(meta.astype(x.dtype)[None], (B, N_META, D_MODEL)), x], axis=1)
    for l in range(DEPTH):
        h = hybrid_layer(h, w_in[l], b_in[l], mh_norm[l], sinks[l], w_a[l], w_b[l], w_out[l],
                         g_pre_mix[l], g_post_mix[l], g_pre_ffn[l], g_post_ffn[l],
                         w_up[l], conv_w[l], conv_b[l], w_down[l])
    return h[:, N_META:]


_drawn_inputs = setup_inputs


def setup_inputs(seed=0):
    import zlib

    import numpy as np

    out = dict(_drawn_inputs(seed))
    spreads = {}
    factors = {'mh_norm': 3.61,
     'sinks': 8.0,
     'g_post_mix': 3.474,
     'g_pre_ffn': 3.488,
     'g_post_ffn': 5.036,
     'conv_b': 3.489}
    for name, (base, spread) in spreads.items():
        noise = np.random.default_rng([zlib.crc32(name.encode()), seed]).standard_normal(out[name].shape)
        drawn = base * np.exp(spread * noise) if base else spread * noise
        out[name] = __import__('jax').numpy.asarray(drawn.astype(out[name].dtype))
    for name, factor in factors.items():
        out[name] = (out[name] * factor).astype(out[name].dtype)
    return out
```

```python
from contextlib import ExitStack

import concourse.bass as bass
from concourse import mybir

F32 = mybir.dt.float32
F32R = mybir.dt.float32r
ACT = mybir.ActivationFunctionType
ALU = mybir.AluOpType
AX_X = mybir.AxisListType.X

P = 128
D = 2048
KT = D // P
N_META = 16
SEQ = 256
T = N_META + SEQ
CONV_W = 3
QO = N_META - (CONV_W - 1)
NQ = T - QO
CHUNK = 64
M_HEADS = 8
A_HEADS, A_KV, DH = 32, 4, 64
D_FF = 256 * ((8 * D // 3 + 255) // 256)
FT = D_FF // P
EPS = 1e-6
NEG = -1e30

C_Q, C_K, C_V = 0, 1024, 2048
C_GATE = 4096
C_MO = C_GATE + 2 * M_HEADS
C_AQ = C_MO + D
C_AK = C_AQ + D
C_AV = C_AK + A_KV * DH
C_GA = C_AV + A_KV * DH
C_GB = C_GA + D
B_Q, B_K, B_V, B_MO, B_AQ, B_AK, B_AV, B_GA, B_GB, B_ALL = 0, 8, 16, 32, 48, 64, 66, 68, 84, 100
G_PRE_MIX, G_POST_MIX, G_PRE_FFN, G_MH = 0, 16, 32, 48

RING = 4
START = 3
UK = 4
BLK = 256
U_M, U_KV, U_AW, U_P2, U_WO, U_UP, U_DN = 0, 128, 136, 200, 264, 296, 472
Q_M, Q_KV, Q_AW, Q_P2, Q_WO, Q_UP, Q_DN = 0, 32, 34, 50, 66, 74, 118
DN_K = 2
DN_U = FT // DN_K
DN_BLOCKS = D // 512
STEPS = 9


def layer(nc, x, meta, w_in, b_in, mh_norm, sinks, w_a, w_b, w_out, g_pre_mix, g_post_mix,
          g_pre_ffn, g_post_ffn, w_up, conv_w, conv_b, w_down, out):
    with ExitStack() as ctx:
        base = [16512]

        def put(name, shape, dt=F32, at=None):
            size = 4
            for n in shape[1:]:
                size *= n
            size = (size + 31) // 32 * 32
            if at is None:
                at = base[0]
                base[0] += size
            assert at + size <= 229344, name
            return nc.alloc_sbuf_tensor_at(name, list(shape), dt, offset=at)

        def sem(name):
            return ctx.enter_context(nc.semaphore(name))

        raw = put("raw", [P, RING, 1024])
        w_hi = put("w_hi", [P, RING, 1024], F32R)
        w_lo = put("w_lo", [P, RING, 1024], F32R)
        xn_at = base[0]
        xn_hi = put("xn_hi", [P, KT, T], F32R)
        xn_lo = put("xn_lo", [P, KT, T], F32R)
        xt_at = base[0]
        xt = put("xt", [P, KT, T])
        big_at = base[0]
        base[0] += 2 * FT * SEQ * 4
        g_hi = put("g_hi", [P, FT, SEQ], F32R, big_at)
        g_lo = put("g_lo", [P, FT, SEQ], F32R, big_at + FT * SEQ * 4)
        half = KT * NQ * 4
        ya_hi = put("ya_hi", [P, KT, NQ], F32R, big_at)
        ya_lo = put("ya_lo", [P, KT, NQ], F32R, big_at + half)
        yb_hi = put("yb_hi", [P, KT, NQ], F32R, big_at + 2 * half)
        yb_lo = put("yb_lo", [P, KT, NQ], F32R, big_at + 3 * half)
        z1 = put("z1", [P, KT, NQ], F32, big_at + 4 * half)
        z_hi, z_lo = ya_hi, ya_lo
        spare_at = big_at + 5 * half
        ident = put("ident", [P, P])
        ones = put("ones", [P, P])
        bias_t = put("bias_t", [P, B_ALL])
        half_bias = put("half_bias", [P, B_ALL])
        gains = put("gains", [P, 64])
        conv_t = put("conv_t", [P, 4, 2 * FT])
        cst = put("cst", [P, 4])
        small = put("small", [P, 64])
        EPS_C, ONE_C = cst[:, 0:1], cst[:, 1:2]
        tmp_at = base[0]

        class Area:
            def __init__(self, at):
                self.at = at

            def put(self, name, shape, dt=F32):
                size = 4
                for n in shape[1:]:
                    size *= n
                size = (size + 31) // 32 * 32
                a = self.at
                self.at += size
                return put(name, shape, dt, a)

        area = Area(big_at + 2 * half)
        xs = area.put("xs", [P, 3, D])
        sq_junk = area.put("sq_junk", [P, D])
        area = Area(big_at)
        wg = area.put("wg", [P, KT, 16])
        wg_hi = area.put("wg_hi", [P, KT, P], F32R)
        wg_lo = area.put("wg_lo", [P, KT, P], F32R)
        bias_rows = area.put("bias_rows", [B_ALL, P])
        gain_rows = area.put("gain_rows", [64, P])
        conv_rows = area.put("conv_rows", [2 * FT, 4, P])
        rs_diag = area.put("rs_diag", [P, 3, P])
        xn_f = area.put("xn_f", [P, 2, T])
        rs_b = area.put("rs_b", [P, T])
        area = Area(big_at + 4 * half)
        PAD = 256
        scan_a = area.put("scan_a", [M_HEADS, PAD + T])
        scan_b = area.put("scan_b", [M_HEADS, PAD + T])
        i_pre = area.put("i_pre", [M_HEADS, T])
        f_pre = area.put("f_pre", [M_HEADS, T])
        f_neg = area.put("f_neg", [M_HEADS, T])
        f_soft = area.put("f_soft", [M_HEADS, T])
        b_cum = area.put("b_cum", [M_HEADS, T])
        u_row = area.put("u_row", [M_HEADS, T])

        area = Area(spare_at)
        mask = area.put("mask", [P, T])
        neg_m = area.put("neg_m", [M_HEADS, T])
        m_row = area.put("m_row", [M_HEADS, T])
        q_t = area.put("q_t", [P, NQ])
        k_t = area.put("k_t", [P, T])
        u_col = area.put("u_col", [P, 3, M_HEADS])
        sel = area.put("sel", [M_HEADS, P])
        em = area.put("em", [P, NQ])
        assert area.at <= big_at + 2 * FT * SEQ * 4
        area = Area(tmp_at)
        SP1, SP2 = NQ, NQ + T - P
        probs = area.put("probs", [P, SP2 + 16])
        v_t = area.put("v_t", [P, 2, T])
        v_tok = area.put("v_tok", [P, 2, BLK])
        v_tok2 = area.put("v_tok2", [16, BLK])
        den_r = area.put("den_r", [P, NQ])
        hm = area.put("hm", [P, 2, NQ])
        hm_sq = area.put("hm_sq", [P, 2, NQ])
        sig_o = area.put("sig_o", [P, 2, NQ])
        rs_m = area.put("rs_m", [P, NQ])

        area = Area(spare_at)
        q_pairs = area.put("q_pairs", [P, 4, NQ])
        v_group = area.put("v_group", [P, 4, DH])
        k_group = area.put("k_group", [P, T])
        q_meta = area.put("q_meta", [P, 2, 4])
        prob_t0 = area.put("prob_t0", [N_META, 16])
        probs0 = area.put("probs0", [8, 2, N_META])
        sink_col = area.put("sink_col", [P, A_HEADS // 2])
        sink_meta = area.put("sink_meta", [8, A_KV, 2])
        att = area.put("att", [P, 16])
        att0 = area.put("att0", [8, 16])
        assert area.at <= big_at + 2 * FT * SEQ * 4
        area = Area(tmp_at)
        k_dup = area.put("k_dup", [P, A_KV, T])
        v_win = area.put("v_win", [P, A_KV, 4, DH])
        av_t = area.put("av_t", [P, 2, T])
        probs_a = area.put("probs_a", [P, 2, 2, 144])
        prob_t = area.put("prob_t", [P, 2, P])
        prob_tm = area.put("prob_tm", [N_META, 2, P])

        area = Area(tmp_at)
        gate_b = area.put("gate_b", [P, 4, NQ])
        zt = area.put("zt", [P, 4, NQ])
        area = Area(tmp_at)
        rs2 = area.put("rs2", [P, NQ])
        ffn_at = area.at
        y_sq = area.put("y_sq", [P, 2, NQ])
        ss_acc = area.put("ss_acc", [P, NQ])
        rs1 = area.put("rs1", [P, NQ])
        h_sq = area.put("h_sq", [P, 2, NQ])
        ss2_acc = area.put("ss2_acc", [P, NQ])
        h_a = area.put("h_a", [P, 2, NQ])
        area = Area(ffn_at)
        u_t = area.put("u_t", [P, 4, NQ])
        c_t = area.put("c_t", [P, 4, SEQ])
        ge_t = area.put("ge_t", [P, 2, SEQ])
        h_tok_st = put("h_tok_st", [P, 2, D], F32, big_at)
        h_tok = put("h_tok", [P, 2, D], F32, xn_at)
        gain_b = put("gain_b", [P, D], F32, xn_at + KT * T * 4)
        y_dn = put("y_dn", [P, 2, D], F32, xt_at)
        u_scratch = nc.dram_tensor("u_scratch", [M_HEADS, T], F32).ap()
        h_scratch = nc.dram_tensor("h_scratch", [P, 2, D], F32).ap()

        ps_g = ctx.enter_context(nc.psum_tensor("ps_g", [P, 4, 512], F32))
        ps_x = [ctx.enter_context(nc.psum_tensor(f"ps_x{n}", [P, 512], F32)) for n in range(4)]
        X0, X1, X2, X3 = ps_x

        raw_full = [sem(f"raw_full{n}") for n in range(RING)]
        hi_done = sem("hi_done")
        lo_done = sem("lo_done")
        unit_done = sem("unit_done")
        bank_free = [sem("bank_free0"), sem("bank_free1")]
        x_in = [sem(f"x_in{n}") for n in range(3)]
        wg_in, par_in = sem("wg_in"), sem("par_in")
        const_ready, zero_ready = sem("const_ready"), sem("zero_ready")
        names = {}

        def ev(name):
            if name not in names:
                names[name] = sem(name)
            return names[name]

        par_turned, par_ready, half_ready = ev("par_turned"), ev("par_ready"), ev("half_ready")
        sum_sq, root_ready, rs_ready, diag_ready = ev("sum_sq"), ev("root_ready"), ev("rs_ready"), ev("diag_ready")
        rs_spread, rs_b_ready = ev("rs_spread"), ev("rs_b_ready")
        x_turned, xt_ready, xn_f_ready = ev("x_turned"), ev("xt_ready"), ev("xn_f_ready")
        xn_hi_ready, xn_lo_ready = ev("xn_hi_ready"), ev("xn_lo_ready")
        wg_zeroed, wg_hi_ready, wg_ready = ev("wg_zeroed"), ev("wg_hi_ready"), ev("wg_ready")
        gates_done, pre_ready, f_neg_ready = ev("gates_done"), ev("pre_ready"), ev("f_neg_ready")
        exp_f_ready, soft_ready, chain = ev("exp_f_ready"), ev("soft_ready"), ev("chain")
        rows_ready, u_row_ready, u_col_in = ev("rows_ready"), ev("u_row_ready"), ev("u_col_in")
        pe_held, pool_held, sp_held = ev("pe_held"), ev("pool_held"), ev("sp_held")
        meta_scored = ev("meta_scored")
        u_stored, max_chain = ev("u_stored"), ev("max_chain")

        qk_ready, v_t_ready, sel_ready = ev("qk_ready"), ev("v_t_ready"), ev("sel_ready")
        scores_done, expo_ready, decay_ready = ev("scores_done"), ev("expo_ready"), ev("decay_ready")
        em_ready, probs_ready = ev("em_ready"), ev("probs_ready")
        v_turned, v_tok_ready = ev("v_turned"), ev("v_tok_ready")
        heads_done, den_ready, rden_ready, hm_ready = ev("heads_done"), ev("den_ready"), ev("rden_ready"), ev("hm_ready")
        hm_sq_ready, hm_ss_done, hm_root, hm_rs = ev("hm_sq_ready"), ev("hm_ss_done"), ev("hm_root"), ev("hm_rs")
        tanh_o_ready, sig_o_ready, normed_ready = ev("tanh_o_ready"), ev("sig_o_ready"), ev("normed_ready")
        ya_f_ready, ya_hi_ready, ya_ready = ev("ya_f_ready"), ev("ya_hi_ready"), ev("ya_ready")

        k_dup_ready, av_t_ready, av_turned, v_win_ready = ev("k_dup_ready"), ev("av_t_ready"), ev("av_turned"), ev("v_win_ready")
        sinks_in = ev("sinks_in")
        v_group_ready, q_pairs_ready = ev("v_group_ready"), ev("q_pairs_ready")
        att_scored, att_max, att_maxed, att_nm = ev("att_scored"), ev("att_max"), ev("att_maxed"), ev("att_nm")
        att_sum_in, att_exp, att_den, att_rec, att_probs = ev("att_sum_in"), ev("att_exp"), ev("att_den"), ev("att_rec"), ev("att_probs")
        att_turned, att_prob_t, att_mixed, att_yb_hi, att_yb = ev("att_turned"), ev("att_prob_t"), ev("att_mixed"), ev("att_yb_hi"), ev("att_yb")
        wa_gated = ev("wa_gated")

        gate_b_ready, zt_ready, z_f_ready, z_hi_ready, z_ready = ev("gate_b_ready"), ev("zt_ready"), ev("z_f_ready"), ev("z_hi_ready"), ev("z_ready")
        y_sq_ready, y_acc, y_ss_done, y_root, y_rs = ev("y_sq_ready"), ev("y_acc"), ev("y_ss_done"), ev("y_root"), ev("y_rs")
        h_a_ready, h_ready, h_hi_ready, h_lo_ready, h_sq_ready, h_acc = ev("h_a_ready"), ev("h_ready"), ev("h_hi_ready"), ev("h_lo_ready"), ev("h_sq_ready"), ev("h_acc")
        h_ss_done, h_root, h_rs = ev("h_ss_done"), ev("h_root"), ev("h_rs")
        h_turned, h_tok_ready, h_stored, h_loaded, gain_b_in = ev("h_turned"), ev("h_tok_ready"), ev("h_stored"), ev("h_loaded"), ev("gain_b_in")
        up_scaled, up_tap2, up_tap1, up_tap0, gelu_ready = ev("up_scaled"), ev("up_tap2"), ev("up_tap1"), ev("up_tap0"), ev("gelu_ready")
        g_f_ready, g_hi_ready, g_ready = ev("g_f_ready"), ev("g_hi_ready"), ev("g_ready")
        dn_ss, dn_ss_sum, dn_root, dn_rs, dn_out, out_stored = ev("dn_ss"), ev("dn_ss_sum"), ev("dn_root"), ev("dn_rs"), ev("dn_out"), ev("out_stored")

        from_start = (scores_done, ya_ready, zt_ready, g_f_ready, g_ready, z_ready, tanh_o_ready, bank_free[1], hm_root,
                      wa_gated, att_prob_t, att_yb, att_mixed, y_sq_ready, up_scaled)

        block = ctx.enter_context(nc.Block())

        def chunks_of(e):
            return (1, 2) if e % 2 == 0 else (3, 4)

        def window(c):
            return (N_META, CHUNK) if c == 1 else (N_META + CHUNK * (c - 2), 2 * CHUNK)

        @block.sync
        def _(sp):
            sp.dma_start(xs[0:N_META, 0, :], meta).then_inc(x_in[0], 16)
            sp.dma_start(xs[N_META:P, 0, :], x[0, 0:P - N_META, :]).then_inc(x_in[0], 16)
            sp.dma_start(xs[:, 1, :], x[0, P - N_META:2 * P - N_META, :]).then_inc(x_in[1], 16)
            sp.dma_start(xs[0:N_META, 2, :], x[0, 2 * P - N_META:SEQ, :]).then_inc(x_in[2], 16)
            sp.dma_start(wg[:], w_in[0, :, C_GATE:C_MO].rearrange("(t p) n -> p t n", p=P)).then_inc(wg_in, 16)

            def units_of(u0, w, col, col2=None):
                for q in range(KT // UK):
                    rows = w[q * UK * P:(q + 1) * UK * P, :]
                    dst = raw[:, q, :].rearrange("p (t n) -> p t n", t=UK)
                    sp.wait_ge(lo_done, u0 + q + 1)
                    nc.sync.sem_inc(sp_held, 1)
                    if col2 is None:
                        sp.dma_start(dst, rows[:, bass.ds(col, BLK)].rearrange("(t p) n -> p t n", p=P)).then_inc(raw_full[q], 16)
                    else:
                        for n, c in enumerate((col, col2)):
                            sp.dma_start(dst[:, :, n * P:(n + 1) * P],
                                         rows[:, bass.ds(c, P)].rearrange("(t p) n -> p t n", p=P)).then_inc(raw_full[q], 16)

            w = w_in[0]
            with sp.Fori(0, M_HEADS) as h:
                units_of(h * 16 + U_M, w, h * P + C_Q, h * P + C_K)
                units_of(h * 16 + U_M + 4, w, h * BLK + C_V)
                units_of(h * 16 + U_M + 8, w, h * BLK + C_MO)
                units_of(h * 16 + U_M + 12, w, h * BLK + C_GA)
            units_of(U_KV, w, C_AV, C_AV + P)
            units_of(U_KV + 4, w, C_AK)
            with sp.Fori(0, A_KV) as g:
                units_of(g * 16 + U_AW, w, g * (2 * BLK) + C_AQ)
                units_of(g * 16 + U_AW + 4, w, g * (2 * BLK) + C_AQ + BLK)
                units_of(g * 16 + U_AW + 8, w_a[0], g * (2 * BLK))
                units_of(g * 16 + U_AW + 12, w_a[0], g * (2 * BLK) + BLK)
            with sp.Fori(0, 4) as i:
                units_of(i * 16 + U_P2, w, i * (2 * BLK) + C_GB)
                units_of(i * 16 + U_P2 + 4, w, i * (2 * BLK) + C_GB + BLK)
                units_of(i * 16 + U_P2 + 8, w_b[0], i * (2 * BLK))
                units_of(i * 16 + U_P2 + 12, w_b[0], i * (2 * BLK) + BLK)
            with sp.Fori(0, 8) as i:
                units_of(i * 4 + U_WO, w_out[0], i * BLK)
            with sp.Fori(0, FT // 2) as i:
                units_of(i * 8 + U_UP, w_up[0], i * BLK)
                units_of(i * 8 + U_UP + 4, w_up[0], i * BLK + D_FF)
            with sp.Fori(0, DN_BLOCKS // 2) as i:
                for k in range(2 * DN_U):
                    b, q = divmod(k, DN_U)
                    src = w_down[0][q * DN_K * P:(q + 1) * DN_K * P, bass.ds(i * 1024 + b * 512, 512)]
                    sp.wait_ge(lo_done, i * (2 * DN_U) + U_DN + k + 1)
                    nc.sync.sem_inc(sp_held, 1)
                    sp.dma_start(raw[:, k % RING, :].rearrange("p (t n) -> p t n", t=DN_K),
                                 src.rearrange("(t p) n -> p t n", p=P)).then_inc(raw_full[k % RING], 16)

        @block.gpsimd
        def _(pool):
            nc.gpsimd.memset(ident[:], 0.0).then_inc(zero_ready, 1)
            nc.gpsimd.memset(mask[:], 0.0).then_inc(zero_ready, 1)
            pool.wait_ge(zero_ready, 1)
            nc.gpsimd.affine_select(out=ident[:], in_=ident[:], compare_op=ALU.not_equal, fill=1.0, base=0,
                                    pattern=[[-1, P]], channel_multiplier=1).then_inc(const_ready, 1)
            nc.gpsimd.memset(ones[:], 1.0).then_inc(const_ready, 1)
            nc.gpsimd.memset(cst[:, 0:1], EPS).then_inc(const_ready, 1)
            nc.gpsimd.memset(cst[:, 1:2], 1.0).then_inc(const_ready, 1)
            nc.gpsimd.memset(wg_hi[:].bitcast(F32), 0.0).then_inc(wg_zeroed, 1)
            nc.gpsimd.memset(wg_lo[:].bitcast(F32), 0.0).then_inc(wg_zeroed, 1)
            for s in from_start:
                nc.gpsimd.sem_inc(s, START)
            pool.wait_ge(zero_ready, 2)
            nc.gpsimd.affine_select(out=mask[:], in_=mask[:], compare_op=ALU.is_ge, fill=NEG, base=0,
                                    pattern=[[1, T]], channel_multiplier=-1).then_inc(const_ready, 1)
            nc.gpsimd.memset(scan_a[:, 0:PAD], 0.0).then_inc(zero_ready, 1)
            nc.gpsimd.memset(scan_b[:, 0:PAD], 0.0).then_inc(zero_ready, 1)

            n = 0

            def link(ins):
                ins.then_inc(chain, 1)

            pool.wait_ge(pre_ready, 2)
            link(nc.gpsimd.tensor_scalar(f_pre[:], f_pre[:], 0.0, None, ALU.min))
            pool.wait_ge(chain, 1)
            pool.wait_ge(soft_ready, 1)
            pool.wait_ge(zero_ready, 4)
            link(nc.gpsimd.tensor_tensor(scan_a[:, PAD:], f_pre[:], f_soft[:], ALU.subtract))
            n = 2
            src, dst = scan_a, scan_b
            for d in (1, 2, 4, 8, 16, 32, 64, 128, 256):
                pool.wait_ge(chain, n)
                link(nc.gpsimd.tensor_tensor(dst[:, PAD:], src[:, PAD:], src[:, PAD - d:PAD - d + T], ALU.add))
                n += 1
                src, dst = dst, src
            pool.wait_ge(chain, n)
            link(nc.gpsimd.tensor_copy(b_cum[:], src[:, PAD:]))
            n += 1
            pool.wait_ge(chain, n)
            nc.gpsimd.tensor_tensor(u_row[:], i_pre[:], b_cum[:], ALU.subtract).then_inc(u_row_ready, 1)
            nc.gpsimd.tensor_tensor(dst[:, PAD:], i_pre[:], b_cum[:], ALU.subtract).then_inc(u_row_ready, 1)
            pool.wait_ge(u_row_ready, 1)
            pool.dma_start(u_scratch, u_row[:]).then_inc(u_stored, 16)
            pool.wait_ge(u_stored, 16)
            with nc.allow_non_contiguous_dma(reason="2176 values of the gates, once"):
                for st, w in ((0, P), (1, P), (2, N_META)):
                    pool.dma_start(u_col[0:w, st, :], u_scratch[:, st * P:st * P + w].rearrange("h p -> p h")).then_inc(u_col_in, 16)
            with pool.Fori(0, M_HEADS) as h:
                pool.wait_ge(scores_done, h + START)
                nc.gpsimd.tensor_copy(sel[:], ident[0:M_HEADS, bass.ds(h, 1)].to_broadcast([M_HEADS, P])).then_inc(sel_ready, 1)
                pool.wait_ge(tanh_o_ready, h + 1 + START)
                nc.gpsimd.sem_inc(pool_held, 1)
                nc.gpsimd.tensor_scalar(sig_o[:], sig_o[:], 0.5, 0.5, ALU.mult, ALU.add).then_inc(sig_o_ready, 1)
                pool.wait_ge(normed_ready, h + 1)
                pool.wait_ge(sig_o_ready, h + 1)
                nc.gpsimd.tensor_tensor(hm_sq[:], hm_sq[:], sig_o[:], ALU.mult).then_inc(ya_f_ready, 1)
                pool.wait_ge(ya_f_ready, h + 1)
                hi = ya_hi[:, bass.ds(h * 2, 2), :]
                nc.gpsimd.tensor_copy(hi, hm_sq[:]).then_inc(ya_hi_ready, 1)
                pool.wait_ge(ya_hi_ready, h + 1)
                nc.gpsimd.tensor_tensor(ya_lo[:, bass.ds(h * 2, 2), :], hm_sq[:], hi.bitcast(F32), ALU.subtract).then_inc(ya_ready, 1)

            pool.wait_ge(v_win_ready, 5)
            pool.wait_ge(k_dup_ready, 1)
            with pool.Fori(0, A_KV) as g:
                pool.wait_ge(att_mixed, g * STEPS + START)
                nc.gpsimd.tensor_copy(k_group[:], k_dup[:, bass.ds(g, 1), :].rearrange("p g n -> p (g n)")).then_inc(v_group_ready, 1)
                nc.gpsimd.tensor_copy(v_group[:, 1:4, :], v_win[:, bass.ds(g, 1), 1:4, :].rearrange("p g w d -> p (g w) d")).then_inc(v_group_ready, 1)
                nc.gpsimd.tensor_copy(v_group[0:N_META, 0, :], v_win[0:N_META, bass.ds(g, 1), 0, :].rearrange("p g d -> p (g d)")).then_inc(v_group_ready, 1)

            with pool.Fori(0, 4) as i:
                for m in range(4):
                    n = i * 4 + m + 1
                    t = bass.ds(i * 4 + m, 1)
                    zf = zt[:, m:m + 1, :]
                    pool.wait_ge(zt_ready, n + START)
                    nc.gpsimd.tensor_tensor(zf, zf, z1[:, t, :], ALU.add).then_inc(z_f_ready, 1)
                    pool.wait_ge(z_f_ready, n)
                    nc.gpsimd.tensor_copy(z_hi[:, t, :], zf).then_inc(z_hi_ready, 1)
                    pool.wait_ge(z_hi_ready, n)
                    nc.gpsimd.tensor_tensor(z_lo[:, t, :], zf, z_hi[:, t, :].bitcast(F32), ALU.subtract).then_inc(z_ready, 1)

            pool.wait_ge(z_ready, 16 + START)
            nc.gpsimd.memset(ss_acc[:], 0.0).then_inc(y_acc, 1)
            with pool.Fori(0, 8) as i:
                for m in range(2):
                    pool.wait_ge(y_sq_ready, i * 2 + m + 1 + START)
                    pool.wait_ge(y_acc, i * 2 + m + 1)
                    nc.gpsimd.tensor_tensor(ss_acc[:], ss_acc[:], y_sq[:, m, :], ALU.add).then_inc(y_acc, 1)

            for k in range(KT):
                pool.wait_ge(h_a_ready, k + 1)
                hk = xt[:, k, QO:T]
                nc.gpsimd.tensor_tensor(hk, hk, h_a[:, k % 2, :], ALU.add).then_inc(h_ready, 1)
                if k == 0:
                    nc.gpsimd.memset(ss2_acc[:], 0.0).then_inc(h_acc, 1)
                if k >= 1:
                    pool.wait_ge(h_sq_ready, k)
                    pool.wait_ge(h_acc, k)
                    nc.gpsimd.tensor_tensor(ss2_acc[:], ss2_acc[:], h_sq[:, (k - 1) % 2, :], ALU.add).then_inc(h_acc, 1)
            pool.wait_ge(h_sq_ready, KT)
            pool.wait_ge(h_acc, KT)
            nc.gpsimd.tensor_tensor(ss2_acc[:], ss2_acc[:], h_sq[:, (KT - 1) % 2, :], ALU.add).then_inc(h_acc, 1)

            pool.wait_ge(h_tok_ready, 8)
            pool.dma_start(h_scratch, h_tok_st[:]).then_inc(h_stored, 16)

            pool.wait_ge(h_stored, 16)
            with pool.Fori(0, FT // 2) as i:
                pool.wait_ge(gelu_ready, i * 2 + 2)
                pool.wait_ge(up_tap0, i * 4 + 4)
                t = bass.ds(i * 2, 2)
                nc.gpsimd.tensor_tensor(ge_t[:], ge_t[:], c_t[:, 2:4, :], ALU.mult).then_inc(g_f_ready, 1)
                pool.wait_ge(g_f_ready, i + 1 + START)
                nc.gpsimd.tensor_copy(g_hi[:, t, :], ge_t[:]).then_inc(g_hi_ready, 1)
                pool.wait_ge(g_hi_ready, i + 1)
                nc.gpsimd.tensor_tensor(g_lo[:, t, :], ge_t[:], g_hi[:, t, :].bitcast(F32), ALU.subtract).then_inc(g_ready, 1)

            pool.wait_ge(unit_done, RING + U_DN)
            pool.dma_start(h_tok[:], h_scratch).then_inc(h_loaded, 16)
            pool.dma_start(gain_b[:], g_post_ffn[0].partition_broadcast(P)).then_inc(gain_b_in, 16)

        @block.scalar
        def _(act):
            act.dma_start(bias_rows[0:32, :], b_in[0, 0:C_GATE].rearrange("(m p) -> m p", p=P)).then_inc(par_in, 16)
            act.dma_start(bias_rows[32:B_ALL, :], b_in[0, C_MO:].rearrange("(m p) -> m p", p=P)).then_inc(par_in, 16)
            for n, gain in enumerate((g_pre_mix[0], g_post_mix[0], g_pre_ffn[0])):
                act.dma_start(gain_rows[16 * n:16 * n + 16, :], gain.rearrange("(m p) -> m p", p=P)).then_inc(par_in, 16)
            act.dma_start(gain_rows[48:64, :], mh_norm[0].rearrange("h (c p) -> (h c) p", p=P)).then_inc(par_in, 16)
            act.dma_start(conv_rows[:, 0:3, :], conv_w[0].rearrange("j (m p) -> m j p", p=P)).then_inc(par_in, 16)
            act.dma_start(conv_rows[:, 3, :], conv_b[0].rearrange("(m p) -> m p", p=P)).then_inc(par_in, 16)
            with nc.allow_non_contiguous_dma(reason="16 biases of the gates, once"):
                act.dma_start(small[0:8, 0:1], b_in[0, C_GATE:C_GATE + 8].rearrange("(p a) -> p a", a=1)).then_inc(par_in, 16)
                act.dma_start(small[32:40, 0:1], b_in[0, C_GATE + 8:C_MO].rearrange("(p a) -> p a", a=1)).then_inc(par_in, 16)

            for n, w in ((0, P), (1, P), (2, N_META)):
                act.wait_ge(x_in[n], 32 if n == 0 else 16)
                if n:
                    act.wait_ge(sum_sq, n)
                nc.scalar.activation(sq_junk[0:w, :], xs[0:w, n, :], ACT.Square,
                                     accum_out=small[0:w, 8 + n:9 + n]).then_inc(sum_sq, 1)
            act.wait_ge(const_ready, 4)
            act.wait_ge(sum_sq, 3)
            nc.scalar.activation(small[:, 16:18], small[:, 8:10], ACT.Sqrt, scale=1.0 / D, bias=EPS_C).then_inc(root_ready, 1)
            nc.scalar.activation(small[0:N_META, 18:19], small[0:N_META, 10:11], ACT.Sqrt, scale=1.0 / D,
                                 bias=cst[0:N_META, 0:1]).then_inc(root_ready, 1)
            act.wait_ge(wg_in, 16)
            act.wait_ge(wg_zeroed, 2)
            nc.scalar.copy(wg_hi[:, :, 0:8], wg[:, :, 0:8]).then_inc(wg_hi_ready, 1)
            nc.scalar.copy(wg_hi[:, :, 32:40], wg[:, :, 8:16]).then_inc(wg_hi_ready, 1)
            for k in range(KT):
                act.wait_ge(xn_f_ready, k + 1)
                nc.scalar.copy(xn_hi[:, k, :], xn_f[:, k % 2, :]).then_inc(xn_hi_ready, 1)

            def hi(u, s, n):
                act.wait_ge(raw_full[s], n * 16)
                act.wait_ge(unit_done, u + 1)
                nc.scalar.copy(w_hi[:, s, :], raw[:, s, :]).then_inc(hi_done, 1)

            def split(i, u0, per, k):
                u = k + RING
                if u0 == U_M:
                    loads = i * 5 + 1 + u // RING + 1 + (u // 16)
                else:
                    loads = i * (per // RING) + (u0 + u) // RING + 1 + M_HEADS + 1
                hi(i * per + u0 + u, u % RING, loads)

            for k in range(RING):
                hi(k, k, 2)
            act.wait_ge(f_neg_ready, 1)
            nc.scalar.activation(f_soft[:], f_neg[:], ACT.Exp).then_inc(exp_f_ready, 1)
            act.wait_ge(exp_f_ready, 1)
            nc.scalar.activation(f_soft[:], f_soft[:], ACT.Ln, bias=cst[0:M_HEADS, 1:2]).then_inc(soft_ready, 1)

            with act.Fori(0, M_HEADS) as h:
                for k in range(16):
                    split(h, U_M, 16, k)
                    if k == 4:
                        act.wait_ge(scores_done, h + 1 + START)
                        nc.scalar.activation(em[:], X2[:, 0:NQ], ACT.Exp, scale=-1.0).then_inc(em_ready, 1)
                        act.wait_ge(expo_ready, h + 1)
                        for st, c0, c1, w in ((0, 0, SP1, P), (1, SP1, SP2, P), (2, SP2, SP2 + 16, N_META)):
                            nc.scalar.activation(probs[0:w, c0:c1], probs[0:w, c0:c1], ACT.Exp,
                                                 bias=u_col[0:w, st, bass.ds(h, 1)]).then_inc(decay_ready, 1)
                    if k == 8:
                        act.wait_ge(v_turned, h + 1)
                        nc.scalar.copy(v_tok[:], X3[:, :].rearrange("p (s v) -> p s v", s=2)).then_inc(v_tok_ready, 1)
                        nc.scalar.copy(v_tok2[:], X2[0:N_META, 0:BLK]).then_inc(v_tok_ready, 1)
                    if k == 11:
                        act.wait_ge(unit_done, h * 16 + U_M + k + 1 + RING)
                        act.wait_ge(ya_ready, h + START)
                        for m in range(2):
                            last = nc.scalar.activation(sig_o[:, m, :], ps_g[:, m, 0:NQ], ACT.Tanh, scale=0.5,
                                                        bias=half_bias[:, bass.ds(h * 2 + B_MO + m, 1)])
                        last.then_inc(tanh_o_ready, 1)
                        act.wait_ge(hm_ready, h + 1)
                        nc.scalar.activation(hm_sq[:], hm[:], ACT.Square).then_inc(hm_sq_ready, 1)
                    if k == 14:
                        act.wait_ge(hm_ss_done, h + 1)
                        nc.scalar.activation(rs_m[:], X0[:, 0:NQ], ACT.Sqrt, scale=1.0 / BLK, bias=EPS_C).then_inc(hm_root, 1)
                    if k == 15:
                        act.wait_ge(unit_done, h * 16 + U_M + k + 1 + RING)
                        for m in range(2):
                            last = nc.scalar.activation(z1[:, bass.ds(h * 2 + m, 1), :], ps_g[:, 2 + m:3 + m, 0:NQ], ACT.Tanh, scale=0.5,
                                                        bias=half_bias[:, bass.ds(h * 2 + B_GA + m, 1)])
                        last.then_inc(bank_free[1], 1)

            for k in range(8):
                split(0, U_KV, 8, k)
                if k == 0:
                    act.wait_ge(ya_ready, M_HEADS + START)
                    with nc.allow_non_contiguous_dma(reason="sinks, once"):
                        for par in range(2):
                            act.dma_start(sink_col[64 * par:64 * par + 64, :],
                                          sinks[0].rearrange("(j a) -> a j", a=2)[par].partition_broadcast(64)).then_inc(sinks_in, 16)
                        for tok in range(2):
                            act.dma_start(sink_meta[4 * tok:4 * tok + 4, :, :],
                                          sinks[0].rearrange("(g j a) -> j g a", j=4, a=2)).then_inc(sinks_in, 16)
                if k == 5:
                    act.wait_ge(av_turned, 1)
                    for t in range(2):
                        ps = ps_x[t][:, 0:384].rearrange("p (w g d) -> p g w d", w=3, g=2)
                        for g in range(2):
                            nc.scalar.copy(v_win[:, 2 * t + g, 1:4, :], ps[:, g, :, :]).then_inc(v_win_ready, 1)
                    for t in range(2):
                        ps = ps_x[t][0:N_META, 384:512].rearrange("p (g d) -> p g d", g=2)
                        last = nc.scalar.copy(v_win[0:N_META, 2 * t:2 * t + 2, 0, :], ps)
                    last.then_inc(v_win_ready, 1)

            def softmax(g, e):
                n = g * STEPS + e + 1
                act.wait_ge(att_nm, n)
                if e < 8:
                    for c in range(2):
                        w = N_META + window(chunks_of(e)[c])[1]
                        nc.scalar.activation(probs_a[:, e % 2, c, 0:w], ps_x[e % 2][:, 144 * c:144 * c + w], ACT.Exp,
                                             bias=att[:, 2 + c:3 + c], accum_out=att[:, 4 + c:5 + c])
                    nc.scalar.activation(att[:, 6:8], att[:, 2:4], ACT.Exp,
                                         bias=sink_col[:, bass.ds(g * 4 + e // 2, 1)]).then_inc(att_exp, 1)
                else:
                    for c in range(2):
                        nc.scalar.activation(probs0[:, c, :], ps_x[0][0:8, 16 * c:16 * c + 16], ACT.Exp,
                                             bias=att0[:, 2 + c:3 + c], accum_out=att0[:, 4 + c:5 + c])
                    nc.scalar.activation(att0[:, 6:8], att0[:, 8:10], ACT.Exp).then_inc(att_exp, 1)

            def turn_out(g, e):
                act.wait_ge(att_turned, g * STEPS + e + 1)
                if e < 8:
                    nc.scalar.copy(prob_t[:], X2[:, 0:256].rearrange("p (c n) -> p c n", c=2))
                    nc.scalar.copy(prob_tm[:], X2[0:N_META, 256:512].rearrange("p (c n) -> p c n", c=2)).then_inc(att_prob_t, 1)
                else:
                    nc.scalar.copy(prob_t0[:], X2[0:N_META, 0:16]).then_inc(att_prob_t, 1)

            def mix_out(g, e):
                act.wait_ge(att_mixed, g * STEPS + e + 1 + START)
                if e < 8:
                    c0 = chunks_of(e)[0]
                    dst = yb_hi[:, bass.ds(g * 4 + e // 2, 1), 2 + CHUNK * (c0 - 1):2 + CHUNK * (c0 + 1)]
                    nc.scalar.copy(dst, X3[:, 0:P].rearrange("p (a n) -> p a n", a=1)).then_inc(att_yb_hi, 1)
                else:
                    src = X3[:, 256:264].rearrange("p (t j) -> p j t", t=2)
                    nc.scalar.copy(yb_hi[:, bass.ds(g * 4, 4), 0:2], src).then_inc(att_yb_hi, 1)

            with act.Fori(0, A_KV) as g:
                for k in range(16):
                    split(g, U_AW, 16, k)
                    if 7 <= k <= 15:
                        mix_out(g, k - 7)
                    if 6 <= k <= 14:
                        turn_out(g, k - 6)
                    if 4 <= k <= 12:
                        softmax(g, k - 4)

            with act.Fori(0, 4) as i:
                for k in range(16):
                    split(i, U_P2, 16, k)
                    if k in (3, 7):
                        par = k // 4
                        act.wait_ge(unit_done, i * 16 + U_P2 + k + 1 + RING)
                        act.wait_ge(zt_ready, i * 4 + START)
                        for m in range(2):
                            last = nc.scalar.activation(gate_b[:, 2 * par + m, :], ps_g[:, 2 * par + m, 0:NQ], ACT.Tanh, scale=0.5,
                                                        bias=half_bias[:, bass.ds(i * 4 + B_GB + 2 * par + m, 1)])
                        last.then_inc(gate_b_ready, 1)

            with act.Fori(0, 4) as i:
                for k in range(8):
                    split(i, U_WO, 8, k)
                    if k in (3, 7):
                        par = k // 4
                        act.wait_ge(unit_done, i * 8 + U_WO + k + 1 + RING)
                        for m in range(2):
                            nc.scalar.activation(z1[:, bass.ds(i * 4 + 2 * par + m, 1), :],
                                                 ps_g[:, 2 * par + m:2 * par + m + 1, 0:NQ], ACT.Copy, scale=0.5)
                            if m == 0:
                                act.wait_ge(y_acc, i * 4 + 2 * par + 1)
                            sq = nc.scalar.activation(y_sq[:, m, :], ps_g[:, 2 * par + m, 0:NQ], ACT.Square, scale=0.5)
                            if m == 0:
                                sq.then_inc(y_sq_ready, 1)
                        sq.then_inc(y_sq_ready, 1)

            act.wait_ge(y_ss_done, 1)
            nc.scalar.activation(rs1[:], X0[:, 0:NQ], ACT.Sqrt, scale=1.0 / D, bias=EPS_C).then_inc(y_root, 1)
            for k in range(KT):
                act.wait_ge(h_ready, k + 1)
                nc.scalar.activation(xn_hi[:, k, 0:NQ], xt[:, k, QO:T], ACT.Copy,
                                     scale=gains[:, G_PRE_FFN + k:G_PRE_FFN + k + 1]).then_inc(h_hi_ready, 1)
                if k >= 2:
                    act.wait_ge(h_acc, k)
                nc.scalar.activation(h_sq[:, k % 2, :], xt[:, k, QO:T], ACT.Square).then_inc(h_sq_ready, 1)
            act.wait_ge(h_ss_done, 1)
            nc.scalar.activation(rs2[:], X1[:, 0:NQ], ACT.Sqrt, scale=1.0 / D, bias=EPS_C).then_inc(h_root, 1)
            for n in range(8):
                act.wait_ge(h_turned, n + 1)
                tok, quarter = divmod(n, 4)
                nc.scalar.copy(h_tok_st[:, tok, quarter * 512:quarter * 512 + 512], ps_x[2 + n % 2][:, :]).then_inc(h_tok_ready, 1)

            def up_taps(i, par):
                for m in range(2):
                    t = 2 * par + m
                    act.wait_ge(up_scaled, i * 4 + t + 1 + START)
                    tile = bass.ds(i * 2 + par * FT + m, 1)
                    nc.scalar.activation(c_t[:, t, :], u_t[:, t, 2:NQ], ACT.Identity,
                                         scale=conv_t[:, 2, tile], bias=conv_t[:, 3, tile]).then_inc(up_tap2, 1)

            with act.Fori(0, FT // 2) as i:
                for k in range(8):
                    split(i, U_UP, 8, k)
                    if k == 3:
                        act.wait_ge(g_f_ready, i + START)
                        up_taps(i, 0)
                    if k == 4:
                        act.wait_ge(g_ready, i + START)
                        for m in range(2):
                            act.wait_ge(up_tap0, i * 4 + m + 1)
                            nc.scalar.activation(ge_t[:, m, :], c_t[:, m, :], ACT.Gelu_apprx_tanh).then_inc(gelu_ready, 1)
                    if k == 7:
                        up_taps(i, 1)

            for b in range(DN_BLOCKS):
                for k in range(b * DN_U, (b + 1) * DN_U):
                    if k < DN_BLOCKS * DN_U - RING:
                        split(0, U_DN, 0, k)
                act.wait_ge(unit_done, U_DN + (b + 1) * DN_U + RING)
                for tok in range(2):
                    ps = ps_g[:, 2 * (b % 2) + tok, :]
                    nc.scalar.activation(y_dn[:, tok, 512 * b:512 * b + 512], ps, ACT.Square,
                                         accum_out=small[:, 24 + 4 * tok + b:25 + 4 * tok + b]).then_inc(ev("dn_sq"), 1)
                    act.wait_ge(ev("dn_sq"), 2 * b + tok + 1)
                    last = nc.scalar.copy(y_dn[:, tok, 512 * b:512 * b + 512], ps)
                    last.then_inc(ev("dn_copied"), 1)
            act.wait_ge(dn_ss_sum, 1)
            nc.scalar.activation(small[:, 34:36], small[:, 32:34], ACT.Sqrt, scale=1.0 / D, bias=EPS_C).then_inc(dn_root, 1)
            for n in range(8):
                tok, quarter = divmod(n, 4)
                cols = slice(quarter * 512, quarter * 512 + 512)
                act.wait_ge(dn_out, n + 1)
                t0 = 0 if tok == 0 else P
                act.dma_start(out[0, t0:t0 + P, cols], h_tok[:, tok, cols]).then_inc(out_stored, 16)
            act.wait_ge(out_stored, 8 * 16)

        @block.vector
        def _(dve):
            nc.vector.sem_inc(lo_done, RING)
            dve.wait_ge(par_turned, 1)
            nc.vector.tensor_copy(bias_t[:], X0[:, 0:B_ALL]).then_inc(par_ready, 1)
            nc.vector.tensor_copy(gains[:], X0[:, 128:192]).then_inc(par_ready, 1)
            nc.vector.tensor_copy(conv_t[:], X1[:, 0:8 * FT].rearrange("p (j m) -> p j m", j=4)).then_inc(par_ready, 1)
            dve.wait_ge(par_ready, 1)
            nc.vector.tensor_scalar(half_bias[:], bias_t[:], 0.5, None, ALU.mult).then_inc(half_ready, 1)
            for k in range(8):
                dve.wait_ge(x_turned, k + 1)
                nc.vector.tensor_copy(xt[:, k, :], ps_g[:, k % 4, 0:T]).then_inc(xt_ready, 1)
            dve.wait_ge(root_ready, 2)
            nc.vector.reciprocal(small[:, 20:22], small[:, 16:18]).then_inc(rs_ready, 1)
            nc.vector.reciprocal(small[0:N_META, 22:23], small[0:N_META, 18:19]).then_inc(rs_ready, 1)
            dve.wait_ge(rs_ready, 2)
            dve.wait_ge(const_ready, 1)
            for n, w in ((0, P), (1, P), (2, N_META)):
                last = nc.vector.tensor_scalar(rs_diag[0:w, n, 0:w], ident[0:w, 0:w], small[0:w, 20 + n:21 + n], None, ALU.mult)
            last.then_inc(diag_ready, 1)
            for k in range(8, KT):
                dve.wait_ge(x_turned, k + 1)
                nc.vector.tensor_copy(xt[:, k, :], ps_g[:, k % 4, 0:T]).then_inc(xt_ready, 1)
            dve.wait_ge(rs_spread, 1)
            nc.vector.tensor_copy(rs_b[:], X3[:, 0:T]).then_inc(rs_b_ready, 1)
            dve.wait_ge(rs_b_ready, 1)
            dve.wait_ge(par_ready, 3)
            dve.wait_ge(xt_ready, KT)

            def xn_lo_tile(k):
                dve.wait_ge(xn_hi_ready, k + 1)
                nc.vector.tensor_tensor(xn_lo[:, k, :], xn_f[:, k % 2, :], xn_hi[:, k, :].bitcast(F32),
                                        ALU.subtract).then_inc(xn_lo_ready, 1)

            for k in range(KT):
                if k >= 2:
                    dve.wait_ge(xn_lo_ready, k - 1)
                nc.vector.scalar_tensor_tensor(xn_f[:, k % 2, :], xt[:, k, :], gains[:, G_PRE_MIX + k:G_PRE_MIX + k + 1],
                                               rs_b[:], ALU.mult, ALU.mult).then_inc(xn_f_ready, 1)
                if k == 0:
                    dve.wait_ge(wg_hi_ready, 2)
                    nc.vector.tensor_tensor(wg_lo[:, :, 0:8], wg[:, :, 0:8], wg_hi[:, :, 0:8].bitcast(F32), ALU.subtract).then_inc(wg_ready, 1)
                    nc.vector.tensor_tensor(wg_lo[:, :, 32:40], wg[:, :, 8:16], wg_hi[:, :, 32:40].bitcast(F32), ALU.subtract).then_inc(wg_ready, 1)
                if k >= 1:
                    xn_lo_tile(k - 1)
            xn_lo_tile(KT - 1)

            def lo(u, s):
                dve.wait_ge(hi_done, u + 1)
                nc.vector.tensor_tensor(w_lo[:, s, :], raw[:, s, :], w_hi[:, s, :].bitcast(F32), ALU.subtract).then_inc(lo_done, 1)

            def split(i, u0, per, k):
                lo(i * per + u0 + k + RING, k % RING)

            for k in range(RING):
                lo(k, k)
            dve.wait_ge(gates_done, 1)
            nc.vector.tensor_scalar(i_pre[:], X3[0:8, 0:T], small[0:8, 0:1], None, ALU.add).then_inc(pre_ready, 1)
            nc.vector.tensor_scalar(f_pre[:], X3[32:40, 0:T], small[32:40, 0:1], None, ALU.add).then_inc(ev("f_ready"), 1)
            dve.wait_ge(ev("f_ready"), 1)
            nc.vector.scalar_tensor_tensor(f_neg[:], f_pre[:], -1.0, f_pre[:], ALU.mult, ALU.min).then_inc(f_neg_ready, 1)
            dve.wait_ge(f_neg_ready, 1)
            nc.vector.sem_inc(pre_ready, 1)
            src, dst = scan_a, scan_b
            dve.wait_ge(u_row_ready, 2)
            for n, d in enumerate((1, 2, 4, 8, 16, 32, 64, 128, 256)):
                if n:
                    dve.wait_ge(max_chain, n)
                nc.vector.tensor_tensor(dst[:, PAD:], src[:, PAD:], src[:, PAD - d:PAD - d + T], ALU.max).then_inc(max_chain, 1)
                src, dst = dst, src
            dve.wait_ge(max_chain, 9)
            nc.vector.tensor_scalar(neg_m[:], src[:, PAD:], 0.0, -1.0, ALU.max, ALU.mult).then_inc(max_chain, 1)
            dve.wait_ge(max_chain, 10)
            nc.vector.tensor_tensor(m_row[:], b_cum[:], neg_m[:], ALU.subtract).then_inc(rows_ready, 1)

            with dve.Fori(0, M_HEADS) as h:
                for k in range(16):
                    split(h, U_M, 16, k)
                    if k == 3:
                        dve.wait_ge(unit_done, h * 16 + U_M + k + 1 + RING)
                        nc.vector.tensor_scalar(q_t[:], ps_g[:, 0, 0:NQ], bias_t[:, bass.ds(h + B_Q, 1)], None, ALU.add)
                        nc.vector.tensor_scalar(k_t[:], ps_g[:, 1, 0:T], bias_t[:, bass.ds(h + B_K, 1)], float(P) ** -0.5,
                                                ALU.add, ALU.mult).then_inc(qk_ready, 1)
                    if k == 4:
                        dve.wait_ge(scores_done, h + 1 + START)
                        dve.wait_ge(const_ready, 5)
                        nc.vector.tensor_tensor(probs[:, 0:SP1], X1[:, 0:NQ], mask[:, QO:T], ALU.add)
                        nc.vector.tensor_tensor(probs[:, SP1:SP2], X1[:, P - QO:NQ], mask[:, 0:T - P], ALU.add)
                        nc.vector.tensor_tensor(probs[0:N_META, SP2:SP2 + 16], X1[0:N_META, 2 * P - QO:NQ], mask[0:N_META, 0:16],
                                                ALU.add).then_inc(expo_ready, 1)
                        dve.wait_ge(decay_ready, h * 3 + 3)
                        nc.vector.tensor_tensor(probs[:, 0:SP2], probs[:, 0:SP2], X0[:, 0:SP2], ALU.mult)
                        nc.vector.tensor_tensor(probs[0:N_META, SP2:SP2 + 16], probs[0:N_META, SP2:SP2 + 16],
                                                X0[0:N_META, SP2:SP2 + 16], ALU.mult).then_inc(probs_ready, 1)
                    if k == 7:
                        dve.wait_ge(unit_done, h * 16 + U_M + k + 1 + RING)
                        for c in range(2):
                            last = nc.vector.tensor_scalar(v_t[:, c, :], ps_g[:, 2 + c, 0:T], bias_t[:, bass.ds(h * 2 + B_V + c, 1)],
                                                           None, ALU.add)
                        last.then_inc(v_t_ready, 1)
                    if k == 11:
                        dve.wait_ge(heads_done, h + 1)
                        dve.wait_ge(em_ready, h + 1)
                        nc.vector.scalar_tensor_tensor(den_r[:], X3[:, 0:NQ], -1.0, em[:], ALU.mult, ALU.max).then_inc(den_ready, 1)
                        dve.wait_ge(den_ready, h * 2 + 1)
                        nc.vector.tensor_tensor(den_r[:], X3[:, 0:NQ], den_r[:], ALU.max).then_inc(den_ready, 1)
                        dve.wait_ge(den_ready, h * 2 + 2)
                        nc.vector.reciprocal(den_r[:], den_r[:]).then_inc(rden_ready, 1)
                        dve.wait_ge(rden_ready, h + 1)
                        for c, ps in ((0, X1), (1, X2)):
                            last = nc.vector.tensor_tensor(hm[:, c, :], ps[:, 0:NQ], den_r[:], ALU.mult)
                        last.then_inc(hm_ready, 1)
                    if k == 14:
                        dve.wait_ge(hm_root, h + 1 + START)
                        nc.vector.reciprocal(rs_m[:], rs_m[:]).then_inc(hm_rs, 1)
                        dve.wait_ge(hm_rs, h + 1)
                        for c in range(2):
                            last = nc.vector.scalar_tensor_tensor(hm_sq[:, c, :], hm[:, c, :], gains[:, bass.ds(h * 2 + G_MH + c, 1)],
                                                                  rs_m[:], ALU.mult, ALU.mult)
                        last.then_inc(normed_ready, 1)

            dve.wait_ge(ya_ready, M_HEADS + START)
            for k in range(8):
                split(0, U_KV, 8, k)
                if k == 3:
                    dve.wait_ge(unit_done, U_KV + k + 1 + RING)
                    for c in range(2):
                        last = nc.vector.tensor_scalar(av_t[:, c, :], ps_g[:, c, 0:T], bias_t[:, B_AV + c:B_AV + c + 1], None, ALU.add)
                    last.then_inc(av_t_ready, 1)
                if k == 7:
                    dve.wait_ge(unit_done, U_KV + k + 1 + RING)
                    for c in range(2):
                        for half_in in range(2):
                            for half_out in range(2):
                                pi, po = 64 * half_in, 64 * half_out
                                last = nc.vector.tensor_scalar(k_dup[po:po + 64, 2 * c + half_in, :], ps_g[pi:pi + 64, 2 + c, 0:T],
                                                               bias_t[pi:pi + 64, B_AK + c:B_AK + c + 1], float(DH) ** -0.5,
                                                               ALU.add, ALU.mult)
                    last.then_inc(k_dup_ready, 1)
            dve.wait_ge(sinks_in, 64)

            def softmax(g, e):
                n = g * STEPS + e + 1
                dve.wait_ge(att_scored, n)
                if e < 8:
                    ps = ps_x[e % 2]
                    for c in range(2):
                        w = N_META + window(chunks_of(e)[c])[1]
                        last = nc.vector.tensor_reduce(att[:, c:c + 1], ps[:, 144 * c:144 * c + w], AX_X, ALU.max)
                    last.then_inc(att_max, 1)
                    dve.wait_ge(att_max, n)
                    nc.vector.tensor_scalar(att[:, 2:4], att[:, 0:2], sink_col[:, bass.ds(g * 4 + e // 2, 1)], -1.0,
                                            ALU.max, ALU.mult).then_inc(att_nm, 1)
                    dve.wait_ge(att_exp, n)
                    nc.vector.tensor_tensor(att[:, 8:10], att[:, 4:6], att[:, 6:8], ALU.add).then_inc(att_den, 1)
                    dve.wait_ge(att_den, n)
                    nc.vector.reciprocal(att[:, 10:12], att[:, 8:10]).then_inc(att_rec, 1)
                    dve.wait_ge(att_rec, n)
                    for c in range(2):
                        w = N_META + window(chunks_of(e)[c])[1]
                        pr = probs_a[:, e % 2, c, 0:w]
                        last = nc.vector.tensor_scalar(pr, pr, att[:, 10 + c:11 + c], None, ALU.mult)
                    last.then_inc(att_probs, 1)
                else:
                    nc.vector.tensor_reduce(att0[:, 0:2], ps_x[0][0:8, 0:32].rearrange("p (a n) -> p a n", a=2), AX_X,
                                            ALU.max).then_inc(att_max, 1)
                    dve.wait_ge(att_max, n)
                    sk = sink_meta[:, bass.ds(g, 1), :].rearrange("p g a -> p (g a)")
                    nc.vector.tensor_tensor(att0[:, 10:12], att0[:, 0:2], sk, ALU.max).then_inc(att_maxed, 1)
                    dve.wait_ge(att_maxed, g * 2 + 1)
                    nc.vector.tensor_scalar(att0[:, 2:4], att0[:, 10:12], -1.0, None, ALU.mult).then_inc(att_maxed, 1)
                    dve.wait_ge(att_maxed, g * 2 + 2)
                    nc.vector.tensor_tensor(att0[:, 8:10], att0[:, 2:4], sk, ALU.add).then_inc(att_nm, 1)
                    dve.wait_ge(att_exp, n)
                    nc.vector.tensor_tensor(att0[:, 12:14], att0[:, 4:6], att0[:, 6:8], ALU.add).then_inc(att_den, 1)
                    dve.wait_ge(att_den, n)
                    nc.vector.reciprocal(att0[:, 14:16], att0[:, 12:14]).then_inc(att_rec, 1)
                    dve.wait_ge(att_rec, n)
                    for c in range(2):
                        last = nc.vector.tensor_scalar(probs0[:, c, :], probs0[:, c, :], att0[:, 14 + c:15 + c], None, ALU.mult)
                    last.then_inc(att_probs, 1)

            def mix_out(g, e):
                dve.wait_ge(att_yb_hi, g * STEPS + e + 1)
                if e < 8:
                    c0 = chunks_of(e)[0]
                    at = (slice(None), bass.ds(g * 4 + e // 2, 1), slice(2 + CHUNK * (c0 - 1), 2 + CHUNK * (c0 + 1)))
                    nc.vector.tensor_tensor(yb_lo[at], X3[:, 0:P].rearrange("p (a n) -> p a n", a=1), yb_hi[at].bitcast(F32),
                                            ALU.subtract).then_inc(att_yb, 1)
                else:
                    at = (slice(None), bass.ds(g * 4, 4), slice(0, 2))
                    nc.vector.tensor_tensor(yb_lo[at], X3[:, 256:264].rearrange("p (t j) -> p j t", t=2), yb_hi[at].bitcast(F32),
                                            ALU.subtract).then_inc(att_yb, 1)

            with dve.Fori(0, A_KV) as g:
                for k in range(16):
                    split(g, U_AW, 16, k)
                    if k in (3, 7):
                        par = k // 4
                        dve.wait_ge(unit_done, g * 16 + U_AW + k + 1 + RING)
                        for m in range(2):
                            nc.vector.tensor_scalar(q_meta[:, :, 2 * par + m], ps_g[:, 2 * par + m, 0:2],
                                                    bias_t[:, bass.ds(g * 4 + B_AQ + 2 * par + m, 1)], None, ALU.add)
                            last = nc.vector.tensor_scalar(q_pairs[:, 2 * par + m, :], ps_g[:, 2 * par + m, 0:NQ],
                                                           bias_t[:, bass.ds(g * 4 + B_AQ + 2 * par + m, 1)], None, ALU.add)
                        last.then_inc(q_pairs_ready, 1)
                    if 7 <= k <= 15:
                        mix_out(g, k - 7)
                    if k in (11, 15):
                        par = k // 4 - 2
                        dve.wait_ge(unit_done, g * 16 + U_AW + k + 1 + RING)
                        for m in range(2):
                            zz = z1[:, bass.ds(g * 4 + 2 * par + m, 1), :]
                            last = nc.vector.scalar_tensor_tensor(zz, zz, 1.0, ps_g[:, 2 * par + m:2 * par + m + 1, 0:NQ],
                                                                  ALU.add, ALU.mult)
                        last.then_inc(wa_gated, 1)
                    if 4 <= k <= 12:
                        softmax(g, k - 4)

            dve.wait_ge(wa_gated, 8 + START)
            with dve.Fori(0, 4) as i:
                for k in range(16):
                    split(i, U_P2, 16, k)
                    if k in (11, 15):
                        par = k // 4 - 2
                        dve.wait_ge(unit_done, i * 16 + U_P2 + k + 1 + RING)
                        dve.wait_ge(gate_b_ready, i * 2 + 2)
                        dve.wait_ge(z_ready, i * 4 + START)
                        for m in range(2):
                            t = 2 * par + m
                            last = nc.vector.scalar_tensor_tensor(zt[:, t, :], gate_b[:, t, :], 1.0, ps_g[:, t, 0:NQ],
                                                                  ALU.add, ALU.mult)
                            last.then_inc(zt_ready, 1)

            with dve.Fori(0, 4) as i:
                for k in range(8):
                    split(i, U_WO, 8, k)

            dve.wait_ge(y_root, 1)
            nc.vector.reciprocal(rs1[:], rs1[:]).then_inc(y_rs, 1)
            dve.wait_ge(y_rs, 1)

            def h_lo_tile(k):
                dve.wait_ge(h_hi_ready, k + 1)
                nc.vector.scalar_tensor_tensor(xn_lo[:, k, 0:NQ], xt[:, k, QO:T], gains[:, G_PRE_FFN + k:G_PRE_FFN + k + 1],
                                               xn_hi[:, k, 0:NQ].bitcast(F32), ALU.mult, ALU.subtract).then_inc(h_lo_ready, 1)

            for k in range(KT):
                if k >= 2:
                    dve.wait_ge(h_ready, k - 1)
                nc.vector.scalar_tensor_tensor(h_a[:, k % 2, :], z1[:, k, :], gains[:, G_POST_MIX + k:G_POST_MIX + k + 1],
                                               rs1[:], ALU.mult, ALU.mult).then_inc(h_a_ready, 1)
                if k >= 1:
                    h_lo_tile(k - 1)
            h_lo_tile(KT - 1)
            dve.wait_ge(h_root, 1)
            nc.vector.reciprocal(rs2[:], rs2[:]).then_inc(h_rs, 1)
            dve.wait_ge(h_rs, 1)

            def up_block(i, par, k):
                dve.wait_ge(unit_done, i * 8 + U_UP + k + 1 + RING)
                for m in range(2):
                    t = 2 * par + m
                    nc.vector.tensor_tensor(u_t[:, t, :], ps_g[:, t, 0:NQ], rs2[:], ALU.mult).then_inc(up_scaled, 1)
                for j in (1, 0):
                    for m in range(2):
                        t = 2 * par + m
                        dve.wait_ge(up_tap2 if j == 1 else up_tap1, i * 4 + t + 1)
                        nc.vector.scalar_tensor_tensor(c_t[:, t, :], u_t[:, t, j:j + SEQ],
                                                       conv_t[:, j, bass.ds(i * 2 + par * FT + m, 1)], c_t[:, t, :],
                                                       ALU.mult, ALU.add).then_inc(up_tap1 if j == 1 else up_tap0, 1)

            with dve.Fori(0, FT // 2) as i:
                for k in range(8):
                    split(i, U_UP, 8, k)
                    if k in (3, 7):
                        up_block(i, k // 4, k)

            for k in range(DN_BLOCKS * DN_U - RING):
                split(0, U_DN, 0, k)
            dve.wait_ge(ev("dn_copied"), 2 * DN_BLOCKS)
            nc.vector.tensor_reduce(small[:, 32:34], small[:, 24:32].rearrange("p (t b) -> p t b", t=2), AX_X, ALU.add).then_inc(dn_ss_sum, 1)
            dve.wait_ge(dn_root, 1)
            nc.vector.reciprocal(small[:, 36:38], small[:, 34:36]).then_inc(dn_rs, 1)
            dve.wait_ge(dn_rs, 1)
            dve.wait_ge(gain_b_in, 16)
            dve.wait_ge(h_loaded, 16)
            for n in range(8):
                tok, quarter = divmod(n, 4)
                cols = slice(quarter * 512, quarter * 512 + 512)
                nc.vector.scalar_tensor_tensor(y_dn[:, tok, cols], y_dn[:, tok, cols], small[:, 36 + tok:37 + tok], gain_b[:, cols],
                                               ALU.mult, ALU.mult).then_inc(ev("dn_scaled"), 1)
                if n >= 1:
                    t1, q1 = divmod(n - 1, 4)
                    c1 = slice(q1 * 512, q1 * 512 + 512)
                    dve.wait_ge(ev("dn_scaled"), n)
                    nc.vector.tensor_tensor(h_tok[:, t1, c1], h_tok[:, t1, c1], y_dn[:, t1, c1], ALU.add).then_inc(dn_out, 1)
            dve.wait_ge(ev("dn_scaled"), 8)
            nc.vector.tensor_tensor(h_tok[:, 1, 1536:2048], h_tok[:, 1, 1536:2048], y_dn[:, 1, 1536:2048], ALU.add).then_inc(dn_out, 1)

        @block.tensor
        def _(pe):
            nc.tensor.sem_inc(unit_done, RING)
            pe.wait_ge(par_in, 10 * 16)
            pe.wait_ge(const_ready, 2)
            nc.tensor.transpose(X0[:, 0:B_ALL], bias_rows[:, :], ident[0:B_ALL, 0:B_ALL])
            nc.tensor.transpose(X0[:, 128:192], gain_rows[:, :], ident[0:64, 0:64])
            for j in range(4):
                last = nc.tensor.transpose(X1[:, j * 2 * FT:(j + 1) * 2 * FT], conv_rows[:, j, :], ident[0:2 * FT, 0:2 * FT])
            last.then_inc(par_turned, 1)
            for n in range(3):
                pe.wait_ge(x_in[n], 32 if n == 0 else 16)
            for k in range(KT):
                if k >= 4:
                    pe.wait_ge(xt_ready, k - 3)
                for n, w in ((0, P), (1, P), (2, N_META)):
                    last = nc.tensor.transpose(ps_g[:, k % 4, n * P:n * P + w], xs[0:w, n, k * P:(k + 1) * P], ident[0:w, 0:w])
                last.then_inc(x_turned, 1)
            pe.wait_ge(diag_ready, 1)
            for n, w in ((0, P), (1, P), (2, N_META)):
                last = nc.tensor.matmul(X3[:, n * P:n * P + w], ones[0:w, :], rs_diag[0:w, n, 0:w], start=True, stop=True)
            last.then_inc(rs_spread, 1)
            pe.wait_ge(wg_ready, 2)
            pe.wait_ge(rs_b_ready, 1)
            for k in range(KT):
                pe.wait_ge(xn_lo_ready, k + 1)
                for a, b in ((wg_hi, xn_hi), (wg_hi, xn_lo), (wg_lo, xn_hi)):
                    last = nc.tensor.matmul(X3[:, 0:T], a[:, k, :], b[:, k, :], start=(k == 0 and a is wg_hi and b is xn_hi),
                                            stop=(k == KT - 1 and a is wg_lo))
            last.then_inc(gates_done, 1)

            def unit(u, q, par, acts, t0=(0, 0), n=(NQ, NQ)):
                pe.wait_ge(lo_done, u + 1 + RING)
                wh = w_hi[:, q, :].rearrange("p (t n) -> p t n", t=UK)
                wl = w_lo[:, q, :].rearrange("p (t n) -> p t n", t=UK)
                for m in range(2):
                    dst = ps_g[:, 2 * par + m, 0:n[m]]
                    for t in range(UK):
                        k = q * UK + t
                        cols = slice(m * P, (m + 1) * P)
                        mh, ml = (a[:, k, t0[m]:t0[m] + n[m]] for a in acts)
                        nc.tensor.matmul(dst, wh[:, t, cols], mh, start=(k == 0), stop=False)
                        nc.tensor.matmul(dst, wh[:, t, cols], ml, start=False, stop=False)
                        last = nc.tensor.matmul(dst, wl[:, t, cols], mh, start=False, stop=(k == KT - 1))
                last.then_inc(unit_done, 1)

            xn, ya, yb, zz = (xn_hi, xn_lo), (ya_hi, ya_lo), (yb_hi, yb_lo), (z_hi, z_lo)
            Q_TOK = dict(t0=(QO, QO), n=(NQ, NQ))
            ALL_TOK = dict(t0=(0, 0), n=(T, T))

            def free(i, per, q0, b):
                pe.wait_ge(bank_free[b % 2], i * (per // 2) + (q0 + b) // 2)

            with pe.Fori(0, M_HEADS) as h:
                for k in range(16):
                    b, q = divmod(k, 4)
                    if q == 0:
                        if b == 0:
                            pe.wait_ge(tanh_o_ready, h + START)
                        elif b == 1:
                            pe.wait_ge(bank_free[1], h + START)
                        elif b == 2:
                            pe.wait_ge(qk_ready, h + 1)
                        else:
                            pe.wait_ge(v_t_ready, h + 1)
                    toks = (dict(t0=(QO, 0), n=(NQ, T)), ALL_TOK, Q_TOK, Q_TOK)[b]
                    unit(h * 16 + U_M + k, q, b % 2, xn, **toks)
                    if k == 4:
                        pe.wait_ge(qk_ready, h + 1)
                        pe.wait_ge(sel_ready, h + 1)
                        pe.wait_ge(rows_ready, 1)
                        pe.wait_ge(u_col_in, 48)
                        pe.wait_ge(hm_root, h + START)
                        nc.tensor.matmul(X0[:, 0:SP1], k_t[:, 0:P], q_t[:, :], start=True, stop=True)
                        nc.tensor.matmul(X0[:, SP1:SP2], k_t[:, P:2 * P], q_t[:, P - QO:NQ], start=True, stop=True)
                        nc.tensor.matmul(X0[0:N_META, SP2:SP2 + 16], k_t[:, 2 * P:T], q_t[:, 2 * P - QO:NQ], start=True, stop=True)
                        nc.tensor.matmul(X1[:, 0:NQ], sel[:, :], neg_m[:, QO:T], start=True, stop=True)
                        nc.tensor.matmul(X2[:, 0:NQ], sel[:, :], m_row[:, QO:T], start=True, stop=True).then_inc(scores_done, 1)
                    if k == 8:
                        pe.wait_ge(v_t_ready, h + 1)
                        pe.wait_ge(em_ready, h + 1)
                        for c in range(2):
                            for st in range(2):
                                nc.tensor.transpose(X3[:, st * BLK + c * P:st * BLK + (c + 1) * P], v_t[:, c, st * P:(st + 1) * P], ident[:, :])
                            last = nc.tensor.transpose(X2[0:N_META, c * P:(c + 1) * P], v_t[:, c, 2 * P:T], ident[:, :])
                        last.then_inc(v_turned, 1)
                    if k == 11:
                        pe.wait_ge(v_tok_ready, h * 2 + 2)
                        pe.wait_ge(probs_ready, h + 1)
                        for c, dst in ((0, X1), (1, X2), (2, X3)):
                            w0 = v_tok[:, 0, c * P:(c + 1) * P] if c < 2 else ones[:, :]
                            w1 = v_tok[:, 1, c * P:(c + 1) * P] if c < 2 else ones[:, :]
                            w2 = v_tok2[:, c * P:(c + 1) * P] if c < 2 else ones[0:N_META, :]
                            nc.tensor.matmul(dst[:, 0:NQ], w0, probs[:, 0:SP1], start=True, stop=False)
                            nc.tensor.matmul(dst[:, P - QO:NQ], w1, probs[:, SP1:SP2], start=False, stop=False)
                            last = nc.tensor.matmul(dst[:, 2 * P - QO:NQ], w2, probs[0:N_META, SP2:SP2 + 16], start=False, stop=True)
                        last.then_inc(heads_done, 1)
                    if k == 14:
                        pe.wait_ge(hm_sq_ready, h + 1)
                        nc.tensor.matmul(X0[:, 0:NQ], ones[:, :], hm_sq[:, 0, :], start=True, stop=False)
                        nc.tensor.matmul(X0[:, 0:NQ], ones[:, :], hm_sq[:, 1, :], start=False, stop=True).then_inc(hm_ss_done, 1)

            for k in range(8):
                b, q = divmod(k, 4)
                if q == 0:
                    pe.wait_ge((tanh_o_ready, bank_free[1])[b], M_HEADS + START)
                unit(U_KV + k, q, b, xn, **ALL_TOK)
                if k == 5:
                    pe.wait_ge(av_t_ready, 1)
                    pe.wait_ge(hm_root, M_HEADS + START)
                    for t in range(2):
                        for n, c in enumerate((2, 3, 4)):
                            w0, w = window(c)
                            nc.tensor.transpose(ps_x[t][:, n * P:(n + 1) * P], av_t[:, t, w0:w0 + w], ident[:, :])
                        last = nc.tensor.transpose(ps_x[t][0:N_META, 384:512], av_t[:, t, 0:N_META], ident[:, :])
                    last.then_inc(av_turned, 1)

            def hold():
                nc.tensor.sem_inc(pe_held, 1)

            def scores(g, e):
                pe.wait_ge(q_pairs_ready, g * 2 + (1 if e < 4 else 2))
                pe.wait_ge(v_group_ready, g * 3 + 1)
                hold()
                ps = ps_x[e % 2]
                for par in range(2):
                    rows = slice(64 * par, 64 * par + 64)
                    if e < 8:
                        for c in range(2):
                            ch = chunks_of(e)[c]
                            w0, w = window(ch)
                            qs = q_pairs[rows, e // 2, 2 + CHUNK * (ch - 1):2 + CHUNK * ch]
                            nc.tensor.matmul(ps[rows, 144 * c:144 * c + N_META], qs,
                                             k_group[rows, 0:N_META], start=True, stop=True)
                            last = nc.tensor.matmul(ps[rows, 144 * c + N_META:144 * c + N_META + w], qs,
                                                    k_group[rows, w0:w0 + w], start=True, stop=True)
                    else:
                        if par:
                            last.then_inc(meta_scored, 1)
                            pe.wait_ge(meta_scored, g + 1)
                            hold()
                        last = nc.tensor.matmul(ps[0:8, 16 * par:16 * par + 16], q_meta[rows, :, :].rearrange("p t j -> p (t j)"),
                                                k_group[rows, 0:N_META], start=True, stop=True)
                last.then_inc(att_scored, 1)

            def turn(g, e):
                pe.wait_ge(att_probs, g * STEPS + e + 1)
                if e == 0:
                    pe.wait_ge(att_prob_t, g * STEPS + START)
                hold()
                if e < 8:
                    for c in range(2):
                        w = window(chunks_of(e)[c])[1]
                        nc.tensor.transpose(X2[0:w, c * P:(c + 1) * P], probs_a[:, e % 2, c, N_META:N_META + w], ident[:, :])
                        last = nc.tensor.transpose(X2[0:N_META, 256 + c * P:256 + (c + 1) * P], probs_a[:, e % 2, c, 0:N_META], ident[:, :])
                else:
                    for c in range(2):
                        last = nc.tensor.transpose(X2[0:N_META, 8 * c:8 * c + 8], probs0[:, c, :], ident[0:8, 0:8])
                last.then_inc(att_turned, 1)

            def mix(g, e):
                pe.wait_ge(att_prob_t, g * STEPS + e + 1 + START)
                pe.wait_ge(att_yb, g * STEPS + e + START)
                pe.wait_ge(v_group_ready, g * 3 + 3)
                hold()
                for par in range(2):
                    rows = slice(64 * par, 64 * par + 64)
                    if e < 8:
                        for c in range(2):
                            ch = chunks_of(e)[c]
                            w = window(ch)[1]
                            slot = 1 if ch <= 2 else ch - 1
                            dst = X3[rows, CHUNK * c:CHUNK * (c + 1)]
                            nc.tensor.matmul(dst, v_group[0:N_META, 0, :], prob_tm[:, c, rows], start=True, stop=False)
                            last = nc.tensor.matmul(dst, v_group[0:w, slot, :], prob_t[0:w, c, rows], start=False, stop=True)
                    else:
                        last = nc.tensor.matmul(X3[rows, 256:264], v_group[0:N_META, 0, :], prob_t0[:, 8 * par:8 * par + 8],
                                                start=True, stop=True)
                last.then_inc(att_mixed, 1)

            pe.wait_ge(k_dup_ready, 1)
            pe.wait_ge(v_win_ready, 5)
            with pe.Fori(0, A_KV) as g:
                for k in range(16):
                    b, q = divmod(k, 4)
                    if q == 0:
                        if b < 2:
                            pe.wait_ge(wa_gated, g * 2 - 1 + b + START)
                        else:
                            pe.wait_ge(q_pairs_ready, g * 2 + b - 1)
                    unit(g * 16 + U_AW + k, q, b % 2, xn if b < 2 else ya, **(Q_TOK if b < 2 else {}))
                    if 7 <= k <= 15:
                        mix(g, k - 7)
                    if 6 <= k <= 14:
                        turn(g, k - 6)
                    if 4 <= k <= 12:
                        scores(g, k - 4)

            pe.wait_ge(att_yb, A_KV * STEPS + START)
            with pe.Fori(0, 4) as i:
                for k in range(16):
                    b, q = divmod(k, 4)
                    if q == 0:
                        if b < 2:
                            pe.wait_ge(wa_gated, 8 + START)
                            pe.wait_ge(zt_ready, i * 4 - 2 + 2 * b + START)
                        else:
                            pe.wait_ge(gate_b_ready, i * 2 + b - 1)
                    unit(i * 16 + U_P2 + k, q, b % 2, xn if b < 2 else yb, **(Q_TOK if b < 2 else {}))

            pe.wait_ge(z_ready, 16 + START)
            with pe.Fori(0, 4) as i:
                for k in range(8):
                    b, q = divmod(k, 4)
                    if q == 0:
                        pe.wait_ge(y_sq_ready, i * 4 - 2 + 2 * b + START)
                    unit(i * 8 + U_WO + k, q, b, zz)
            pe.wait_ge(y_acc, 17)
            nc.tensor.matmul(X0[:, 0:NQ], ones[:, :], ss_acc[:], start=True, stop=True).then_inc(y_ss_done, 1)

            for n in range(8):
                tok, quarter = divmod(n, 4)
                pe.wait_ge(h_ready, KT)
                if n >= 2:
                    pe.wait_ge(h_tok_ready, n - 1)
                if n == 1:
                    pe.wait_ge(h_acc, KT + 1)
                    nc.tensor.matmul(X1[:, 0:NQ], ones[:, :], ss2_acc[:], start=True, stop=True).then_inc(h_ss_done, 1)
                for j in range(4):
                    k = 4 * quarter + j
                    last = nc.tensor.transpose(ps_x[2 + n % 2][:, j * P:(j + 1) * P],
                                               xt[:, k, N_META + tok * P:N_META + (tok + 1) * P], ident[:, :])
                last.then_inc(h_turned, 1)
            pe.wait_ge(h_lo_ready, KT)
            with pe.Fori(0, FT // 2) as i:
                for k in range(8):
                    b, q = divmod(k, 4)
                    if q == 0:
                        pe.wait_ge(up_scaled, i * 4 - 2 + 2 * b + START)
                    unit(i * 8 + U_UP + k, q, b, xn)

            pe.wait_ge(g_ready, FT // 2 + START)
            for b in range(DN_BLOCKS):
                if b >= 2:
                    pe.wait_ge(ev("dn_copied"), 2 * b - 2)
                for q in range(DN_U):
                    k = b * DN_U + q
                    pe.wait_ge(lo_done, U_DN + k + 1 + RING)
                    for tok in range(2):
                        dst = ps_g[:, 2 * (b % 2) + tok, :]
                        for t in range(DN_K):
                            f = q * DN_K + t
                            cols = slice(t * 512, (t + 1) * 512)
                            gh, gl = (a[:, f, tok * P:(tok + 1) * P] for a in (g_hi, g_lo))
                            nc.tensor.matmul(dst, gh, w_hi[:, k % RING, cols], start=(f == 0), stop=False)
                            nc.tensor.matmul(dst, gl, w_hi[:, k % RING, cols], start=False, stop=False)
                            last = nc.tensor.matmul(dst, gh, w_lo[:, k % RING, cols], start=False, stop=(f == FT - 1))
                    last.then_inc(unit_done, 1)


_INS = ['x', 'meta', 'w_in', 'b_in', 'mh_norm', 'sinks', 'w_a', 'w_b', 'w_out', 'g_pre_mix', 'g_post_mix',
        'g_pre_ffn', 'g_post_ffn', 'w_up', 'conv_w', 'conv_b', 'w_down']
_OUTS = [((1, SEQ, D), 'float32')]


def kernel(**inputs):
    import numpy as _np
    import concourse.bacc as _bacc
    from concourse import mybir as _mybir
    from concourse.bass_utils import run_bass_kernel_spmd as _run

    nc = _bacc.Bacc("TRN2", target_bir_lowering=False, num_devices=1)
    arrays, args = {}, []
    for name in _INS:
        a = _np.ascontiguousarray(inputs[name])
        arrays[f"in_{name}_dram"] = a
        args.append(nc.dram_tensor(f"in_{name}_dram", a.shape, _mybir.dt.from_np(a.dtype), kind="ExternalInput").ap())
    for i, (shape, dtype) in enumerate(_OUTS):
        dt = _mybir.dt.from_np(_np.dtype(dtype))
        args.append(nc.dram_tensor(f"out_{i}_dram", shape, dt, kind="ExternalOutput").ap())
    layer(nc, *args)
    r = _run(nc, [arrays], core_ids=[0])
    return r.results[0]["out_0_dram"]
```

```python
from contextlib import ExitStack

import concourse.bass as bass
from concourse import mybir

F32 = mybir.dt.float32
F32R = mybir.dt.float32r
ACT = mybir.ActivationFunctionType
ALU = mybir.AluOpType
AX_X = mybir.AxisListType.X

P = 128
D = 2048
KT = D // P
N_META = 16
SEQ = 256
T = N_META + SEQ
CONV_W = 3
QO = N_META - (CONV_W - 1)
NQ = T - QO
CHUNK = 64
M_HEADS = 8
A_HEADS, A_KV, DH = 32, 4, 64
D_FF = 256 * ((8 * D // 3 + 255) // 256)
FT = D_FF // P
EPS = 1e-6
NEG = -1e30

C_Q, C_K, C_V = 0, 1024, 2048
C_GATE = 4096
C_MO = C_GATE + 2 * M_HEADS
C_AQ = C_MO + D
C_AK = C_AQ + D
C_AV = C_AK + A_KV * DH
C_GA = C_AV + A_KV * DH
C_GB = C_GA + D
B_Q, B_K, B_V, B_MO, B_AQ, B_AK, B_AV, B_GA, B_GB, B_ALL = 0, 8, 16, 32, 48, 64, 66, 68, 84, 100
G_PRE_MIX, G_POST_MIX, G_PRE_FFN, G_MH = 0, 16, 32, 48

RING = 4
START = 3
UK = 4
BLK = 256
U_M, U_KV, U_AW, U_P2, U_WO, U_UP, U_DN = 0, 128, 136, 200, 264, 296, 472
Q_M, Q_KV, Q_AW, Q_P2, Q_WO, Q_UP, Q_DN = 0, 32, 34, 50, 66, 74, 118
DN_K = 2
DN_U = FT // DN_K
DN_BLOCKS = D // 512
STEPS = 9


def layer(nc, x, meta, w_in, b_in, mh_norm, sinks, w_a, w_b, w_out, g_pre_mix, g_post_mix,
          g_pre_ffn, g_post_ffn, w_up, conv_w, conv_b, w_down, out):
    with ExitStack() as ctx:
        base = [16512]

        def put(name, shape, dt=F32, at=None):
            size = 4
            for n in shape[1:]:
                size *= n
            size = (size + 31) // 32 * 32
            if at is None:
                at = base[0]
                base[0] += size
            assert at + size <= 229344, name
            return nc.alloc_sbuf_tensor_at(name, list(shape), dt, offset=at)

        def sem(name):
            return ctx.enter_context(nc.semaphore(name))

        raw = put("raw", [P, RING, 1024])
        w_hi = put("w_hi", [P, RING, 1024], F32R)
        w_lo = put("w_lo", [P, RING, 1024], F32R)
        xn_at = base[0]
        xn_hi = put("xn_hi", [P, KT, T], F32R)
        xn_lo = put("xn_lo", [P, KT, T], F32R)
        xt_at = base[0]
        xt = put("xt", [P, KT, T])
        big_at = base[0]
        base[0] += 2 * FT * SEQ * 4
        g_hi = put("g_hi", [P, FT, SEQ], F32R, big_at)
        g_lo = put("g_lo", [P, FT, SEQ], F32R, big_at + FT * SEQ * 4)
        half = KT * NQ * 4
        ya_hi = put("ya_hi", [P, KT, NQ], F32R, big_at)
        ya_lo = put("ya_lo", [P, KT, NQ], F32R, big_at + half)
        yb_hi = put("yb_hi", [P, KT, NQ], F32R, big_at + 2 * half)
        yb_lo = put("yb_lo", [P, KT, NQ], F32R, big_at + 3 * half)
        z1 = put("z1", [P, KT, NQ], F32, big_at + 4 * half)
        z_hi, z_lo = ya_hi, ya_lo
        spare_at = big_at + 5 * half
        ident = put("ident", [P, P])
        ones = put("ones", [P, P])
        bias_t = put("bias_t", [P, B_ALL])
        half_bias = put("half_bias", [P, B_ALL])
        gains = put("gains", [P, 64])
        half_gain = put("half_gain", [P, KT])
        conv_t = put("conv_t", [P, 4, 2 * FT])
        cst = put("cst", [P, 4])
        small = put("small", [P, 64])
        EPS_C, ONE_C = cst[:, 0:1], cst[:, 1:2]
        tmp_at = base[0]

        class Area:
            def __init__(self, at):
                self.at = at

            def put(self, name, shape, dt=F32):
                size = 4
                for n in shape[1:]:
                    size *= n
                size = (size + 31) // 32 * 32
                a = self.at
                self.at += size
                return put(name, shape, dt, a)

        CHUNKS = ((0, P), (1, P), (2, N_META))
        area = Area(big_at + 2 * half)
        xs = area.put("xs", [P, 3, D])
        area = Area(big_at)
        GC = 40
        wg = area.put("wg", [P, KT, 16])
        wg_hi = area.put("wg_hi", [P, KT, GC], F32R)
        wg_lo = area.put("wg_lo", [P, KT, GC], F32R)
        bias_rows = area.put("bias_rows", [B_ALL, P])
        gain_rows = area.put("gain_rows", [64, P])
        conv_rows = area.put("conv_rows", [2 * FT, 4, P])
        sq_junk = area.put("sq_junk", [P, D])
        m_row = area.put("m_row", [M_HEADS, T])
        area = Area(big_at + 4 * half)
        RC = 32 + M_HEADS
        xn_tok2 = area.put("xn_tok2", [N_META, D])
        i_pre = area.put("i_pre", [M_HEADS, T])
        f_pre = area.put("f_pre", [M_HEADS, T])
        f_neg = area.put("f_neg", [M_HEADS, T])
        f_soft = area.put("f_soft", [M_HEADS, T])
        b_cum = area.put("b_cum", [M_HEADS, T])
        u_row = area.put("u_row", [M_HEADS, T])
        u_max = area.put("u_max", [M_HEADS, T])
        assert area.at <= spare_at

        xn_tok = [put("xn_tok0", [P, D], F32, tmp_at), put("xn_tok1", [P, D], F32, tmp_at + D * 4), xn_tok2]

        area = Area(spare_at)
        mask = area.put("mask", [P, T])
        neg_cut = area.put("neg_cut", [RC, T], F32R)
        m_cut = area.put("m_cut", [RC, T], F32R)
        q_t = area.put("q_t", [P, NQ])
        k_t = area.put("k_t", [P, T])
        u_col = area.put("u_col", [P, 3, M_HEADS])
        sel = area.put("sel", [RC, P], F32R)
        picks = area.put("picks", [RC, M_HEADS])
        em = area.put("em", [P, NQ])
        assert area.at <= big_at + 2 * FT * SEQ * 4
        area = Area(tmp_at)
        SP1, SP2 = NQ, NQ + T - P
        probs = area.put("probs", [P, SP2 + 16])
        v_t = area.put("v_t", [P, 2, T])
        v_tok = area.put("v_tok", [P, 2, BLK])
        v_tok2 = area.put("v_tok2", [16, BLK])
        den_r = area.put("den_r", [P, NQ])
        hm = area.put("hm", [P, 2, NQ])
        hm_sq = area.put("hm_sq", [P, 2, NQ])
        sig_o = area.put("sig_o", [P, 2, NQ])
        rs_m = area.put("rs_m", [P, NQ])
        hm_ss = area.put("hm_ss", [P, NQ])

        area = Area(spare_at)
        q_pairs = area.put("q_pairs", [P, 4, NQ])
        v_group = area.put("v_group", [P, 4, DH])
        k_group = area.put("k_group", [P, T])
        q_meta = area.put("q_meta", [P, 2, 4])
        prob_t0 = area.put("prob_t0", [N_META, 16])
        probs0 = area.put("probs0", [8, 2, N_META])
        sink_col = area.put("sink_col", [P, A_HEADS // 2])
        sink_meta = area.put("sink_meta", [8, A_KV, 2])
        att = area.put("att", [P, 16])
        att0 = area.put("att0", [8, 16])
        assert area.at <= big_at + 2 * FT * SEQ * 4
        area = Area(tmp_at)
        k_dup = area.put("k_dup", [P, A_KV, T])
        v_win = area.put("v_win", [P, A_KV, 4, DH])
        av_t = area.put("av_t", [P, 2, T])
        probs_a = area.put("probs_a", [P, 2, 2, 144])
        prob_t = area.put("prob_t", [P, 2, P])
        prob_tm = area.put("prob_tm", [N_META, 2, P])

        area = Area(tmp_at)
        gate_b = area.put("gate_b", [P, 4, NQ])
        zt = area.put("zt", [P, 4, NQ])
        area = Area(tmp_at)
        rs2 = area.put("rs2", [P, NQ])
        ffn_at = area.at
        y_sq = area.put("y_sq", [P, 2, NQ])
        ss_acc = area.put("ss_acc", [P, NQ])
        rs1 = area.put("rs1", [P, NQ])
        h_a = area.put("h_a", [P, 4, NQ])
        area = Area(ffn_at)
        u_t = area.put("u_t", [P, 4, NQ])
        c_t = area.put("c_t", [P, 4, SEQ])
        ge_t = area.put("ge_t", [P, 2, SEQ])
        y_tok_st = put("y_tok_st", [P, 2, D], F32, big_at)
        h_tok = put("h_tok", [P, 2, D], F32, xn_at)
        area = Area(xn_at + KT * T * 4)
        gain_b = area.put("gain_b", [P, D])
        dn_junk = area.put("dn_junk", [P, 2, 512])
        x_tok = put("x_tok", [P, 2, D], F32, tmp_at)
        y_dn = put("y_dn", [P, 2, D], F32, xt_at)
        u_scratch = nc.dram_tensor("u_scratch", [M_HEADS, T], F32).ap()
        y_scratch = nc.dram_tensor("y_scratch", [P, 2, D], F32).ap()

        ps_g = ctx.enter_context(nc.psum_tensor("ps_g", [P, 4, 512], F32))
        ps_x = [ctx.enter_context(nc.psum_tensor(f"ps_x{n}", [P, 512], F32)) for n in range(4)]
        X0, X1, X2, X3 = ps_x

        raw_full = [sem(f"raw_full{n}") for n in range(RING)]
        hi_done = sem("hi_done")
        lo_done = sem("lo_done")
        unit_done = sem("unit_done")
        bank_free = [sem("bank_free0"), sem("bank_free1")]
        x_in = [sem(f"x_in{n}") for n in range(3)]
        wg_in, gain_in, bias_in, conv_in = sem("wg_in"), sem("gain_in"), sem("bias_in"), sem("conv_in")
        const_ready, zero_ready = sem("const_ready"), sem("zero_ready")
        names = {}

        def ev(name):
            if name not in names:
                names[name] = sem(name)
            return names[name]

        gains_turned, par_turned = ev("gains_turned"), ev("par_turned")
        gains_ready, par_ready, half_ready = ev("gains_ready"), ev("par_ready"), ev("half_ready")
        sum_sq, root_ready, rs_ready = ev("sum_sq"), ev("root_ready"), ev("rs_ready")
        x_turned, xt_ready = ev("x_turned"), ev("xt_ready")
        xn_first, xn_scalar, xn_vector, xn_turned = ev("xn_first"), ev("xn_scalar"), ev("xn_vector"), ev("xn_turned")
        xn_hi_ready, xn_lo_ready = ev("xn_hi_ready"), ev("xn_lo_ready")
        wg_zeroed, wg_hi_ready, wg_ready = ev("wg_zeroed"), ev("wg_hi_ready"), ev("wg_ready")
        gates_done, pre_ready, f_neg_ready = ev("gates_done"), ev("pre_ready"), ev("f_neg_ready")
        exp_f_ready, soft_ready, f_ready = ev("exp_f_ready"), ev("soft_ready"), ev("f_ready")
        rows_ready, u_row_ready, u_col_in = ev("rows_ready"), ev("u_row_ready"), ev("u_col_in")
        pe_held, pool_held, sp_held = ev("pe_held"), ev("pool_held"), ev("sp_held")
        meta_scored = ev("meta_scored")
        rows_zeroed, picks_ready, m_row_ready, rows_cut = ev("rows_zeroed"), ev("picks_ready"), ev("m_row_ready"), ev("rows_cut")
        hm_ss_ready = ev("hm_ss_ready")
        u_stored, b_cum_ready, u_max_ready = ev("u_stored"), ev("b_cum_ready"), ev("u_max_ready")

        qk_ready, v_t_ready, sel_ready = ev("qk_ready"), ev("v_t_ready"), ev("sel_ready")
        scores_done, expo_ready, decay_ready = ev("scores_done"), ev("expo_ready"), ev("decay_ready")
        em_ready, probs_ready = ev("em_ready"), ev("probs_ready")
        v_turned, v_tok_ready = ev("v_turned"), ev("v_tok_ready")
        heads_done, den_ready, rden_ready, hm_ready = ev("heads_done"), ev("den_ready"), ev("rden_ready"), ev("hm_ready")
        hm_sq_ready, hm_ss_done, hm_root, hm_rs = ev("hm_sq_ready"), ev("hm_ss_done"), ev("hm_root"), ev("hm_rs")
        tanh_o_ready, sig_o_ready, normed_ready = ev("tanh_o_ready"), ev("sig_o_ready"), ev("normed_ready")
        ya_f_ready, ya_hi_ready, ya_ready = ev("ya_f_ready"), ev("ya_hi_ready"), ev("ya_ready")

        k_dup_ready, av_t_ready, av_turned, v_win_ready = ev("k_dup_ready"), ev("av_t_ready"), ev("av_turned"), ev("v_win_ready")
        sinks_in = ev("sinks_in")
        v_group_ready, q_pairs_ready = ev("v_group_ready"), ev("q_pairs_ready")
        att_scored, att_max, att_maxed, att_nm = ev("att_scored"), ev("att_max"), ev("att_maxed"), ev("att_nm")
        att_sum_in, att_exp, att_den, att_rec, att_probs = ev("att_sum_in"), ev("att_exp"), ev("att_den"), ev("att_rec"), ev("att_probs")
        att_turned, att_prob_t, att_mixed, att_yb_hi, att_yb = ev("att_turned"), ev("att_prob_t"), ev("att_mixed"), ev("att_yb_hi"), ev("att_yb")
        wa_gated = ev("wa_gated")

        gate_b_ready, zt_ready, z_f_ready, z_hi_ready, z_ready = ev("gate_b_ready"), ev("zt_ready"), ev("z_f_ready"), ev("z_hi_ready"), ev("z_ready")
        y_sq_ready, y_acc, y_ss_done, y_root, y_rs = ev("y_sq_ready"), ev("y_acc"), ev("y_ss_done"), ev("y_root"), ev("y_rs")
        y_turned, y_stored, y_loaded = ev("y_turned"), ev("y_stored"), ev("y_loaded")
        y_tok_ready = [ev("y_tok_vector"), ev("y_tok_scalar")]
        h_a_ready, h_even_ready, h_odd_ready = ev("h_a_ready"), ev("h_even_ready"), ev("h_odd_ready")
        h_hi_ready, h_lo_ready, h_sq_ready, h_sum = ev("h_hi_ready"), ev("h_lo_ready"), ev("h_sq_ready"), ev("h_sum")
        h_ss_done, h_root, h_rs = ev("h_ss_done"), ev("h_root"), ev("h_rs")
        gain_b_in, x_tok_in, h_tok_ready = ev("gain_b_in"), ev("x_tok_in"), ev("h_tok_ready")
        up_scaled, up_tap2, up_tap1, up_tap0, gelu_ready = ev("up_scaled"), ev("up_tap2"), ev("up_tap1"), ev("up_tap0"), ev("gelu_ready")
        g_f_ready, g_hi_ready, g_ready = ev("g_f_ready"), ev("g_hi_ready"), ev("g_ready")
        dn_squared, dn_scaled, dn_ss_sum, dn_root, dn_rs = ev("dn_squared"), ev("dn_scaled"), ev("dn_ss_sum"), ev("dn_root"), ev("dn_rs")
        out_vector, out_normed, out_pool, out_stored = ev("out_vector"), ev("out_normed"), ev("out_pool"), ev("out_stored")
        out_last_stored = ev("out_last_stored")

        from_start = (scores_done, ya_ready, zt_ready, g_f_ready, g_ready, z_ready, tanh_o_ready, bank_free[1], hm_root,
                      wa_gated, att_prob_t, att_yb, att_mixed, y_sq_ready, up_scaled)

        block = ctx.enter_context(nc.Block())

        def chunks_of(e):
            return (1, 2) if e % 2 == 0 else (3, 4)

        def window(c):
            return (N_META, CHUNK) if c == 1 else (N_META + CHUNK * (c - 2), 2 * CHUNK)

        @block.sync
        def _(sp):
            sp.dma_start(xs[0:N_META, 2, :], x[0, 2 * P - N_META:SEQ, :]).then_inc(x_in[2], 16)
            sp.dma_start(xs[0:N_META, 0, :], meta).then_inc(x_in[0], 16)
            sp.dma_start(xs[N_META:P, 0, :], x[0, 0:P - N_META, :]).then_inc(x_in[0], 16)
            sp.dma_start(xs[:, 1, :], x[0, P - N_META:2 * P - N_META, :]).then_inc(x_in[1], 16)
            sp.dma_start(wg[:], w_in[0, :, C_GATE:C_MO].rearrange("(t p) n -> p t n", p=P)).then_inc(wg_in, 16)

            def units_of(u0, w, col, col2=None):
                for q in range(KT // UK):
                    rows = w[q * UK * P:(q + 1) * UK * P, :]
                    dst = raw[:, q, :].rearrange("p (t n) -> p t n", t=UK)
                    sp.wait_ge(lo_done, u0 + q + 1)
                    nc.sync.sem_inc(sp_held, 1)
                    if col2 is None:
                        sp.dma_start(dst, rows[:, bass.ds(col, BLK)].rearrange("(t p) n -> p t n", p=P)).then_inc(raw_full[q], 16)
                    else:
                        for n, c in enumerate((col, col2)):
                            sp.dma_start(dst[:, :, n * P:(n + 1) * P],
                                         rows[:, bass.ds(c, P)].rearrange("(t p) n -> p t n", p=P)).then_inc(raw_full[q], 16)

            w = w_in[0]
            with sp.Fori(0, M_HEADS) as h:
                units_of(h * 16 + U_M, w, h * P + C_Q, h * P + C_K)
                units_of(h * 16 + U_M + 4, w, h * BLK + C_V)
                units_of(h * 16 + U_M + 8, w, h * BLK + C_MO)
                units_of(h * 16 + U_M + 12, w, h * BLK + C_GA)
            units_of(U_KV, w, C_AV, C_AV + P)
            units_of(U_KV + 4, w, C_AK)
            with sp.Fori(0, A_KV) as g:
                units_of(g * 16 + U_AW, w, g * (2 * BLK) + C_AQ)
                units_of(g * 16 + U_AW + 4, w, g * (2 * BLK) + C_AQ + BLK)
                units_of(g * 16 + U_AW + 8, w_a[0], g * (2 * BLK))
                units_of(g * 16 + U_AW + 12, w_a[0], g * (2 * BLK) + BLK)
            with sp.Fori(0, 4) as i:
                units_of(i * 16 + U_P2, w, i * (2 * BLK) + C_GB)
                units_of(i * 16 + U_P2 + 4, w, i * (2 * BLK) + C_GB + BLK)
                units_of(i * 16 + U_P2 + 8, w_b[0], i * (2 * BLK))
                units_of(i * 16 + U_P2 + 12, w_b[0], i * (2 * BLK) + BLK)
            with sp.Fori(0, 8) as i:
                units_of(i * 4 + U_WO, w_out[0], i * BLK)
            with sp.Fori(0, FT // 2) as i:
                units_of(i * 8 + U_UP, w_up[0], i * BLK)
                units_of(i * 8 + U_UP + 4, w_up[0], i * BLK + D_FF)
            with sp.Fori(0, DN_BLOCKS // 2) as i:
                for k in range(2 * DN_U):
                    b, q = divmod(k, DN_U)
                    src = w_down[0][q * DN_K * P:(q + 1) * DN_K * P, bass.ds(i * 1024 + b * 512, 512)]
                    sp.wait_ge(lo_done, i * (2 * DN_U) + U_DN + k + 1)
                    nc.sync.sem_inc(sp_held, 1)
                    sp.dma_start(raw[:, k % RING, :].rearrange("p (t n) -> p t n", t=DN_K),
                                 src.rearrange("(t p) n -> p t n", p=P)).then_inc(raw_full[k % RING], 16)
            sp.wait_ge(out_vector, 4)
            sp.dma_start(out[0, 0:P, :], h_tok[:, 0, :]).then_inc(out_stored, 16)

        @block.gpsimd
        def _(pool):
            nc.gpsimd.memset(ident[:], 0.0).then_inc(zero_ready, 1)
            nc.gpsimd.memset(mask[:], 0.0).then_inc(zero_ready, 1)
            nc.gpsimd.memset(cst[:, 0:1], EPS).then_inc(const_ready, 1)
            nc.gpsimd.memset(cst[:, 1:2], 1.0).then_inc(const_ready, 1)
            pool.wait_ge(zero_ready, 1)
            nc.gpsimd.affine_select(out=ident[:], in_=ident[:], compare_op=ALU.not_equal, fill=1.0, base=0,
                                    pattern=[[-1, P]], channel_multiplier=1).then_inc(const_ready, 1)
            nc.gpsimd.memset(ones[:], 1.0).then_inc(const_ready, 1)
            nc.gpsimd.memset(wg_hi[:].bitcast(F32), 0.0).then_inc(wg_zeroed, 1)
            nc.gpsimd.memset(wg_lo[:].bitcast(F32), 0.0).then_inc(wg_zeroed, 1)
            nc.gpsimd.memset(neg_cut[:].bitcast(F32), 0.0).then_inc(rows_zeroed, 1)
            nc.gpsimd.memset(m_cut[:].bitcast(F32), 0.0).then_inc(rows_zeroed, 1)
            for s in from_start:
                nc.gpsimd.sem_inc(s, START)
            pool.wait_ge(const_ready, 3)
            nc.gpsimd.tensor_tensor(picks[:], ident[0:RC, 0:M_HEADS], ident[0:RC, 32:RC], ALU.add).then_inc(picks_ready, 1)
            pool.wait_ge(picks_ready, 1)
            pool.wait_ge(zero_ready, 2)
            nc.gpsimd.affine_select(out=mask[:], in_=mask[:], compare_op=ALU.is_ge, fill=NEG, base=0,
                                    pattern=[[1, T]], channel_multiplier=-1).then_inc(const_ready, 1)
            for n, gain in enumerate((g_pre_mix[0], g_post_mix[0], g_pre_ffn[0])):
                pool.dma_start(gain_rows[16 * n:16 * n + 16, :], gain.rearrange("(m p) -> m p", p=P)).then_inc(gain_in, 16)
            pool.dma_start(gain_rows[48:64, :], mh_norm[0].rearrange("h (c p) -> (h c) p", p=P)).then_inc(gain_in, 16)
            pool.dma_start(bias_rows[0:32, :], b_in[0, 0:C_GATE].rearrange("(m p) -> m p", p=P)).then_inc(bias_in, 16)
            pool.dma_start(bias_rows[32:B_ALL, :], b_in[0, C_MO:].rearrange("(m p) -> m p", p=P)).then_inc(bias_in, 16)
            with nc.allow_non_contiguous_dma(reason="16 biases of the gates, once"):
                pool.dma_start(small[0:8, 0:1], b_in[0, C_GATE:C_GATE + 8].rearrange("(p a) -> p a", a=1)).then_inc(bias_in, 16)
                pool.dma_start(small[32:40, 0:1], b_in[0, C_GATE + 8:C_MO].rearrange("(p a) -> p a", a=1)).then_inc(bias_in, 16)
            pool.dma_start(conv_rows[:, 0:3, :], conv_w[0].rearrange("j (m p) -> m j p", p=P)).then_inc(conv_in, 16)
            pool.dma_start(conv_rows[:, 3, :], conv_b[0].rearrange("(m p) -> m p", p=P)).then_inc(conv_in, 16)
            pool.wait_ge(u_row_ready, 1)
            pool.dma_start(u_scratch, u_row[:]).then_inc(u_stored, 16)
            pool.wait_ge(u_stored, 16)
            with nc.allow_non_contiguous_dma(reason="2176 values of the gates, once"):
                for st, w in ((0, P), (1, P), (2, N_META)):
                    pool.dma_start(u_col[0:w, st, :], u_scratch[:, st * P:st * P + w].rearrange("h p -> p h")).then_inc(u_col_in, 16)
            with pool.Fori(0, M_HEADS) as h:
                pool.wait_ge(scores_done, h + START)
                nc.gpsimd.tensor_copy(sel[:], picks[:, bass.ds(h, 1)].to_broadcast([RC, P])).then_inc(sel_ready, 1)
                pool.wait_ge(tanh_o_ready, h + 1 + START)
                nc.gpsimd.sem_inc(pool_held, 1)
                nc.gpsimd.tensor_scalar(sig_o[:], sig_o[:], 0.5, 0.5, ALU.mult, ALU.add).then_inc(sig_o_ready, 1)
                pool.wait_ge(hm_sq_ready, h + 1)
                nc.gpsimd.tensor_tensor(hm_ss[:], hm_sq[:, 0, :], hm_sq[:, 1, :], ALU.add).then_inc(hm_ss_ready, 1)
                pool.wait_ge(normed_ready, h + 1)
                pool.wait_ge(sig_o_ready, h + 1)
                nc.gpsimd.tensor_tensor(hm_sq[:], hm_sq[:], sig_o[:], ALU.mult).then_inc(ya_f_ready, 1)
                pool.wait_ge(ya_f_ready, h + 1)
                hi = ya_hi[:, bass.ds(h * 2, 2), :]
                nc.gpsimd.tensor_copy(hi, hm_sq[:]).then_inc(ya_hi_ready, 1)
                pool.wait_ge(ya_hi_ready, h + 1)
                nc.gpsimd.tensor_tensor(ya_lo[:, bass.ds(h * 2, 2), :], hm_sq[:], hi.bitcast(F32), ALU.subtract).then_inc(ya_ready, 1)

            pool.wait_ge(v_win_ready, 4)
            pool.wait_ge(k_dup_ready, 1)
            with pool.Fori(0, A_KV) as g:
                pool.wait_ge(att_mixed, g * STEPS + START)
                nc.gpsimd.tensor_copy(k_group[:], k_dup[:, bass.ds(g, 1), :].rearrange("p g n -> p (g n)")).then_inc(v_group_ready, 1)
                nc.gpsimd.tensor_copy(v_group[:], v_win[:, bass.ds(g, 1), :, :].rearrange("p g w d -> p (g w) d")).then_inc(v_group_ready, 1)

            with pool.Fori(0, 4) as i:
                for m in range(4):
                    n = i * 4 + m + 1
                    t = bass.ds(i * 4 + m, 1)
                    zf = zt[:, m:m + 1, :]
                    pool.wait_ge(zt_ready, n + START)
                    nc.gpsimd.tensor_tensor(zf, zf, z1[:, t, :], ALU.add).then_inc(z_f_ready, 1)
                    pool.wait_ge(z_f_ready, n)
                    nc.gpsimd.tensor_copy(z_hi[:, t, :], zf).then_inc(z_hi_ready, 1)
                    pool.wait_ge(z_hi_ready, n)
                    nc.gpsimd.tensor_tensor(z_lo[:, t, :], zf, z_hi[:, t, :].bitcast(F32), ALU.subtract).then_inc(z_ready, 1)

            pool.wait_ge(z_ready, 16 + START)
            nc.gpsimd.memset(ss_acc[:], 0.0).then_inc(y_acc, 1)
            with pool.Fori(0, 8) as i:
                for m in range(2):
                    pool.wait_ge(y_sq_ready, i * 2 + m + 1 + START)
                    pool.wait_ge(y_acc, i * 2 + m + 1)
                    nc.gpsimd.tensor_tensor(ss_acc[:], ss_acc[:], y_sq[:, m, :], ALU.add).then_inc(y_acc, 1)

            for j in range(KT // 2):
                k = 2 * j + 1
                pool.wait_ge(h_a_ready, k + 1)
                hk = xt[:, k, QO:T]
                nc.gpsimd.tensor_tensor(hk, hk, h_a[:, k % 4, :], ALU.add).then_inc(h_odd_ready, 1)
            pool.wait_ge(y_tok_ready[0], 3)
            pool.wait_ge(y_tok_ready[1], 5)
            pool.dma_start(y_scratch, y_tok_st[:]).then_inc(y_stored, 16)
            pool.wait_ge(h_sq_ready, 2)
            nc.gpsimd.tensor_tensor(z1[:, 0:4, :], z1[:, 0:4, :], z1[:, 4:8, :], ALU.add).then_inc(h_sum, 1)
            for j in (2, 3):
                pool.wait_ge(h_sq_ready, j + 1)
                pool.wait_ge(h_sum, j - 1)
                nc.gpsimd.tensor_tensor(z1[:, 0:4, :], z1[:, 0:4, :], z1[:, 4 * j:4 * j + 4, :], ALU.add).then_inc(h_sum, 1)
            pool.wait_ge(h_sum, 3)
            nc.gpsimd.tensor_tensor(z1[:, 0:2, :], z1[:, 0:2, :], z1[:, 2:4, :], ALU.add).then_inc(h_sum, 1)
            pool.wait_ge(h_sum, 4)
            nc.gpsimd.tensor_tensor(z1[:, 0:1, :], z1[:, 0:1, :], z1[:, 1:2, :], ALU.add).then_inc(h_sum, 1)

            pool.wait_ge(y_stored, 16)
            pool.wait_ge(h_ss_done, 1)
            with pool.Fori(0, FT // 2) as i:
                pool.wait_ge(gelu_ready, i * 2 + 2)
                pool.wait_ge(up_tap0, i * 4 + 4)
                t = bass.ds(i * 2, 2)
                nc.gpsimd.tensor_tensor(ge_t[:], ge_t[:], c_t[:, 2:4, :], ALU.mult).then_inc(g_f_ready, 1)
                pool.wait_ge(g_f_ready, i + 1 + START)
                nc.gpsimd.tensor_copy(g_hi[:, t, :], ge_t[:]).then_inc(g_hi_ready, 1)
                pool.wait_ge(g_hi_ready, i + 1)
                nc.gpsimd.tensor_tensor(g_lo[:, t, :], ge_t[:], g_hi[:, t, :].bitcast(F32), ALU.subtract).then_inc(g_ready, 1)

            pool.wait_ge(unit_done, RING + U_DN)
            pool.dma_start(h_tok[:], y_scratch).then_inc(y_loaded, 16)
            pool.dma_start(gain_b[:], g_post_ffn[0].partition_broadcast(P)).then_inc(gain_b_in, 16)
            pool.wait_ge(g_ready, FT // 2 + START)
            pool.dma_start(x_tok[:], x[0].rearrange("(t p) d -> p t d", p=P)).then_inc(x_tok_in, 16)

            for q in (2, 3):
                cols = slice(q * 512, q * 512 + 512)
                pool.wait_ge(out_normed, q - 1)
                nc.gpsimd.tensor_tensor(y_dn[:, 1, cols], y_dn[:, 1, cols], h_tok[:, 1, cols], ALU.add).then_inc(out_pool, 1)
            pool.wait_ge(out_pool, 2)
            pool.dma_start(out[0, P:SEQ, 1024:2048], y_dn[:, 1, 1024:2048]).then_inc(out_last_stored, 16)
            pool.wait_ge(out_stored, 2 * 16)
            pool.wait_ge(out_last_stored, 16)

        @block.scalar
        def _(act):
            act.wait_ge(const_ready, 1)
            nc.scalar.activation(small[:, 46:47], EPS_C, ACT.Sqrt)
            for n, (c, w) in enumerate((CHUNKS[2], CHUNKS[0], CHUNKS[1])):
                act.wait_ge(x_in[c], 32 if c == 0 else 16)
                nc.scalar.activation(sq_junk[0:w, :], xs[0:w, c, :], ACT.Square,
                                     accum_out=small[0:w, 8 + c:9 + c]).then_inc(sum_sq, 1)
                act.wait_ge(sum_sq, n + 1)
                nc.scalar.activation(small[0:w, 16 + c:17 + c], small[0:w, 8 + c:9 + c], ACT.Sqrt, scale=1.0 / D,
                                     bias=cst[0:w, 0:1]).then_inc(root_ready, 1)
            act.wait_ge(rs_ready, 3)
            for q in (1, 3):
                cols = slice(q * 512, q * 512 + 512)
                nc.scalar.activation(xn_tok[1][:, cols], xs[:, 1, cols], ACT.Copy, scale=small[:, 21:22]).then_inc(xn_scalar, 1)
            act.wait_ge(wg_in, 16)
            act.wait_ge(wg_zeroed, 2)
            nc.scalar.copy(wg_hi[:, :, 0:8], wg[:, :, 0:8]).then_inc(wg_hi_ready, 1)
            nc.scalar.copy(wg_hi[:, :, 32:40], wg[:, :, 8:16]).then_inc(wg_hi_ready, 1)
            act.wait_ge(gains_ready, 1)

            def hi(u, s, n):
                act.wait_ge(raw_full[s], n * 16)
                act.wait_ge(unit_done, u + 1)
                nc.scalar.copy(w_hi[:, s, :], raw[:, s, :]).then_inc(hi_done, 1)

            def split(i, u0, per, k):
                u = k + RING
                if u0 == U_M:
                    loads = i * 5 + 1 + u // RING + 1 + (u // 16)
                else:
                    loads = i * (per // RING) + (u0 + u) // RING + 1 + M_HEADS + 1
                hi(i * per + u0 + u, u % RING, loads)

            for k in range(KT):
                act.wait_ge(xn_turned, k + 1)
                nc.scalar.activation(xn_hi[:, k, :], ps_g[:, k % 4, 0:T], ACT.Copy,
                                     scale=gains[:, G_PRE_MIX + k:G_PRE_MIX + k + 1]).then_inc(xn_hi_ready, 1)
                if k in (1, 3, 5, 7):
                    hi(k // 2, k // 2, 2)
            act.wait_ge(f_neg_ready, 1)
            nc.scalar.activation(f_soft[:], f_neg[:], ACT.Exp).then_inc(exp_f_ready, 1)
            act.wait_ge(exp_f_ready, 1)
            nc.scalar.activation(f_soft[:], f_soft[:], ACT.Ln, bias=cst[0:M_HEADS, 1:2]).then_inc(soft_ready, 1)

            with act.Fori(0, M_HEADS) as h:
                for k in range(16):
                    split(h, U_M, 16, k)
                    if k == 4:
                        act.wait_ge(scores_done, h + 1 + START)
                        nc.scalar.activation(em[:], X2[:, 0:NQ], ACT.Exp, scale=-1.0).then_inc(em_ready, 1)
                        act.wait_ge(expo_ready, h + 1)
                        act.wait_ge(u_col_in, 48)
                        for st, c0, c1, w in ((0, 0, SP1, P), (1, SP1, SP2, P), (2, SP2, SP2 + 16, N_META)):
                            nc.scalar.activation(probs[0:w, c0:c1], probs[0:w, c0:c1], ACT.Exp,
                                                 bias=u_col[0:w, st, bass.ds(h, 1)]).then_inc(decay_ready, 1)
                    if k == 8:
                        act.wait_ge(v_turned, h + 1)
                        nc.scalar.copy(v_tok[:], X3[:, :].rearrange("p (s v) -> p s v", s=2)).then_inc(v_tok_ready, 1)
                        nc.scalar.copy(v_tok2[:], X2[0:N_META, 0:BLK]).then_inc(v_tok_ready, 1)
                    if k == 11:
                        act.wait_ge(unit_done, h * 16 + U_M + k + 1 + RING)
                        act.wait_ge(ya_ready, h + START)
                        for m in range(2):
                            last = nc.scalar.activation(sig_o[:, m, :], ps_g[:, m, 0:NQ], ACT.Tanh, scale=0.5,
                                                        bias=half_bias[:, bass.ds(h * 2 + B_MO + m, 1)])
                        last.then_inc(tanh_o_ready, 1)
                        act.wait_ge(hm_ready, h + 1)
                        nc.scalar.activation(hm_sq[:], hm[:], ACT.Square).then_inc(hm_sq_ready, 1)
                    if k == 14:
                        act.wait_ge(hm_ss_done, h + 1)
                        nc.scalar.activation(rs_m[:], X0[:, 0:NQ], ACT.Sqrt, scale=1.0 / BLK, bias=EPS_C).then_inc(hm_root, 1)
                    if k == 15:
                        act.wait_ge(unit_done, h * 16 + U_M + k + 1 + RING)
                        for m in range(2):
                            last = nc.scalar.activation(z1[:, bass.ds(h * 2 + m, 1), :], ps_g[:, 2 + m:3 + m, 0:NQ], ACT.Tanh, scale=0.5,
                                                        bias=half_bias[:, bass.ds(h * 2 + B_GA + m, 1)])
                        last.then_inc(bank_free[1], 1)

            for k in range(8):
                split(0, U_KV, 8, k)
                if k == 0:
                    act.wait_ge(ya_ready, M_HEADS + START)
                    with nc.allow_non_contiguous_dma(reason="sinks, once"):
                        for par in range(2):
                            act.dma_start(sink_col[64 * par:64 * par + 64, :],
                                          sinks[0].rearrange("(j a) -> a j", a=2)[par].partition_broadcast(64)).then_inc(sinks_in, 16)
                        for tok in range(2):
                            act.dma_start(sink_meta[4 * tok:4 * tok + 4, :, :],
                                          sinks[0].rearrange("(g j a) -> j g a", j=4, a=2)).then_inc(sinks_in, 16)
                if k == 5:
                    act.wait_ge(av_turned, 1)
                    for t in range(2):
                        ps = ps_x[t][:, :].rearrange("p (w g d) -> p g w d", w=4, g=2)
                        for g in range(2):
                            nc.scalar.copy(v_win[:, 2 * t + g, :, :], ps[:, g, :, :]).then_inc(v_win_ready, 1)

            def softmax(g, e):
                n = g * STEPS + e + 1
                act.wait_ge(att_nm, n)
                if e < 8:
                    for c in range(2):
                        w = N_META + window(chunks_of(e)[c])[1]
                        nc.scalar.activation(probs_a[:, e % 2, c, 0:w], ps_x[e % 2][:, 144 * c:144 * c + w], ACT.Exp,
                                             bias=att[:, 2 + c:3 + c], accum_out=att[:, 4 + c:5 + c])
                    nc.scalar.activation(att[:, 6:8], att[:, 2:4], ACT.Exp,
                                         bias=sink_col[:, bass.ds(g * 4 + e // 2, 1)]).then_inc(att_exp, 1)
                else:
                    for c in range(2):
                        nc.scalar.activation(probs0[:, c, :], ps_x[0][0:8, 16 * c:16 * c + 16], ACT.Exp,
                                             bias=att0[:, 2 + c:3 + c], accum_out=att0[:, 4 + c:5 + c])
                    nc.scalar.activation(att0[:, 6:8], att0[:, 8:10], ACT.Exp).then_inc(att_exp, 1)

            def turn_out(g, e):
                act.wait_ge(att_turned, g * STEPS + e + 1)
                if e < 8:
                    nc.scalar.copy(prob_t[:], X2[:, 0:256].rearrange("p (c n) -> p c n", c=2))
                    c0 = 1 - e % 2
                    nc.scalar.copy(prob_tm[:, c0:2, :], X2[0:N_META, 256 + P * c0:512].rearrange("p (c n) -> p c n", c=2 - c0)).then_inc(att_prob_t, 1)
                else:
                    nc.scalar.copy(prob_t0[:], X2[0:N_META, 0:16]).then_inc(att_prob_t, 1)

            def mix_out(g, e):
                act.wait_ge(att_mixed, g * STEPS + e + 1 + START)
                if e < 8:
                    c0 = chunks_of(e)[0]
                    dst = yb_hi[:, bass.ds(g * 4 + e // 2, 1), 2 + CHUNK * (c0 - 1):2 + CHUNK * (c0 + 1)]
                    nc.scalar.copy(dst, X3[:, 0:P].rearrange("p (a n) -> p a n", a=1)).then_inc(att_yb_hi, 1)
                else:
                    src = X3[:, 256:264].rearrange("p (t j) -> p j t", t=2)
                    nc.scalar.copy(yb_hi[:, bass.ds(g * 4, 4), 0:2], src).then_inc(att_yb_hi, 1)

            with act.Fori(0, A_KV) as g:
                for k in range(16):
                    split(g, U_AW, 16, k)
                    if 7 <= k <= 15:
                        mix_out(g, k - 7)
                    if 6 <= k <= 14:
                        turn_out(g, k - 6)
                    if 4 <= k <= 12:
                        softmax(g, k - 4)

            with act.Fori(0, 4) as i:
                for k in range(16):
                    split(i, U_P2, 16, k)
                    if k in (3, 7):
                        par = k // 4
                        act.wait_ge(unit_done, i * 16 + U_P2 + k + 1 + RING)
                        act.wait_ge(zt_ready, i * 4 + START)
                        for m in range(2):
                            last = nc.scalar.activation(gate_b[:, 2 * par + m, :], ps_g[:, 2 * par + m, 0:NQ], ACT.Tanh, scale=0.5,
                                                        bias=half_bias[:, bass.ds(i * 4 + B_GB + 2 * par + m, 1)])
                        last.then_inc(gate_b_ready, 1)

            nc.scalar.activation(small[:, 46:47], EPS_C, ACT.Sqrt)
            with act.Fori(0, 4) as i:
                for k in range(8):
                    split(i, U_WO, 8, k)
                    if k in (3, 7):
                        par = k // 4
                        act.wait_ge(unit_done, i * 8 + U_WO + k + 1 + RING)
                        for m in range(2):
                            nc.scalar.activation(z1[:, bass.ds(i * 4 + 2 * par + m, 1), :],
                                                 ps_g[:, 2 * par + m:2 * par + m + 1, 0:NQ], ACT.Copy,
                                                 scale=half_gain[:, bass.ds(i * 4 + 2 * par + m, 1)])
                            if m == 0:
                                act.wait_ge(y_acc, i * 4 + 2 * par + 1)
                            sq = nc.scalar.activation(y_sq[:, m, :], ps_g[:, 2 * par + m, 0:NQ], ACT.Square, scale=0.5)
                            if m == 0:
                                sq.then_inc(y_sq_ready, 1)
                        sq.then_inc(y_sq_ready, 1)

            act.wait_ge(y_ss_done, 1)
            nc.scalar.activation(rs1[:], X0[:, 0:NQ], ACT.Sqrt, scale=1.0 / D, bias=EPS_C).then_inc(y_root, 1)
            nc.scalar.activation(small[:, 40:42], X0[:, 300:302], ACT.Sqrt, scale=1.0 / D, bias=EPS_C).then_inc(y_root, 1)
            for k in range(KT):
                if k % 2 == 0:
                    act.wait_ge(h_even_ready, k // 2 + 1)
                else:
                    act.wait_ge(h_odd_ready, k // 2 + 1)
                nc.scalar.activation(xn_hi[:, k, 0:NQ], xt[:, k, QO:T], ACT.Copy,
                                     scale=gains[:, G_PRE_FFN + k:G_PRE_FFN + k + 1]).then_inc(h_hi_ready, 1)
                if k >= 5 and k % 2 == 1 and k < 15:
                    n = (k - 5) // 2 + 3
                    tok, quarter = divmod(n, 4)
                    act.wait_ge(y_turned, n + 1)
                    nc.scalar.copy(y_tok_st[:, tok, quarter * 512:quarter * 512 + 512], ps_x[1 + n % 3][:, :]).then_inc(y_tok_ready[1], 1)
            act.wait_ge(h_a_ready, KT)
            act.wait_ge(y_turned, 8)
            for j in range(4):
                nc.scalar.activation(z1[:, 4 * j:4 * j + 4, :], xt[:, 4 * j:4 * j + 4, QO:T], ACT.Square).then_inc(h_sq_ready, 1)

            def up_taps(i, par):
                for m in range(2):
                    t = 2 * par + m
                    act.wait_ge(up_scaled, i * 4 + t + 1 + START)
                    tile = bass.ds(i * 2 + par * FT + m, 1)
                    nc.scalar.activation(c_t[:, t, :], u_t[:, t, 2:NQ], ACT.Identity,
                                         scale=conv_t[:, 2, tile], bias=conv_t[:, 3, tile]).then_inc(up_tap2, 1)

            def up_gelu(i):
                act.wait_ge(g_ready, i + START)
                for m in range(2):
                    act.wait_ge(up_tap0, i * 4 + m + 1)
                    nc.scalar.activation(ge_t[:, m, :], c_t[:, m, :], ACT.Gelu_apprx_tanh).then_inc(gelu_ready, 1)

            for k in range(8):
                split(0, U_UP, 8, k)
                if k == 5:
                    act.wait_ge(h_ss_done, 1)
                    nc.scalar.activation(rs2[:], X0[:, 0:NQ], ACT.Sqrt, scale=1.0 / D, bias=EPS_C).then_inc(h_root, 1)
                if k == 6:
                    up_taps(0, 0)
                if k == 7:
                    up_gelu(0)
                    up_taps(0, 1)
            with act.Fori(1, FT // 2) as i:
                for k in range(8):
                    split(i, U_UP, 8, k)
                    if k == 3:
                        act.wait_ge(g_f_ready, i + START)
                        up_taps(i, 0)
                    if k == 4:
                        up_gelu(i)
                    if k == 7:
                        up_taps(i, 1)

            nc.scalar.activation(small[:, 46:47], EPS_C, ACT.Sqrt)
            for b in range(DN_BLOCKS):
                for k in range(b * DN_U, (b + 1) * DN_U):
                    if k < DN_BLOCKS * DN_U - RING:
                        split(0, U_DN, 0, k)
                act.wait_ge(unit_done, U_DN + (b + 1) * DN_U + RING)
                if b:
                    act.wait_ge(dn_squared, 2 * b)
                for tok in range(2):
                    nc.scalar.activation(dn_junk[:, tok, :], ps_g[:, 2 * (b % 2) + tok, :], ACT.Square,
                                         accum_out=small[:, 24 + 4 * tok + b:25 + 4 * tok + b]).then_inc(dn_squared, 1)
            act.wait_ge(dn_ss_sum, 1)
            nc.scalar.activation(small[:, 34:36], small[:, 32:34], ACT.Sqrt, scale=1.0 / D, bias=EPS_C).then_inc(dn_root, 1)
            act.wait_ge(dn_rs, 1)
            act.wait_ge(dn_scaled, 8)
            for q in (2, 3):
                cols = slice(q * 512, q * 512 + 512)
                nc.scalar.activation(y_dn[:, 1, cols], y_dn[:, 1, cols], ACT.Copy, scale=small[:, 37:38]).then_inc(out_normed, 1)
            act.wait_ge(out_vector, 6)
            act.dma_start(out[0, P:SEQ, 0:1024], h_tok[:, 1, 0:1024]).then_inc(out_stored, 16)

        @block.vector
        def _(dve):
            nc.vector.sem_inc(lo_done, RING)
            def reciprocal_root(n, c, w):
                dve.wait_ge(root_ready, n)
                nc.vector.reciprocal(small[0:w, 20 + c:21 + c], small[0:w, 16 + c:17 + c]).then_inc(rs_ready, 1)

            def x_out(c, j):
                dve.wait_ge(x_turned, c * 4 + j + 1)
                nc.vector.tensor_copy(xt[:, 4 * j:4 * j + 4, c * P:(c + 1) * P],
                                      ps_g[:, j, :].rearrange("p (k n) -> p k n", k=4)).then_inc(xt_ready, 1)

            def norm(c, w, cols, ready):
                nc.vector.tensor_scalar(xn_tok[c][0:w, cols], xs[0:w, c, cols], small[0:w, 20 + c:21 + c], None, ALU.mult).then_inc(ready, 1)

            reciprocal_root(1, 2, N_META)
            dve.wait_ge(rs_ready, 1)
            norm(2, N_META, slice(0, D), xn_first)
            x_out(0, 0)
            x_out(0, 1)
            x_out(0, 2)
            x_out(0, 3)
            reciprocal_root(2, 0, P)
            dve.wait_ge(rs_ready, 2)
            norm(0, P, slice(0, D), xn_first)
            x_out(1, 0)
            reciprocal_root(3, 1, P)
            dve.wait_ge(rs_ready, 3)
            for q in (0, 2):
                norm(1, P, slice(q * 512, q * 512 + 512), xn_vector)
            x_out(1, 1)
            x_out(1, 2)
            x_out(1, 3)
            dve.wait_ge(x_turned, 9)
            nc.vector.tensor_copy(xt[:, :, 2 * P:T], X1[:, 0:KT * N_META].rearrange("p (k n) -> p k n", k=KT)).then_inc(xt_ready, 1)
            dve.wait_ge(gains_turned, 1)
            nc.vector.tensor_copy(gains[:], X0[:, 0:64]).then_inc(gains_ready, 1)
            dve.wait_ge(gains_ready, 1)
            nc.vector.tensor_scalar(half_gain[:], gains[:, G_POST_MIX:G_POST_MIX + KT], 0.5, None, ALU.mult).then_inc(half_ready, 1)
            dve.wait_ge(wg_hi_ready, 2)
            nc.vector.tensor_tensor(wg_lo[:, :, 0:8], wg[:, :, 0:8], wg_hi[:, :, 0:8].bitcast(F32), ALU.subtract).then_inc(wg_ready, 1)
            nc.vector.tensor_tensor(wg_lo[:, :, 32:40], wg[:, :, 8:16], wg_hi[:, :, 32:40].bitcast(F32), ALU.subtract).then_inc(wg_ready, 1)

            def lo(u, s):
                dve.wait_ge(hi_done, u + 1)
                nc.vector.tensor_tensor(w_lo[:, s, :], raw[:, s, :], w_hi[:, s, :].bitcast(F32), ALU.subtract).then_inc(lo_done, 1)

            def split(i, u0, per, k):
                lo(i * per + u0 + k + RING, k % RING)

            for k in range(KT):
                dve.wait_ge(xn_hi_ready, k + 1)
                nc.vector.scalar_tensor_tensor(xn_lo[:, k, :], ps_g[:, k % 4, 0:T], gains[:, G_PRE_MIX + k:G_PRE_MIX + k + 1],
                                               xn_hi[:, k, :].bitcast(F32), ALU.mult, ALU.subtract).then_inc(xn_lo_ready, 1)
                if k in (1, 3, 5, 7):
                    lo(k // 2, k // 2)
            dve.wait_ge(par_turned, 1)
            nc.vector.tensor_copy(bias_t[:], X0[:, 128:128 + B_ALL]).then_inc(par_ready, 1)
            nc.vector.tensor_copy(conv_t[:], X1[:, 0:8 * FT].rearrange("p (j m) -> p j m", j=4)).then_inc(par_ready, 1)
            dve.wait_ge(par_ready, 1)
            nc.vector.tensor_scalar(half_bias[:], bias_t[:], 0.5, None, ALU.mult).then_inc(half_ready, 1)
            dve.wait_ge(gates_done, 1)
            nc.vector.tensor_scalar(f_pre[:], X3[32:40, 0:T], small[32:40, 0:1], None, ALU.add).then_inc(f_ready, 1)
            dve.wait_ge(f_ready, 1)
            nc.vector.scalar_tensor_tensor(f_neg[:], f_pre[:], -1.0, f_pre[:], ALU.mult, ALU.min).then_inc(f_neg_ready, 1)
            nc.vector.tensor_scalar(i_pre[:], X3[0:8, 0:T], small[0:8, 0:1], None, ALU.add).then_inc(pre_ready, 1)
            dve.wait_ge(f_neg_ready, 1)
            nc.vector.tensor_scalar(f_pre[:], f_pre[:], 0.0, None, ALU.min).then_inc(pre_ready, 1)
            dve.wait_ge(soft_ready, 1)
            dve.wait_ge(pre_ready, 2)
            nc.vector.tensor_tensor_scan(b_cum[:], f_pre[:], f_soft[:], 0.0, ALU.add, ALU.subtract).then_inc(b_cum_ready, 1)
            dve.wait_ge(b_cum_ready, 1)
            nc.vector.tensor_tensor(u_row[:], i_pre[:], b_cum[:], ALU.subtract).then_inc(u_row_ready, 1)
            dve.wait_ge(u_row_ready, 1)
            nc.vector.tensor_tensor_scan(u_max[:], u_row[:], u_row[:], 0.0, ALU.max, ALU.max).then_inc(u_max_ready, 1)
            dve.wait_ge(u_max_ready, 1)
            nc.vector.tensor_tensor(m_row[:], b_cum[:], u_max[:], ALU.add).then_inc(m_row_ready, 1)
            dve.wait_ge(rows_zeroed, 2)
            nc.vector.tensor_scalar(neg_cut[0:8, :], u_max[:], -1.0, None, ALU.mult).then_inc(rows_cut, 1)
            dve.wait_ge(m_row_ready, 1)
            nc.vector.tensor_copy(m_cut[0:8, :], m_row[:]).then_inc(rows_cut, 1)
            dve.wait_ge(rows_cut, 2)
            nc.vector.scalar_tensor_tensor(neg_cut[32:40, :], u_max[:], -1.0, neg_cut[0:8, :].bitcast(F32), ALU.mult, ALU.subtract).then_inc(rows_ready, 1)
            nc.vector.tensor_tensor(m_cut[32:40, :], m_row[:], m_cut[0:8, :].bitcast(F32), ALU.subtract).then_inc(rows_ready, 1)

            with dve.Fori(0, M_HEADS) as h:
                for k in range(16):
                    if k not in (3, 7):
                        split(h, U_M, 16, k)
                    if k == 3:
                        dve.wait_ge(unit_done, h * 16 + U_M + k + 1 + RING)
                        nc.vector.tensor_scalar(q_t[:], ps_g[:, 0, 0:NQ], bias_t[:, bass.ds(h + B_Q, 1)], None, ALU.add)
                        nc.vector.tensor_scalar(k_t[:], ps_g[:, 1, 0:T], bias_t[:, bass.ds(h + B_K, 1)], float(P) ** -0.5,
                                                ALU.add, ALU.mult).then_inc(qk_ready, 1)
                        split(h, U_M, 16, k)
                    if k == 4:
                        dve.wait_ge(scores_done, h + 1 + START)
                        dve.wait_ge(const_ready, 5)
                        nc.vector.tensor_tensor(probs[:, 0:SP1], X1[:, 0:NQ], mask[:, QO:T], ALU.add)
                        nc.vector.tensor_tensor(probs[:, SP1:SP2], X1[:, P - QO:NQ], mask[:, 0:T - P], ALU.add)
                        nc.vector.tensor_tensor(probs[0:N_META, SP2:SP2 + 16], X1[0:N_META, 2 * P - QO:NQ], mask[0:N_META, 0:16],
                                                ALU.add).then_inc(expo_ready, 1)
                        dve.wait_ge(decay_ready, h * 3 + 3)
                        nc.vector.tensor_tensor(probs[:, 0:SP2], probs[:, 0:SP2], X0[:, 0:SP2], ALU.mult)
                        nc.vector.tensor_tensor(probs[0:N_META, SP2:SP2 + 16], probs[0:N_META, SP2:SP2 + 16],
                                                X0[0:N_META, SP2:SP2 + 16], ALU.mult).then_inc(probs_ready, 1)
                    if k == 7:
                        dve.wait_ge(unit_done, h * 16 + U_M + k + 1 + RING)
                        for c in range(2):
                            last = nc.vector.tensor_scalar(v_t[:, c, :], ps_g[:, 2 + c, 0:T], bias_t[:, bass.ds(h * 2 + B_V + c, 1)],
                                                           None, ALU.add)
                        last.then_inc(v_t_ready, 1)
                        split(h, U_M, 16, k)
                    if k == 11:
                        dve.wait_ge(heads_done, h + 1)
                        dve.wait_ge(em_ready, h + 1)
                        nc.vector.scalar_tensor_tensor(den_r[:], X3[:, 0:NQ], -1.0, em[:], ALU.mult, ALU.max).then_inc(den_ready, 1)
                        dve.wait_ge(den_ready, h * 2 + 1)
                        nc.vector.tensor_tensor(den_r[:], X3[:, 0:NQ], den_r[:], ALU.max).then_inc(den_ready, 1)
                        dve.wait_ge(den_ready, h * 2 + 2)
                        nc.vector.reciprocal(den_r[:], den_r[:]).then_inc(rden_ready, 1)
                        dve.wait_ge(rden_ready, h + 1)
                        for c, ps in ((0, X1), (1, X2)):
                            last = nc.vector.tensor_tensor(hm[:, c, :], ps[:, 0:NQ], den_r[:], ALU.mult)
                        last.then_inc(hm_ready, 1)
                    if k == 14:
                        dve.wait_ge(hm_root, h + 1 + START)
                        nc.vector.reciprocal(rs_m[:], rs_m[:]).then_inc(hm_rs, 1)
                        dve.wait_ge(hm_rs, h + 1)
                        for c in range(2):
                            last = nc.vector.scalar_tensor_tensor(hm_sq[:, c, :], hm[:, c, :], gains[:, bass.ds(h * 2 + G_MH + c, 1)],
                                                                  rs_m[:], ALU.mult, ALU.mult)
                        last.then_inc(normed_ready, 1)

            dve.wait_ge(ya_ready, M_HEADS + START)
            for k in range(8):
                split(0, U_KV, 8, k)
                if k == 3:
                    dve.wait_ge(unit_done, U_KV + k + 1 + RING)
                    for c in range(2):
                        last = nc.vector.tensor_scalar(av_t[:, c, :], ps_g[:, c, 0:T], bias_t[:, B_AV + c:B_AV + c + 1], None, ALU.add)
                    last.then_inc(av_t_ready, 1)
                if k == 7:
                    dve.wait_ge(unit_done, U_KV + k + 1 + RING)
                    for c in range(2):
                        for half_in in range(2):
                            for half_out in range(2):
                                pi, po = 64 * half_in, 64 * half_out
                                last = nc.vector.tensor_scalar(k_dup[po:po + 64, 2 * c + half_in, :], ps_g[pi:pi + 64, 2 + c, 0:T],
                                                               bias_t[pi:pi + 64, B_AK + c:B_AK + c + 1], float(DH) ** -0.5,
                                                               ALU.add, ALU.mult)
                    last.then_inc(k_dup_ready, 1)
            dve.wait_ge(sinks_in, 64)

            def softmax(g, e):
                n = g * STEPS + e + 1
                dve.wait_ge(att_scored, n)
                if e < 8:
                    ps = ps_x[e % 2]
                    for c in range(2):
                        w = N_META + window(chunks_of(e)[c])[1]
                        last = nc.vector.tensor_reduce(att[:, c:c + 1], ps[:, 144 * c:144 * c + w], AX_X, ALU.max)
                    last.then_inc(att_max, 1)
                    dve.wait_ge(att_max, n)
                    nc.vector.tensor_scalar(att[:, 2:4], att[:, 0:2], sink_col[:, bass.ds(g * 4 + e // 2, 1)], -1.0,
                                            ALU.max, ALU.mult).then_inc(att_nm, 1)
                    dve.wait_ge(att_exp, n)
                    nc.vector.tensor_tensor(att[:, 8:10], att[:, 4:6], att[:, 6:8], ALU.add).then_inc(att_den, 1)
                    dve.wait_ge(att_den, n)
                    nc.vector.reciprocal(att[:, 10:12], att[:, 8:10]).then_inc(att_rec, 1)
                    dve.wait_ge(att_rec, n)
                    for c in range(2):
                        w = N_META + window(chunks_of(e)[c])[1]
                        pr = probs_a[:, e % 2, c, 0:w]
                        last = nc.vector.tensor_scalar(pr, pr, att[:, 10 + c:11 + c], None, ALU.mult)
                    last.then_inc(att_probs, 1)
                else:
                    nc.vector.tensor_reduce(att0[:, 0:2], ps_x[0][0:8, 0:32].rearrange("p (a n) -> p a n", a=2), AX_X,
                                            ALU.max).then_inc(att_max, 1)
                    dve.wait_ge(att_max, n)
                    sk = sink_meta[:, bass.ds(g, 1), :].rearrange("p g a -> p (g a)")
                    nc.vector.tensor_tensor(att0[:, 10:12], att0[:, 0:2], sk, ALU.max).then_inc(att_maxed, 1)
                    dve.wait_ge(att_maxed, g * 2 + 1)
                    nc.vector.tensor_scalar(att0[:, 2:4], att0[:, 10:12], -1.0, None, ALU.mult).then_inc(att_maxed, 1)
                    dve.wait_ge(att_maxed, g * 2 + 2)
                    nc.vector.tensor_tensor(att0[:, 8:10], att0[:, 2:4], sk, ALU.add).then_inc(att_nm, 1)
                    dve.wait_ge(att_exp, n)
                    nc.vector.tensor_tensor(att0[:, 12:14], att0[:, 4:6], att0[:, 6:8], ALU.add).then_inc(att_den, 1)
                    dve.wait_ge(att_den, n)
                    nc.vector.reciprocal(att0[:, 14:16], att0[:, 12:14]).then_inc(att_rec, 1)
                    dve.wait_ge(att_rec, n)
                    for c in range(2):
                        last = nc.vector.tensor_scalar(probs0[:, c, :], probs0[:, c, :], att0[:, 14 + c:15 + c], None, ALU.mult)
                    last.then_inc(att_probs, 1)

            def mix_out(g, e):
                dve.wait_ge(att_yb_hi, g * STEPS + e + 1)
                if e < 8:
                    c0 = chunks_of(e)[0]
                    at = (slice(None), bass.ds(g * 4 + e // 2, 1), slice(2 + CHUNK * (c0 - 1), 2 + CHUNK * (c0 + 1)))
                    nc.vector.tensor_tensor(yb_lo[at], X3[:, 0:P].rearrange("p (a n) -> p a n", a=1), yb_hi[at].bitcast(F32),
                                            ALU.subtract).then_inc(att_yb, 1)
                else:
                    at = (slice(None), bass.ds(g * 4, 4), slice(0, 2))
                    nc.vector.tensor_tensor(yb_lo[at], X3[:, 256:264].rearrange("p (t j) -> p j t", t=2), yb_hi[at].bitcast(F32),
                                            ALU.subtract).then_inc(att_yb, 1)

            with dve.Fori(0, A_KV) as g:
                for k in range(16):
                    if k % 4 != 3:
                        split(g, U_AW, 16, k)
                    if k in (3, 7):
                        par = k // 4
                        dve.wait_ge(unit_done, g * 16 + U_AW + k + 1 + RING)
                        for m in range(2):
                            nc.vector.tensor_scalar(q_meta[:, :, 2 * par + m], ps_g[:, 2 * par + m, 0:2],
                                                    bias_t[:, bass.ds(g * 4 + B_AQ + 2 * par + m, 1)], None, ALU.add)
                            last = nc.vector.tensor_scalar(q_pairs[:, 2 * par + m, :], ps_g[:, 2 * par + m, 0:NQ],
                                                           bias_t[:, bass.ds(g * 4 + B_AQ + 2 * par + m, 1)], None, ALU.add)
                        last.then_inc(q_pairs_ready, 1)
                    if k in (11, 15):
                        par = k // 4 - 2
                        dve.wait_ge(unit_done, g * 16 + U_AW + k + 1 + RING)
                        for m in range(2):
                            zz = z1[:, bass.ds(g * 4 + 2 * par + m, 1), :]
                            last = nc.vector.scalar_tensor_tensor(zz, zz, 1.0, ps_g[:, 2 * par + m:2 * par + m + 1, 0:NQ],
                                                                  ALU.add, ALU.mult)
                        last.then_inc(wa_gated, 1)
                    if k % 4 == 3:
                        split(g, U_AW, 16, k)
                    if 7 <= k <= 15:
                        mix_out(g, k - 7)
                    if 4 <= k <= 12:
                        softmax(g, k - 4)

            dve.wait_ge(wa_gated, 8 + START)
            with dve.Fori(0, 4) as i:
                for k in range(16):
                    if k not in (11, 15):
                        split(i, U_P2, 16, k)
                    if k in (11, 15):
                        par = k // 4 - 2
                        dve.wait_ge(unit_done, i * 16 + U_P2 + k + 1 + RING)
                        dve.wait_ge(gate_b_ready, i * 2 + 2)
                        dve.wait_ge(z_ready, i * 4 + START)
                        for m in range(2):
                            t = 2 * par + m
                            last = nc.vector.scalar_tensor_tensor(zt[:, t, :], gate_b[:, t, :], 1.0, ps_g[:, t, 0:NQ],
                                                                  ALU.add, ALU.mult)
                            last.then_inc(zt_ready, 1)
                        split(i, U_P2, 16, k)

            with dve.Fori(0, 4) as i:
                for k in range(8):
                    split(i, U_WO, 8, k)

            for n in range(3):
                dve.wait_ge(y_turned, n + 1)
                nc.vector.tensor_copy(y_tok_st[:, 0, n * 512:n * 512 + 512], ps_x[1 + n % 3][:, :]).then_inc(y_tok_ready[0], 1)
            dve.wait_ge(y_root, 2)
            nc.vector.reciprocal(rs1[:], rs1[:]).then_inc(y_rs, 1)
            nc.vector.reciprocal(small[:, 42:44], small[:, 40:42]).then_inc(y_rs, 1)
            dve.wait_ge(y_rs, 1)

            def h_lo_tile(k):
                dve.wait_ge(h_hi_ready, k + 1)
                nc.vector.scalar_tensor_tensor(xn_lo[:, k, 0:NQ], xt[:, k, QO:T], gains[:, G_PRE_FFN + k:G_PRE_FFN + k + 1],
                                               xn_hi[:, k, 0:NQ].bitcast(F32), ALU.mult, ALU.subtract).then_inc(h_lo_ready, 1)

            for j in range(KT // 2):
                if j >= 2:
                    dve.wait_ge(h_even_ready, j - 1)
                    dve.wait_ge(h_odd_ready, j - 1)
                for k in (2 * j, 2 * j + 1):
                    nc.vector.tensor_tensor(h_a[:, k % 4, :], z1[:, k, :], rs1[:], ALU.mult).then_inc(h_a_ready, 1)
                dve.wait_ge(h_a_ready, 2 * j + 1)
                hk = xt[:, 2 * j, QO:T]
                nc.vector.tensor_tensor(hk, hk, h_a[:, (2 * j) % 4, :], ALU.add).then_inc(h_even_ready, 1)
                if j >= 1:
                    h_lo_tile(2 * j - 2)
                    h_lo_tile(2 * j - 1)
            h_lo_tile(KT - 2)
            h_lo_tile(KT - 1)

            def up_block(i, par, k):
                dve.wait_ge(unit_done, i * 8 + U_UP + k + 1 + RING)
                for m in range(2):
                    t = 2 * par + m
                    nc.vector.tensor_tensor(u_t[:, t, :], ps_g[:, t, 0:NQ], rs2[:], ALU.mult).then_inc(up_scaled, 1)
                for j in (1, 0):
                    for m in range(2):
                        t = 2 * par + m
                        dve.wait_ge(up_tap2 if j == 1 else up_tap1, i * 4 + t + 1)
                        nc.vector.scalar_tensor_tensor(c_t[:, t, :], u_t[:, t, j:j + SEQ],
                                                       conv_t[:, j, bass.ds(i * 2 + par * FT + m, 1)], c_t[:, t, :],
                                                       ALU.mult, ALU.add).then_inc(up_tap1 if j == 1 else up_tap0, 1)

            for k in range(8):
                split(0, U_UP, 8, k)
                if k == 5:
                    dve.wait_ge(h_root, 1)
                    nc.vector.reciprocal(rs2[:], rs2[:]).then_inc(h_rs, 1)
                    dve.wait_ge(h_rs, 1)
                if k == 6:
                    up_block(0, 0, k)
                if k == 7:
                    up_block(0, 1, k)
            with dve.Fori(1, FT // 2) as i:
                for k in range(8):
                    split(i, U_UP, 8, k)
                    if k in (3, 7):
                        up_block(i, k // 4, k)

            for b in range(DN_BLOCKS):
                for k in range(b * DN_U, (b + 1) * DN_U):
                    if k < DN_BLOCKS * DN_U - RING:
                        split(0, U_DN, 0, k)
                    if b == 1 and k % 2 == 0 and k // 2 - DN_U // 2 < 8:
                        tok, quarter = divmod(k // 2 - DN_U // 2, 4)
                        cols = slice(quarter * 512, quarter * 512 + 512)
                        dve.wait_ge(y_loaded, 16)
                        dve.wait_ge(x_tok_in, 16)
                        dve.wait_ge(y_rs, 2)
                        nc.vector.scalar_tensor_tensor(h_tok[:, tok, cols], h_tok[:, tok, cols], small[:, 42 + tok:43 + tok],
                                                       x_tok[:, tok, cols], ALU.mult, ALU.add).then_inc(h_tok_ready, 1)
                dve.wait_ge(unit_done, U_DN + (b + 1) * DN_U + RING)
                dve.wait_ge(gain_b_in, 16)
                cols = slice(512 * b, 512 * b + 512)
                for tok in range(2):
                    dve.wait_ge(dn_squared, 2 * b + tok + 1)
                    if b == DN_BLOCKS - 1 and tok == 1:
                        nc.vector.tensor_reduce(small[:, 32:34], small[:, 24:32].rearrange("p (t b) -> p t b", t=2), AX_X,
                                                ALU.add).then_inc(dn_ss_sum, 1)
                    nc.vector.tensor_tensor(y_dn[:, tok, cols], ps_g[:, 2 * (b % 2) + tok, :], gain_b[:, cols], ALU.mult).then_inc(dn_scaled, 1)
            dve.wait_ge(dn_root, 1)
            nc.vector.reciprocal(small[:, 36:38], small[:, 34:36]).then_inc(dn_rs, 1)
            dve.wait_ge(dn_rs, 1)
            dve.wait_ge(dn_scaled, 2 * DN_BLOCKS)
            dve.wait_ge(h_tok_ready, 8)
            for tok, quarter in ((0, 0), (0, 1), (0, 2), (0, 3), (1, 0), (1, 1)):
                cols = slice(quarter * 512, quarter * 512 + 512)
                nc.vector.scalar_tensor_tensor(h_tok[:, tok, cols], y_dn[:, tok, cols], small[:, 36 + tok:37 + tok], h_tok[:, tok, cols],
                                               ALU.mult, ALU.add).then_inc(out_vector, 1)

        @block.tensor
        def _(pe):
            nc.tensor.sem_inc(unit_done, RING)
            pe.wait_ge(const_ready, 3)
            for c in range(2):
                pe.wait_ge(x_in[c], 32 if c == 0 else 16)
                for j in range(4):
                    if c:
                        pe.wait_ge(xt_ready, j + 1)
                    for k in range(4):
                        last = nc.tensor.transpose(ps_g[:, j, k * P:(k + 1) * P], xs[:, c, (4 * j + k) * P:(4 * j + k + 1) * P], ident[:, :])
                    last.then_inc(x_turned, 1)
            pe.wait_ge(x_in[2], 16)
            for k in range(KT):
                last = nc.tensor.transpose(X1[:, k * N_META:(k + 1) * N_META], xs[0:N_META, 2, k * P:(k + 1) * P], ident[0:N_META, 0:N_META])
            last.then_inc(x_turned, 1)

            pe.wait_ge(gain_in, 4 * 16)
            nc.tensor.transpose(X0[:, 0:64], gain_rows[:, :], ident[0:64, 0:64]).then_inc(gains_turned, 1)

            def gates_tile(k):
                pe.wait_ge(xn_lo_ready, k + 1)
                for a, b in ((wg_hi, xn_hi), (wg_hi, xn_lo), (wg_lo, xn_hi)):
                    last = nc.tensor.matmul(X3[0:GC, 0:T], a[:, k, :], b[:, k, :], start=(k == 0 and a is wg_hi and b is xn_hi),
                                            stop=(k == KT - 1 and a is wg_lo))
                if k == KT - 1:
                    last.then_inc(gates_done, 1)

            pe.wait_ge(xn_first, 2)
            for k in range(KT):
                if k % 4 == 0:
                    if k % 8 == 0:
                        pe.wait_ge(xn_vector, k // 8 + 1)
                    else:
                        pe.wait_ge(xn_scalar, k // 8 + 1)
                if k < 4:
                    pe.wait_ge(xt_ready, 4 + k + 1)
                else:
                    pe.wait_ge(xn_lo_ready, k - 3)
                for c, w in CHUNKS:
                    last = nc.tensor.transpose(ps_g[:, k % 4, c * P:c * P + w], xn_tok[c][0:w, k * P:(k + 1) * P], ident[0:w, 0:w])
                last.then_inc(xn_turned, 1)
                if k == 1:
                    pe.wait_ge(wg_ready, 2)
                if k >= 2:
                    gates_tile(k - 2)
            pe.wait_ge(bias_in, 4 * 16)
            pe.wait_ge(conv_in, 2 * 16)
            pe.wait_ge(gains_ready, 1)
            pe.wait_ge(xt_ready, 9)
            nc.tensor.transpose(X0[:, 128:128 + B_ALL], bias_rows[:, :], ident[0:B_ALL, 0:B_ALL])
            for j in range(4):
                last = nc.tensor.transpose(X1[:, j * 2 * FT:(j + 1) * 2 * FT], conv_rows[:, j, :], ident[0:2 * FT, 0:2 * FT])
            last.then_inc(par_turned, 1)
            gates_tile(KT - 2)
            gates_tile(KT - 1)

            def unit(u, q, par, acts, t0=(0, 0), n=(NQ, NQ)):
                pe.wait_ge(lo_done, u + 1 + RING)
                wh = w_hi[:, q, :].rearrange("p (t n) -> p t n", t=UK)
                wl = w_lo[:, q, :].rearrange("p (t n) -> p t n", t=UK)
                for m in range(2):
                    dst = ps_g[:, 2 * par + m, 0:n[m]]
                    for t in range(UK):
                        k = q * UK + t
                        cols = slice(m * P, (m + 1) * P)
                        mh, ml = (a[:, k, t0[m]:t0[m] + n[m]] for a in acts)
                        nc.tensor.matmul(dst, wh[:, t, cols], mh, start=(k == 0), stop=False)
                        nc.tensor.matmul(dst, wh[:, t, cols], ml, start=False, stop=False)
                        last = nc.tensor.matmul(dst, wl[:, t, cols], mh, start=False, stop=(k == KT - 1))
                last.then_inc(unit_done, 1)

            xn, ya, yb, zz = (xn_hi, xn_lo), (ya_hi, ya_lo), (yb_hi, yb_lo), (z_hi, z_lo)
            Q_TOK = dict(t0=(QO, QO), n=(NQ, NQ))
            ALL_TOK = dict(t0=(0, 0), n=(T, T))

            def free(i, per, q0, b):
                pe.wait_ge(bank_free[b % 2], i * (per // 2) + (q0 + b) // 2)

            with pe.Fori(0, M_HEADS) as h:
                for k in range(16):
                    b, q = divmod(k, 4)
                    if q == 0:
                        if b == 0:
                            pe.wait_ge(tanh_o_ready, h + START)
                        elif b == 1:
                            pe.wait_ge(bank_free[1], h + START)
                        elif b == 2:
                            pe.wait_ge(qk_ready, h + 1)
                        else:
                            pe.wait_ge(v_t_ready, h + 1)
                    toks = (dict(t0=(QO, 0), n=(NQ, T)), ALL_TOK, Q_TOK, Q_TOK)[b]
                    unit(h * 16 + U_M + k, q, b % 2, xn, **toks)
                    if k == 4:
                        pe.wait_ge(qk_ready, h + 1)
                        pe.wait_ge(sel_ready, h + 1)
                        pe.wait_ge(rows_ready, 2)
                        pe.wait_ge(hm_root, h + START)
                        pe.wait_ge(par_ready, 2)
                        nc.tensor.matmul(X0[:, 0:SP1], k_t[:, 0:P], q_t[:, :], start=True, stop=True)
                        nc.tensor.matmul(X0[:, SP1:SP2], k_t[:, P:2 * P], q_t[:, P - QO:NQ], start=True, stop=True)
                        nc.tensor.matmul(X0[0:N_META, SP2:SP2 + 16], k_t[:, 2 * P:T], q_t[:, 2 * P - QO:NQ], start=True, stop=True)
                        nc.tensor.matmul(X1[:, 0:NQ], sel[:, :], neg_cut[:, QO:T], start=True, stop=True)
                        nc.tensor.matmul(X2[:, 0:NQ], sel[:, :], m_cut[:, QO:T], start=True, stop=True).then_inc(scores_done, 1)
                    if k == 8:
                        pe.wait_ge(v_t_ready, h + 1)
                        pe.wait_ge(em_ready, h + 1)
                        for c in range(2):
                            for st in range(2):
                                nc.tensor.transpose(X3[:, st * BLK + c * P:st * BLK + (c + 1) * P], v_t[:, c, st * P:(st + 1) * P], ident[:, :])
                            last = nc.tensor.transpose(X2[0:N_META, c * P:(c + 1) * P], v_t[:, c, 2 * P:T], ident[:, :])
                        last.then_inc(v_turned, 1)
                    if k == 11:
                        pe.wait_ge(v_tok_ready, h * 2 + 2)
                        pe.wait_ge(probs_ready, h + 1)
                        for c, dst in ((0, X1), (1, X2), (2, X3)):
                            w0 = v_tok[:, 0, c * P:(c + 1) * P] if c < 2 else ones[:, :]
                            w1 = v_tok[:, 1, c * P:(c + 1) * P] if c < 2 else ones[:, :]
                            w2 = v_tok2[:, c * P:(c + 1) * P] if c < 2 else ones[0:N_META, :]
                            nc.tensor.matmul(dst[:, 0:NQ], w0, probs[:, 0:SP1], start=True, stop=False)
                            nc.tensor.matmul(dst[:, P - QO:NQ], w1, probs[:, SP1:SP2], start=False, stop=False)
                            last = nc.tensor.matmul(dst[:, 2 * P - QO:NQ], w2, probs[0:N_META, SP2:SP2 + 16], start=False, stop=True)
                        last.then_inc(heads_done, 1)
                    if k == 14:
                        pe.wait_ge(hm_ss_ready, h + 1)
                        nc.tensor.matmul(X0[:, 0:NQ], ones[:, :], hm_ss[:], start=True, stop=True).then_inc(hm_ss_done, 1)

            for k in range(8):
                b, q = divmod(k, 4)
                if q == 0:
                    pe.wait_ge((tanh_o_ready, bank_free[1])[b], M_HEADS + START)
                unit(U_KV + k, q, b, xn, **ALL_TOK)
                if k == 5:
                    pe.wait_ge(av_t_ready, 1)
                    pe.wait_ge(hm_root, M_HEADS + START)
                    for t in range(2):
                        for n, w0 in enumerate((0, *(window(c)[0] for c in (2, 3, 4)))):
                            last = nc.tensor.transpose(ps_x[t][:, n * P:(n + 1) * P], av_t[:, t, w0:w0 + P], ident[:, :])
                    last.then_inc(av_turned, 1)

            def hold():
                nc.tensor.sem_inc(pe_held, 1)

            def scores(g, e):
                pe.wait_ge(q_pairs_ready, g * 2 + (1 if e < 4 else 2))
                pe.wait_ge(v_group_ready, g * 2 + 1)
                hold()
                ps = ps_x[e % 2]
                for par in range(2):
                    rows = slice(64 * par, 64 * par + 64)
                    if e < 8:
                        for c in range(2):
                            ch = chunks_of(e)[c]
                            w0, w = window(ch)
                            qs = q_pairs[rows, e // 2, 2 + CHUNK * (ch - 1):2 + CHUNK * ch]
                            if w0 == N_META:
                                last = nc.tensor.matmul(ps[rows, 144 * c:144 * c + N_META + w], qs,
                                                        k_group[rows, 0:N_META + w], start=True, stop=True)
                            else:
                                nc.tensor.matmul(ps[rows, 144 * c:144 * c + N_META], qs,
                                                 k_group[rows, 0:N_META], start=True, stop=True)
                                last = nc.tensor.matmul(ps[rows, 144 * c + N_META:144 * c + N_META + w], qs,
                                                        k_group[rows, w0:w0 + w], start=True, stop=True)
                    else:
                        if par:
                            last.then_inc(meta_scored, 1)
                            pe.wait_ge(meta_scored, g + 1)
                            hold()
                        last = nc.tensor.matmul(ps[0:8, 16 * par:16 * par + 16], q_meta[rows, :, :].rearrange("p t j -> p (t j)"),
                                                k_group[rows, 0:N_META], start=True, stop=True)
                last.then_inc(att_scored, 1)

            def turn(g, e):
                pe.wait_ge(att_probs, g * STEPS + e + 1)
                if e == 0:
                    pe.wait_ge(att_prob_t, g * STEPS + START)
                hold()
                if e < 8:
                    for c in range(2):
                        w = window(chunks_of(e)[c])[1]
                        if w < P:
                            last = nc.tensor.transpose(X2[0:N_META + w, c * P:(c + 1) * P], probs_a[:, e % 2, c, 0:N_META + w], ident[:, :])
                            continue
                        nc.tensor.transpose(X2[0:w, c * P:(c + 1) * P], probs_a[:, e % 2, c, N_META:N_META + w], ident[:, :])
                        last = nc.tensor.transpose(X2[0:N_META, 256 + c * P:256 + (c + 1) * P], probs_a[:, e % 2, c, 0:N_META], ident[:, :])
                else:
                    for c in range(2):
                        last = nc.tensor.transpose(X2[0:N_META, 8 * c:8 * c + 8], probs0[:, c, :], ident[0:8, 0:8])
                last.then_inc(att_turned, 1)

            def mix(g, e):
                pe.wait_ge(att_prob_t, g * STEPS + e + 1 + START)
                pe.wait_ge(att_yb, g * STEPS + e + START)
                pe.wait_ge(v_group_ready, g * 2 + 2)
                hold()
                for par in range(2):
                    rows = slice(64 * par, 64 * par + 64)
                    if e < 8:
                        for c in range(2):
                            ch = chunks_of(e)[c]
                            w = window(ch)[1]
                            slot = ch - 1
                            dst = X3[rows, CHUNK * c:CHUNK * (c + 1)]
                            if w < P:
                                nc.tensor.matmul(dst, v_group[0:N_META + w, 0, :], prob_t[0:N_META + w, c, rows], start=True, stop=True)
                                continue
                            nc.tensor.matmul(dst, v_group[0:N_META, 0, :], prob_tm[:, c, rows], start=True, stop=False)
                            last = nc.tensor.matmul(dst, v_group[0:w, slot, :], prob_t[0:w, c, rows], start=False, stop=True)
                    else:
                        last = nc.tensor.matmul(X3[rows, 256:264], v_group[0:N_META, 0, :], prob_t0[:, 8 * par:8 * par + 8],
                                                start=True, stop=True)
                last.then_inc(att_mixed, 1)

            pe.wait_ge(av_t_ready, 1)
            with pe.Fori(0, A_KV) as g:
                for k in range(16):
                    b, q = divmod(k, 4)
                    if q == 0:
                        if b < 2:
                            pe.wait_ge(wa_gated, g * 2 - 1 + b + START)
                            if b == 1:
                                pe.wait_ge(k_dup_ready, 1)
                                pe.wait_ge(v_win_ready, 4)
                        else:
                            pe.wait_ge(q_pairs_ready, g * 2 + b - 1)
                    unit(g * 16 + U_AW + k, q, b % 2, xn if b < 2 else ya, **(Q_TOK if b < 2 else {}))
                    if 7 <= k <= 15:
                        mix(g, k - 7)
                    if 6 <= k <= 14:
                        turn(g, k - 6)
                    if 4 <= k <= 12:
                        scores(g, k - 4)

            with pe.Fori(0, 4) as i:
                for k in range(16):
                    b, q = divmod(k, 4)
                    if q == 0:
                        if b < 2:
                            pe.wait_ge(wa_gated, 7 + b + START)
                            pe.wait_ge(zt_ready, i * 4 - 2 + 2 * b + START)
                        else:
                            pe.wait_ge(gate_b_ready, i * 2 + b - 1)
                            pe.wait_ge(att_yb, A_KV * STEPS + START)
                    unit(i * 16 + U_P2 + k, q, b % 2, xn if b < 2 else yb, **(Q_TOK if b < 2 else {}))

            pe.wait_ge(zt_ready, 14 + START)
            with pe.Fori(0, 4) as i:
                for k in range(8):
                    b, q = divmod(k, 4)
                    if b == 0:
                        pe.wait_ge(z_ready, UK * (q + 1) + START)
                    if q == 0:
                        pe.wait_ge(y_sq_ready, i * 4 - 2 + 2 * b + START)
                    unit(i * 8 + U_WO + k, q, b, zz)

            def turn_y(n):
                tok, quarter = divmod(n, 4)
                if n >= 6:
                    pe.wait_ge(y_tok_ready[1], n - 5)
                elif n >= 3:
                    pe.wait_ge(y_tok_ready[0], n - 2)
                for j in range(4):
                    k = 4 * quarter + j
                    last = nc.tensor.transpose(ps_x[1 + n % 3][:, j * P:(j + 1) * P], z1[:, k, 2 + tok * P:2 + (tok + 1) * P], ident[:, :])
                last.then_inc(y_turned, 1)

            pe.wait_ge(y_sq_ready, KT - 4 + START)
            for n in range(3):
                turn_y(n)
            pe.wait_ge(y_acc, 17)
            nc.tensor.matmul(X0[:, 0:NQ], ones[:, :], ss_acc[:], start=True, stop=True)
            for tok in range(2):
                last = nc.tensor.matmul(X0[:, 300 + tok:301 + tok], ss_acc[:, 2 + tok * P:2 + (tok + 1) * P], ones[:, 0:1], start=True, stop=True)
            last.then_inc(y_ss_done, 1)
            for n in range(3, 6):
                turn_y(n)

            pe.wait_ge(y_sq_ready, KT + START)
            for k in range(8):
                if k < 4:
                    pe.wait_ge(h_lo_ready, UK * (k + 1))
                unit(U_UP + k, k % 4, k // 4, xn)
                if k in (0, 1):
                    turn_y(6 + k)
                if k == 5:
                    pe.wait_ge(h_sum, 5)
                    pe.wait_ge(y_root, 2)
                    nc.tensor.matmul(X0[:, 0:NQ], ones[:, :], z1[:, 0, :], start=True, stop=True).then_inc(h_ss_done, 1)
            with pe.Fori(1, FT // 2) as i:
                for k in range(8):
                    b, q = divmod(k, 4)
                    if q == 0:
                        pe.wait_ge(up_scaled, i * 4 - 2 + 2 * b + START)
                    unit(i * 8 + U_UP + k, q, b, xn)

            for b in range(DN_BLOCKS):
                if b < 2:
                    pe.wait_ge(up_scaled, 2 * FT - 2 + 2 * b + START)
                else:
                    pe.wait_ge(dn_squared, 2 * b - 2)
                    pe.wait_ge(dn_scaled, 2 * b - 2)
                for q in range(DN_U):
                    k = b * DN_U + q
                    if b == 0:
                        pe.wait_ge(g_ready, q + 1 + START)
                    pe.wait_ge(lo_done, U_DN + k + 1 + RING)
                    for tok in range(2):
                        dst = ps_g[:, 2 * (b % 2) + tok, :]
                        for t in range(DN_K):
                            f = q * DN_K + t
                            cols = slice(t * 512, (t + 1) * 512)
                            gh, gl = (a[:, f, tok * P:(tok + 1) * P] for a in (g_hi, g_lo))
                            nc.tensor.matmul(dst, gh, w_hi[:, k % RING, cols], start=(f == 0), stop=False)
                            nc.tensor.matmul(dst, gl, w_hi[:, k % RING, cols], start=False, stop=False)
                            last = nc.tensor.matmul(dst, gh, w_lo[:, k % RING, cols], start=False, stop=(f == FT - 1))
                    last.then_inc(unit_done, 1)


_INS = ['x', 'meta', 'w_in', 'b_in', 'mh_norm', 'sinks', 'w_a', 'w_b', 'w_out', 'g_pre_mix', 'g_post_mix',
        'g_pre_ffn', 'g_post_ffn', 'w_up', 'conv_w', 'conv_b', 'w_down']
_OUTS = [((1, SEQ, D), 'float32')]


def kernel(**inputs):
    import numpy as _np
    import concourse.bacc as _bacc
    from concourse import mybir as _mybir
    from concourse.bass_utils import run_bass_kernel_spmd as _run

    nc = _bacc.Bacc("TRN2", target_bir_lowering=False, num_devices=1)
    arrays, args = {}, []
    for name in _INS:
        a = _np.ascontiguousarray(inputs[name])
        arrays[f"in_{name}_dram"] = a
        args.append(nc.dram_tensor(f"in_{name}_dram", a.shape, _mybir.dt.from_np(a.dtype), kind="ExternalInput").ap())
    for i, (shape, dtype) in enumerate(_OUTS):
        dt = _mybir.dt.from_np(_np.dtype(dtype))
        args.append(nc.dram_tensor(f"out_{i}_dram", shape, dt, kind="ExternalOutput").ap())
    layer(nc, *args)
    r = _run(nc, [arrays], core_ids=[0])
    return r.results[0]["out_0_dram"]
```

```python
from contextlib import ExitStack

import concourse.bass as bass
from concourse import mybir

F32 = mybir.dt.float32
F32R = mybir.dt.float32r
ACT = mybir.ActivationFunctionType
ALU = mybir.AluOpType
AX_X = mybir.AxisListType.X

P = 128
D = 2048
KT = D // P
N_META = 16
SEQ = 256
T = N_META + SEQ
CONV_W = 3
QO = N_META - (CONV_W - 1)
NQ = T - QO
CHUNK = 64
M_HEADS = 8
A_HEADS, A_KV, DH = 32, 4, 64
D_FF = 256 * ((8 * D // 3 + 255) // 256)
FT = D_FF // P
EPS = 1e-6
NEG = -1e30

C_Q, C_K, C_V = 0, 1024, 2048
C_GATE = 4096
C_MO = C_GATE + 2 * M_HEADS
C_AQ = C_MO + D
C_AK = C_AQ + D
C_AV = C_AK + A_KV * DH
C_GA = C_AV + A_KV * DH
C_GB = C_GA + D
B_Q, B_K, B_V, B_MO, B_AQ, B_AK, B_AV, B_GA, B_GB, B_ALL = 0, 8, 16, 32, 48, 64, 66, 68, 84, 100
G_PRE_MIX, G_POST_MIX, G_PRE_FFN, G_MH = 0, 16, 32, 48

RING = 4
START = 3
UK = 4
BLK = 256
U_M, U_KV, U_AW, U_P2, U_WO, U_UP, U_DN = 0, 128, 136, 200, 264, 296, 472
Q_M, Q_KV, Q_AW, Q_P2, Q_WO, Q_UP, Q_DN = 0, 32, 34, 50, 66, 74, 118
DN_K = 2
DN_U = FT // DN_K
DN_BLOCKS = D // 512
OUT_VECTOR = [(0, 0), (0, 1), (0, 2), (0, 3), (1, 0), (1, 1)]
OUT_POOL = [(1, 2), (1, 3)]
OUT_ORDER = [("vector", 0, 0), ("vector", 0, 1), ("vector", 0, 2), ("vector", 0, 3), ("vector", 1, 0), ("vector", 1, 1),
             ("pool", 1, 2), ("pool", 1, 3)]
H_VECTOR = (0, 2)
H_POOL = tuple(k for k in range(KT) if k not in H_VECTOR)
POOL_STEPS = (7, 11)
STEPS = 9


def layer(nc, x, meta, w_in, b_in, mh_norm, sinks, w_a, w_b, w_out, g_pre_mix, g_post_mix,
          g_pre_ffn, g_post_ffn, w_up, conv_w, conv_b, w_down, out):
    with ExitStack() as ctx:
        base = [16512]

        def put(name, shape, dt=F32, at=None):
            size = 4
            for n in shape[1:]:
                size *= n
            size = (size + 31) // 32 * 32
            if at is None:
                at = base[0]
                base[0] += size
            assert at + size <= 229344, name
            return nc.alloc_sbuf_tensor_at(name, list(shape), dt, offset=at)

        def sem(name):
            return ctx.enter_context(nc.semaphore(name))

        raw = put("raw", [P, RING, 1024])
        w_hi = put("w_hi", [P, RING, 1024], F32R)
        w_lo = put("w_lo", [P, RING, 1024], F32R)
        xn_at = base[0]
        xn_hi = put("xn_hi", [P, KT, T], F32R)
        xn_lo = put("xn_lo", [P, KT, T], F32R)
        xt_at = base[0]
        xt = put("xt", [P, KT, T])
        big_at = base[0]
        base[0] += 2 * FT * SEQ * 4
        g_hi = put("g_hi", [P, FT, SEQ], F32R, big_at)
        g_lo = put("g_lo", [P, FT, SEQ], F32R, big_at + FT * SEQ * 4)
        half = KT * NQ * 4
        ya_hi = put("ya_hi", [P, KT, NQ], F32R, big_at)
        ya_lo = put("ya_lo", [P, KT, NQ], F32R, big_at + half)
        yb_hi = put("yb_hi", [P, KT, NQ], F32R, big_at + 2 * half)
        yb_lo = put("yb_lo", [P, KT, NQ], F32R, big_at + 3 * half)
        z1 = put("z1", [P, KT, NQ], F32, big_at + 4 * half)
        z_hi, z_lo = ya_hi, ya_lo
        spare_at = big_at + 5 * half
        ident = put("ident", [P, P])
        ones = put("ones", [P, P])
        bias_t = put("bias_t", [P, B_ALL])
        half_bias = put("half_bias", [P, B_ALL])
        gains = put("gains", [P, 64])
        half_gain = put("half_gain", [P, KT])
        conv_t = put("conv_t", [P, 4, 2 * FT])
        cst = put("cst", [P, 4])
        small = put("small", [P, 64])
        EPS_C, ONE_C = cst[:, 0:1], cst[:, 1:2]
        tmp_at = base[0]

        class Area:
            def __init__(self, at):
                self.at = at

            def put(self, name, shape, dt=F32):
                size = 4
                for n in shape[1:]:
                    size *= n
                size = (size + 31) // 32 * 32
                a = self.at
                self.at += size
                return put(name, shape, dt, a)

        CHUNKS = ((0, P), (1, P), (2, N_META))
        area = Area(big_at + 2 * half)
        xs = area.put("xs", [P, 3, D])
        area = Area(big_at)
        GC = 40
        wg = area.put("wg", [P, KT, 16])
        wg_hi = area.put("wg_hi", [P, KT, GC], F32R)
        wg_lo = area.put("wg_lo", [P, KT, GC], F32R)
        bias_rows = area.put("bias_rows", [B_ALL, P])
        gain_rows = area.put("gain_rows", [64, P])
        conv_rows = area.put("conv_rows", [2 * FT, 4, P])
        sq_junk = area.put("sq_junk", [P, D])
        m_row = area.put("m_row", [M_HEADS, T])
        area = Area(big_at + 4 * half)
        RC = 32 + M_HEADS
        xn_tok2 = area.put("xn_tok2", [N_META, D])
        i_pre = area.put("i_pre", [M_HEADS, T])
        f_pre = area.put("f_pre", [M_HEADS, T])
        f_neg = area.put("f_neg", [M_HEADS, T])
        f_soft = area.put("f_soft", [M_HEADS, T])
        b_cum = area.put("b_cum", [M_HEADS, T])
        u_row = area.put("u_row", [M_HEADS, T])
        u_max = area.put("u_max", [M_HEADS, T])
        assert area.at <= spare_at

        xn_tok = [put("xn_tok0", [P, D], F32, tmp_at), put("xn_tok1", [P, D], F32, tmp_at + D * 4), xn_tok2]

        area = Area(spare_at)
        mask = area.put("mask", [P, T])
        neg_cut = area.put("neg_cut", [RC, T], F32R)
        m_cut = area.put("m_cut", [RC, T], F32R)
        q_t = area.put("q_t", [P, NQ])
        k_t = area.put("k_t", [P, T])
        u_col = area.put("u_col", [P, 3, M_HEADS])
        sel = area.put("sel", [RC, P], F32R)
        picks = area.put("picks", [RC, M_HEADS])
        em = area.put("em", [P, NQ])
        assert area.at <= big_at + 2 * FT * SEQ * 4
        area = Area(tmp_at)
        SP1, SP2 = NQ, NQ + T - P
        probs = area.put("probs", [P, SP2 + 16])
        v_t = area.put("v_t", [P, 2, T])
        v_tok = area.put("v_tok", [P, 2, BLK])
        v_tok2 = area.put("v_tok2", [16, BLK])
        den_r = area.put("den_r", [P, NQ])
        hm = area.put("hm", [P, 2, NQ])
        hm_sq = area.put("hm_sq", [P, 2, NQ])
        sig_o = area.put("sig_o", [P, 2, NQ])
        rs_m = area.put("rs_m", [P, NQ])
        hm_ss = area.put("hm_ss", [P, NQ])

        area = Area(spare_at)
        q_pairs = area.put("q_pairs", [P, 4, NQ])
        v_group = area.put("v_group", [P, 4, DH])
        KW = N_META + P
        k_group = area.put("k_group", [P, 3 * KW])
        q_meta = area.put("q_meta", [P, 2, 4])
        prob_t0 = area.put("prob_t0", [N_META, 16])
        probs0 = area.put("probs0", [8, 2, N_META])
        sink_col = area.put("sink_col", [P, A_HEADS // 2])
        sink_meta = area.put("sink_meta", [8, A_KV, 2])
        att = area.put("att", [P, 16])
        att0 = area.put("att0", [8, 16])
        assert area.at <= big_at + 2 * FT * SEQ * 4
        area = Area(tmp_at)
        k_dup = area.put("k_dup", [P, A_KV, T])
        v_win = area.put("v_win", [P, A_KV, 4, DH])
        av_t = area.put("av_t", [P, 2, T])
        probs_a = area.put("probs_a", [P, 2, 2, 144])
        prob_t = area.put("prob_t", [P, 2, P])
        prob_tm = area.put("prob_tm", [N_META, 2, P])

        area = Area(tmp_at)
        gate_b = area.put("gate_b", [P, 4, NQ])
        zt = area.put("zt", [P, 4, NQ])
        area = Area(tmp_at)
        rs2 = area.put("rs2", [P, NQ])
        ffn_at = area.at
        y_sq = area.put("y_sq", [P, 2, NQ])
        ss_acc = area.put("ss_acc", [P, NQ])
        rs1 = area.put("rs1", [P, NQ])
        h_a = area.put("h_a", [P, 4, NQ])
        area = Area(ffn_at)
        u_t = area.put("u_t", [P, 4, NQ])
        c_t = area.put("c_t", [P, 4, SEQ])
        ge_t = area.put("ge_t", [P, 2, SEQ])
        y_tok_st = put("y_tok_st", [P, 2, D], F32, big_at)
        h_tok = put("h_tok", [P, 2, D], F32, xn_at)
        area = Area(xn_at + KT * T * 4)
        gain_b = area.put("gain_b", [P, D])
        dn_junk = area.put("dn_junk", [P, 2, 512])
        x_tok = put("x_tok", [P, 2, D], F32, tmp_at)
        y_dn = put("y_dn", [P, 2, D], F32, xt_at)
        u_scratch = nc.dram_tensor("u_scratch", [M_HEADS, T], F32).ap()
        y_scratch = nc.dram_tensor("y_scratch", [P, 2, D], F32).ap()

        ps_g = ctx.enter_context(nc.psum_tensor("ps_g", [P, 4, 512], F32))
        ps_x = [ctx.enter_context(nc.psum_tensor(f"ps_x{n}", [P, 512], F32)) for n in range(4)]
        X0, X1, X2, X3 = ps_x

        raw_full = [sem(f"raw_full{n}") for n in range(RING)]
        hi_done = sem("hi_done")
        lo_done = sem("lo_done")
        unit_done = sem("unit_done")
        tanh_a_ready = sem("tanh_a_ready")
        x_in = [sem(f"x_in{n}") for n in range(3)]
        wg_in, gain_in, bias_in, conv_in = sem("wg_in"), sem("gain_in"), sem("bias_in"), sem("conv_in")
        const_ready, zero_ready = sem("const_ready"), sem("zero_ready")
        gains_turned, par_turned = sem("gains_turned"), sem("par_turned")
        gains_ready, par_ready, half_ready = sem("gains_ready"), sem("par_ready"), sem("half_ready")
        sum_sq, root_ready, rs_ready = sem("sum_sq"), sem("root_ready"), sem("rs_ready")
        x_turned, xt_ready = sem("x_turned"), sem("xt_ready")
        xn_first, xn_scalar, xn_vector, xn_turned = sem("xn_first"), sem("xn_scalar"), sem("xn_vector"), sem("xn_turned")
        xn_hi_ready, xn_lo_ready = sem("xn_hi_ready"), sem("xn_lo_ready")
        wg_zeroed, wg_hi_ready, wg_ready = sem("wg_zeroed"), sem("wg_hi_ready"), sem("wg_ready")
        gates_done, pre_ready, f_neg_ready = sem("gates_done"), sem("pre_ready"), sem("f_neg_ready")
        exp_f_ready, soft_ready, f_ready = sem("exp_f_ready"), sem("soft_ready"), sem("f_ready")
        rows_ready, u_row_ready, u_col_in = sem("rows_ready"), sem("u_row_ready"), sem("u_col_in")
        pe_held, pool_held, sp_held = sem("pe_held"), sem("pool_held"), sem("sp_held")
        meta_scored = sem("meta_scored")
        rows_zeroed, picks_ready, m_row_ready, rows_cut = sem("rows_zeroed"), sem("picks_ready"), sem("m_row_ready"), sem("rows_cut")
        hm_ss_ready = sem("hm_ss_ready")
        u_stored, b_cum_ready, u_max_ready = sem("u_stored"), sem("b_cum_ready"), sem("u_max_ready")

        qk_ready, v_t_ready, sel_ready = sem("qk_ready"), sem("v_t_ready"), sem("sel_ready")
        scores_done, expo_ready, decay_ready = sem("scores_done"), sem("expo_ready"), sem("decay_ready")
        em_ready, probs_ready = sem("em_ready"), sem("probs_ready")
        v_turned, v_tok_ready = sem("v_turned"), sem("v_tok_ready")
        heads_done, den_ready, rden_ready, hm_ready = sem("heads_done"), sem("den_ready"), sem("rden_ready"), sem("hm_ready")
        hm_sq_ready, hm_ss_done, hm_root, hm_rs = sem("hm_sq_ready"), sem("hm_ss_done"), sem("hm_root"), sem("hm_rs")
        tanh_o_ready, sig_o_ready, normed_ready = sem("tanh_o_ready"), sem("sig_o_ready"), sem("normed_ready")
        ya_f_ready, ya_hi_ready, ya_ready = sem("ya_f_ready"), sem("ya_hi_ready"), sem("ya_ready")

        k_dup_ready, av_t_ready, av_turned, v_win_ready = sem("k_dup_ready"), sem("av_t_ready"), sem("av_turned"), sem("v_win_ready")
        sinks_in, q_meta_ready = sem("sinks_in"), sem("q_meta_ready")
        v_group_ready, q_pairs_ready = sem("v_group_ready"), sem("q_pairs_ready")
        att_scored, att_max, att_maxed, att_nm = sem("att_scored"), sem("att_max"), sem("att_maxed"), sem("att_nm")
        att_exp, att_den, att_rec, att_probs = sem("att_exp"), sem("att_den"), sem("att_rec"), sem("att_probs")
        att_turned, att_prob_t, att_mixed, att_yb_hi, att_yb = sem("att_turned"), sem("att_prob_t"), sem("att_mixed"), sem("att_yb_hi"), sem("att_yb")
        wa_gated = sem("wa_gated")

        gate_b_ready, zt_ready, z_f_ready, z_hi_ready, z_ready = sem("gate_b_ready"), sem("zt_ready"), sem("z_f_ready"), sem("z_hi_ready"), sem("z_ready")
        y_sq_ready, y_out, y_acc, y_ss_done, y_root, y_rs = sem("y_sq_ready"), sem("y_out"), sem("y_acc"), sem("y_ss_done"), sem("y_root"), sem("y_rs")
        y_turned, y_stored, y_loaded = sem("y_turned"), sem("y_stored"), sem("y_loaded")
        y_tok_ready = [sem("y_tok_vector"), sem("y_tok_scalar")]
        h_a_ready, h_vector_ready, h_pool_ready = sem("h_a_ready"), sem("h_vector_ready"), sem("h_pool_ready")
        h_hi_ready, h_lo_ready, h_sq_ready, h_sum = sem("h_hi_ready"), sem("h_lo_ready"), sem("h_sq_ready"), sem("h_sum")
        h_sum_pool = sem("h_sum_pool")
        h_ss_done, h_root, h_rs = sem("h_ss_done"), sem("h_root"), sem("h_rs")
        gain_b_in, x_tok_in, h_tok_ready = sem("gain_b_in"), sem("x_tok_in"), sem("h_tok_ready")
        up_scaled, up_tap2, up_tap1, up_tap0, gelu_ready = sem("up_scaled"), sem("up_tap2"), sem("up_tap1"), sem("up_tap0"), sem("gelu_ready")
        g_f_ready, g_hi_ready, g_ready = sem("g_f_ready"), sem("g_hi_ready"), sem("g_ready")
        dn_first_done, dn_squared, dn_scaled, dn_ss_sum, dn_root, dn_rs = sem("dn_first_done"), sem("dn_squared"), sem("dn_scaled"), sem("dn_ss_sum"), sem("dn_root"), sem("dn_rs")
        out_vector, out_normed, out_pool, out_stored = sem("out_vector"), sem("out_normed"), sem("out_pool"), sem("out_stored")

        from_start = (scores_done, ya_ready, zt_ready, g_f_ready, g_ready, z_ready, tanh_o_ready, tanh_a_ready, hm_root,
                      wa_gated, att_prob_t, att_yb, att_mixed, y_sq_ready, y_out, up_scaled)

        block = ctx.enter_context(nc.Block())

        def chunks_of(e):
            return (1, 2) if e % 2 == 0 else (3, 4)

        def window(c):
            return (N_META, CHUNK) if c == 1 else (N_META + CHUNK * (c - 2), 2 * CHUNK)

        def h_added(engine, k):
            if k in H_VECTOR:
                engine.wait_ge(h_vector_ready, H_VECTOR.index(k) + 1)
            else:
                engine.wait_ge(h_pool_ready, H_POOL.index(k) + 1)

        @block.sync
        def _(sp):
            sp.dma_start(xs[0:N_META, 2, :], x[0, 2 * P - N_META:SEQ, :]).then_inc(x_in[2], 16)
            sp.dma_start(xs[0:N_META, 0, :], meta).then_inc(x_in[0], 16)
            sp.dma_start(xs[N_META:P, 0, :], x[0, 0:P - N_META, :]).then_inc(x_in[0], 16)
            for n, gain in enumerate((g_pre_mix[0], g_post_mix[0], g_pre_ffn[0])):
                sp.dma_start(gain_rows[16 * n:16 * n + 16, :], gain.rearrange("(m p) -> m p", p=P)).then_inc(gain_in, 16)
            sp.dma_start(gain_rows[48:64, :], mh_norm[0].rearrange("h (c p) -> (h c) p", p=P)).then_inc(gain_in, 16)
            sp.dma_start(xs[:, 1, :], x[0, P - N_META:2 * P - N_META, :]).then_inc(x_in[1], 16)
            sp.dma_start(wg[:], w_in[0, :, C_GATE:C_MO].rearrange("(t p) n -> p t n", p=P)).then_inc(wg_in, 16)

            def units_of(u0, w, col, col2=None):
                for q in range(KT // UK):
                    rows = w[q * UK * P:(q + 1) * UK * P, :]
                    dst = raw[:, q, :].rearrange("p (t n) -> p t n", t=UK)
                    sp.wait_ge(lo_done, u0 + q + 1)
                    nc.sync.sem_inc(sp_held, 1)
                    if col2 is None:
                        sp.dma_start(dst, rows[:, bass.ds(col, BLK)].rearrange("(t p) n -> p t n", p=P)).then_inc(raw_full[q], 16)
                    else:
                        for n, c in enumerate((col, col2)):
                            sp.dma_start(dst[:, :, n * P:(n + 1) * P],
                                         rows[:, bass.ds(c, P)].rearrange("(t p) n -> p t n", p=P)).then_inc(raw_full[q], 16)

            w = w_in[0]
            with sp.Fori(0, M_HEADS) as h:
                units_of(h * 16 + U_M, w, h * P + C_Q, h * P + C_K)
                units_of(h * 16 + U_M + 4, w, h * BLK + C_V)
                units_of(h * 16 + U_M + 8, w, h * BLK + C_MO)
                units_of(h * 16 + U_M + 12, w, h * BLK + C_GA)
            units_of(U_KV, w, C_AV, C_AV + P)
            units_of(U_KV + 4, w, C_AK)
            with sp.Fori(0, A_KV) as g:
                units_of(g * 16 + U_AW, w, g * (2 * BLK) + C_AQ)
                units_of(g * 16 + U_AW + 4, w, g * (2 * BLK) + C_AQ + BLK)
                units_of(g * 16 + U_AW + 8, w_a[0], g * (2 * BLK))
                units_of(g * 16 + U_AW + 12, w_a[0], g * (2 * BLK) + BLK)
            with sp.Fori(0, 4) as i:
                units_of(i * 16 + U_P2, w, i * (2 * BLK) + C_GB)
                units_of(i * 16 + U_P2 + 4, w, i * (2 * BLK) + C_GB + BLK)
                units_of(i * 16 + U_P2 + 8, w_b[0], i * (2 * BLK))
                units_of(i * 16 + U_P2 + 12, w_b[0], i * (2 * BLK) + BLK)
            with sp.Fori(0, 8) as i:
                units_of(i * 4 + U_WO, w_out[0], i * BLK)
            with sp.Fori(0, FT // 2) as i:
                units_of(i * 8 + U_UP, w_up[0], i * BLK)
                units_of(i * 8 + U_UP + 4, w_up[0], i * BLK + D_FF)
            with sp.Fori(0, DN_BLOCKS // 2) as i:
                for k in range(2 * DN_U):
                    b, q = divmod(k, DN_U)
                    src = w_down[0][q * DN_K * P:(q + 1) * DN_K * P, bass.ds(i * 1024 + b * 512, 512)]
                    sp.wait_ge(lo_done, i * (2 * DN_U) + U_DN + k + 1)
                    nc.sync.sem_inc(sp_held, 1)
                    sp.dma_start(raw[:, k % RING, :].rearrange("p (t n) -> p t n", t=DN_K),
                                 src.rearrange("(t p) n -> p t n", p=P)).then_inc(raw_full[k % RING], 16)
            for n, (who, tok, q) in enumerate(OUT_ORDER):
                cols = slice(q * 512, q * 512 + 512)
                if who == "vector":
                    sp.wait_ge(out_vector, OUT_VECTOR.index((tok, q)) + 1)
                else:
                    sp.wait_ge(out_pool, OUT_POOL.index((tok, q)) + 1)
                src = (h_tok if who == "vector" else y_dn)[:, tok, cols]
                sp.dma_start(out[0, tok * P:(tok + 1) * P, cols], src).then_inc(out_stored, 16)
            sp.wait_ge(out_stored, len(OUT_ORDER) * 16)

        @block.gpsimd
        def _(pool):
            nc.gpsimd.memset(ident[:], 0.0).then_inc(zero_ready, 1)
            nc.gpsimd.memset(mask[:], 0.0).then_inc(zero_ready, 1)
            nc.gpsimd.memset(cst[:, 0:1], EPS).then_inc(const_ready, 1)
            nc.gpsimd.memset(cst[:, 1:2], 1.0).then_inc(const_ready, 1)
            pool.wait_ge(zero_ready, 1)
            nc.gpsimd.affine_select(out=ident[:], in_=ident[:], compare_op=ALU.not_equal, fill=1.0, base=0,
                                    pattern=[[-1, P]], channel_multiplier=1).then_inc(const_ready, 1)
            nc.gpsimd.memset(ones[:], 1.0).then_inc(const_ready, 1)
            nc.gpsimd.memset(wg_hi[:].bitcast(F32), 0.0).then_inc(wg_zeroed, 1)
            nc.gpsimd.memset(wg_lo[:].bitcast(F32), 0.0).then_inc(wg_zeroed, 1)
            nc.gpsimd.memset(neg_cut[:].bitcast(F32), 0.0).then_inc(rows_zeroed, 1)
            nc.gpsimd.memset(m_cut[:].bitcast(F32), 0.0).then_inc(rows_zeroed, 1)
            for s in from_start:
                nc.gpsimd.sem_inc(s, START)
            pool.wait_ge(const_ready, 3)
            nc.gpsimd.tensor_tensor(picks[:], ident[0:RC, 0:M_HEADS], ident[0:RC, 32:RC], ALU.add).then_inc(picks_ready, 1)
            pool.wait_ge(picks_ready, 1)
            pool.wait_ge(zero_ready, 2)
            nc.gpsimd.affine_select(out=mask[:], in_=mask[:], compare_op=ALU.is_ge, fill=NEG, base=0,
                                    pattern=[[1, T]], channel_multiplier=-1).then_inc(const_ready, 1)
            pool.dma_start(bias_rows[0:32, :], b_in[0, 0:C_GATE].rearrange("(m p) -> m p", p=P)).then_inc(bias_in, 16)
            pool.dma_start(bias_rows[32:B_ALL, :], b_in[0, C_MO:].rearrange("(m p) -> m p", p=P)).then_inc(bias_in, 16)
            with nc.allow_non_contiguous_dma(reason="16 biases of the gates, once"):
                pool.dma_start(small[0:8, 0:1], b_in[0, C_GATE:C_GATE + 8].rearrange("(p a) -> p a", a=1)).then_inc(bias_in, 16)
                pool.dma_start(small[32:40, 0:1], b_in[0, C_GATE + 8:C_MO].rearrange("(p a) -> p a", a=1)).then_inc(bias_in, 16)
            pool.dma_start(conv_rows[:, 0:3, :], conv_w[0].rearrange("j (m p) -> m j p", p=P)).then_inc(conv_in, 16)
            pool.dma_start(conv_rows[:, 3, :], conv_b[0].rearrange("(m p) -> m p", p=P)).then_inc(conv_in, 16)
            pool.wait_ge(wg_hi_ready, 2)
            nc.gpsimd.tensor_tensor(wg_lo[:, :, 0:8], wg[:, :, 0:8], wg_hi[:, :, 0:8].bitcast(F32), ALU.subtract).then_inc(wg_ready, 1)
            nc.gpsimd.tensor_tensor(wg_lo[:, :, 32:40], wg[:, :, 8:16], wg_hi[:, :, 32:40].bitcast(F32), ALU.subtract).then_inc(wg_ready, 1)
            for k in range(RING):
                pool.wait_ge(hi_done, k + 1)
                nc.gpsimd.tensor_tensor(w_lo[:, k, :], raw[:, k, :], w_hi[:, k, :].bitcast(F32), ALU.subtract).then_inc(lo_done, 1)
            pool.wait_ge(u_row_ready, 1)
            pool.dma_start(u_scratch, u_row[:]).then_inc(u_stored, 16)
            pool.wait_ge(u_stored, 16)
            with nc.allow_non_contiguous_dma(reason="2176 values of the gates, once"):
                for st, w in ((0, P), (1, P), (2, N_META)):
                    pool.dma_start(u_col[0:w, st, :], u_scratch[:, st * P:st * P + w].rearrange("h p -> p h")).then_inc(u_col_in, 16)
            with pool.Fori(0, M_HEADS) as h:
                pool.wait_ge(scores_done, h + START)
                nc.gpsimd.tensor_copy(sel[:], picks[:, bass.ds(h, 1)].to_broadcast([RC, P])).then_inc(sel_ready, 1)
                pool.wait_ge(tanh_o_ready, h + 1 + START)
                nc.gpsimd.sem_inc(pool_held, 1)
                nc.gpsimd.tensor_scalar(sig_o[:], sig_o[:], 0.5, 0.5, ALU.mult, ALU.add).then_inc(sig_o_ready, 1)
                pool.wait_ge(hm_sq_ready, h + 1)
                nc.gpsimd.tensor_tensor(hm_ss[:], hm_sq[:, 0, :], hm_sq[:, 1, :], ALU.add).then_inc(hm_ss_ready, 1)
                pool.wait_ge(normed_ready, h + 1)
                pool.wait_ge(sig_o_ready, h + 1)
                nc.gpsimd.tensor_tensor(hm_sq[:], hm_sq[:], sig_o[:], ALU.mult).then_inc(ya_f_ready, 1)
                pool.wait_ge(ya_f_ready, h + 1)
                hi = ya_hi[:, bass.ds(h * 2, 2), :]
                nc.gpsimd.tensor_copy(hi, hm_sq[:]).then_inc(ya_hi_ready, 1)
                pool.wait_ge(ya_hi_ready, h + 1)
                nc.gpsimd.tensor_tensor(ya_lo[:, bass.ds(h * 2, 2), :], hm_sq[:], hi.bitcast(F32), ALU.subtract).then_inc(ya_ready, 1)

            pool.wait_ge(v_win_ready, 4)
            pool.wait_ge(k_dup_ready, 1)
            with pool.Fori(0, A_KV) as g:
                pool.wait_ge(att_mixed, g * STEPS + START)
                for n in range(3):
                    pieces = [(0, 0, KW)] if n == 0 else [(n * KW, 0, N_META), (n * KW + N_META, window(n + 2)[0], P)]
                    for to, t0, w in pieces:
                        nc.gpsimd.tensor_copy(k_group[:, to:to + w], k_dup[:, bass.ds(g, 1), t0:t0 + w].rearrange("p g n -> p (g n)")).then_inc(v_group_ready, 1)
                nc.gpsimd.tensor_copy(v_group[:], v_win[:, bass.ds(g, 1), :, :].rearrange("p g w d -> p (g w) d")).then_inc(v_group_ready, 1)
                for n, k in enumerate(POOL_STEPS):
                    u = g * 16 + U_AW + k + RING
                    pool.wait_ge(hi_done, u + 1)
                    pool.wait_ge(lo_done, u + RING)
                    nc.gpsimd.sem_inc(pool_held, 1)
                    slot = k % RING
                    nc.gpsimd.tensor_tensor(w_lo[:, slot, :], raw[:, slot, :], w_hi[:, slot, :].bitcast(F32), ALU.subtract).then_inc(lo_done, 1)
                    if n == 0:
                        pool.wait_ge(q_pairs_ready, g * 2 + 2)
                        nc.gpsimd.sem_inc(pool_held, 1)
                        nc.gpsimd.tensor_copy(q_meta[:], q_pairs[:, :, 0:2].rearrange("p j t -> p t j")).then_inc(q_meta_ready, 1)

            with pool.Fori(0, 4) as i:
                for m in range(4):
                    n = i * 4 + m + 1
                    t = bass.ds(i * 4 + m, 1)
                    zf = zt[:, m:m + 1, :]
                    pool.wait_ge(zt_ready, n + START)
                    nc.gpsimd.tensor_tensor(zf, zf, z1[:, t, :], ALU.add).then_inc(z_f_ready, 1)
                    pool.wait_ge(z_f_ready, n)
                    nc.gpsimd.tensor_copy(z_hi[:, t, :], zf).then_inc(z_hi_ready, 1)
                    pool.wait_ge(z_hi_ready, n)
                    nc.gpsimd.tensor_tensor(z_lo[:, t, :], zf, z_hi[:, t, :].bitcast(F32), ALU.subtract).then_inc(z_ready, 1)

            pool.wait_ge(z_ready, 16 + START)
            nc.gpsimd.memset(ss_acc[:], 0.0).then_inc(y_acc, 1)
            with pool.Fori(0, 7) as i:
                for m in range(2):
                    pool.wait_ge(y_sq_ready, i * 2 + m + 1 + START)
                    pool.wait_ge(y_acc, i * 2 + m + 1)
                    nc.gpsimd.tensor_tensor(ss_acc[:], ss_acc[:], y_sq[:, m, :], ALU.add).then_inc(y_acc, 1)

            for k in H_POOL:
                pool.wait_ge(h_a_ready, k + 1)
                hk = xt[:, k, QO:T]
                nc.gpsimd.tensor_tensor(hk, hk, h_a[:, k % 4, :], ALU.add).then_inc(h_pool_ready, 1)
            pool.wait_ge(y_tok_ready[0], 3)
            pool.wait_ge(y_tok_ready[1], 5)
            pool.dma_start(y_scratch, y_tok_st[:]).then_inc(y_stored, 16)
            pool.wait_ge(h_sq_ready, 4)
            nc.gpsimd.tensor_tensor(z1[:, 8:12, :], z1[:, 8:12, :], z1[:, 12:16, :], ALU.add).then_inc(h_sum_pool, 1)

            pool.wait_ge(y_stored, 16)
            pool.wait_ge(h_ss_done, 1)
            with pool.Fori(0, FT // 2) as i:
                pool.wait_ge(gelu_ready, i * 2 + 2)
                pool.wait_ge(up_tap0, i * 4 + 4)
                t = bass.ds(i * 2, 2)
                nc.gpsimd.tensor_tensor(ge_t[:], ge_t[:], c_t[:, 2:4, :], ALU.mult).then_inc(g_f_ready, 1)
                pool.wait_ge(g_f_ready, i + 1 + START)
                nc.gpsimd.tensor_copy(g_hi[:, t, :], ge_t[:]).then_inc(g_hi_ready, 1)
                pool.wait_ge(g_hi_ready, i + 1)
                nc.gpsimd.tensor_tensor(g_lo[:, t, :], ge_t[:], g_hi[:, t, :].bitcast(F32), ALU.subtract).then_inc(g_ready, 1)

            pool.wait_ge(unit_done, RING + U_DN)
            pool.dma_start(h_tok[:], y_scratch).then_inc(y_loaded, 16)
            pool.wait_ge(unit_done, RING + U_DN + 7)
            pool.dma_start(gain_b[:], g_post_ffn[0].partition_broadcast(P)).then_inc(gain_b_in, 16)
            pool.wait_ge(g_ready, FT // 2 + START)
            for tok in range(2):
                pool.wait_ge(unit_done, RING + U_DN + 14 + 7 * tok)
                pool.dma_start(x_tok[:, tok, :], x[0, tok * P:(tok + 1) * P, :]).then_inc(x_tok_in, 16)

            for n, (tok, q) in enumerate(OUT_POOL):
                cols = slice(q * 512, q * 512 + 512)
                pool.wait_ge(out_normed, n + 1)
                nc.gpsimd.tensor_tensor(y_dn[:, tok, cols], y_dn[:, tok, cols], h_tok[:, tok, cols], ALU.add).then_inc(out_pool, 1)

        @block.scalar
        def _(act):
            act.wait_ge(const_ready, 1)
            nc.scalar.activation(small[:, 46:47], EPS_C, ACT.Sqrt)
            for n, (c, w) in enumerate((CHUNKS[2], CHUNKS[0], CHUNKS[1])):
                act.wait_ge(x_in[c], 32 if c == 0 else 16)
                nc.scalar.activation(sq_junk[0:w, :], xs[0:w, c, :], ACT.Square,
                                     accum_out=small[0:w, 8 + c:9 + c]).then_inc(sum_sq, 1)
                act.wait_ge(sum_sq, n + 1)
                nc.scalar.activation(small[0:w, 16 + c:17 + c], small[0:w, 8 + c:9 + c], ACT.Sqrt, scale=1.0 / D,
                                     bias=cst[0:w, 0:1]).then_inc(root_ready, 1)
            act.wait_ge(rs_ready, 3)
            for q in (1, 3):
                cols = slice(q * 512, q * 512 + 512)
                nc.scalar.activation(xn_tok[1][:, cols], xs[:, 1, cols], ACT.Copy, scale=small[:, 21:22]).then_inc(xn_scalar, 1)
            act.wait_ge(wg_in, 16)
            act.wait_ge(wg_zeroed, 2)
            nc.scalar.copy(wg_hi[:, :, 0:8], wg[:, :, 0:8]).then_inc(wg_hi_ready, 1)
            nc.scalar.copy(wg_hi[:, :, 32:40], wg[:, :, 8:16]).then_inc(wg_hi_ready, 1)
            act.wait_ge(gains_ready, 1)

            def hi(u, s, n):
                act.wait_ge(raw_full[s], n * 16)
                act.wait_ge(unit_done, u + 1)
                nc.scalar.copy(w_hi[:, s, :], raw[:, s, :]).then_inc(hi_done, 1)

            def split(i, u0, per, k):
                u = k + RING
                if u0 == U_M:
                    loads = i * 5 + 1 + u // RING + 1 + (u // 16)
                else:
                    loads = i * (per // RING) + (u0 + u) // RING + 1 + M_HEADS + 1
                hi(i * per + u0 + u, u % RING, loads)

            for k in range(KT):
                act.wait_ge(xn_turned, k + 1)
                nc.scalar.activation(xn_hi[:, k, :], ps_g[:, k % 4, 0:T], ACT.Copy,
                                     scale=gains[:, G_PRE_MIX + k:G_PRE_MIX + k + 1]).then_inc(xn_hi_ready, 1)
                if k in (1, 3, 5, 7):
                    hi(k // 2, k // 2, 2)
            act.wait_ge(f_neg_ready, 1)
            nc.scalar.activation(f_soft[:], f_neg[:], ACT.Exp).then_inc(exp_f_ready, 1)
            act.wait_ge(exp_f_ready, 1)
            nc.scalar.activation(f_soft[:], f_soft[:], ACT.Ln, bias=cst[0:M_HEADS, 1:2]).then_inc(soft_ready, 1)

            with act.Fori(0, M_HEADS) as h:
                for k in range(16):
                    split(h, U_M, 16, k)
                    if k == 4:
                        act.wait_ge(scores_done, h + 1 + START)
                        nc.scalar.activation(em[:], X2[:, 0:NQ], ACT.Exp, scale=-1.0).then_inc(em_ready, 1)
                        act.wait_ge(expo_ready, h + 1)
                        act.wait_ge(u_col_in, 48)
                        for st, c0, c1, w in ((0, 0, SP1, P), (1, SP1, SP2, P), (2, SP2, SP2 + 16, N_META)):
                            nc.scalar.activation(probs[0:w, c0:c1], probs[0:w, c0:c1], ACT.Exp,
                                                 bias=u_col[0:w, st, bass.ds(h, 1)]).then_inc(decay_ready, 1)
                    if k == 8:
                        act.wait_ge(v_turned, h + 1)
                        nc.scalar.copy(v_tok[:], X3[:, :].rearrange("p (s v) -> p s v", s=2)).then_inc(v_tok_ready, 1)
                        nc.scalar.copy(v_tok2[:], X2[0:N_META, 0:BLK]).then_inc(v_tok_ready, 1)
                    if k == 11:
                        act.wait_ge(unit_done, h * 16 + U_M + k + 1 + RING)
                        act.wait_ge(ya_ready, h + START)
                        for m in range(2):
                            last = nc.scalar.activation(sig_o[:, m, :], ps_g[:, m, 0:NQ], ACT.Tanh, scale=0.5,
                                                        bias=half_bias[:, bass.ds(h * 2 + B_MO + m, 1)])
                        last.then_inc(tanh_o_ready, 1)
                        act.wait_ge(hm_ready, h + 1)
                        nc.scalar.activation(hm_sq[:], hm[:], ACT.Square).then_inc(hm_sq_ready, 1)
                    if k == 14:
                        act.wait_ge(hm_ss_done, h + 1)
                        nc.scalar.activation(rs_m[:], X0[:, 0:NQ], ACT.Sqrt, scale=1.0 / BLK, bias=EPS_C).then_inc(hm_root, 1)
                    if k == 15:
                        act.wait_ge(unit_done, h * 16 + U_M + k + 1 + RING)
                        for m in range(2):
                            last = nc.scalar.activation(z1[:, bass.ds(h * 2 + m, 1), :], ps_g[:, 2 + m:3 + m, 0:NQ], ACT.Tanh, scale=0.5,
                                                        bias=half_bias[:, bass.ds(h * 2 + B_GA + m, 1)])
                        last.then_inc(tanh_a_ready, 1)

            for k in range(8):
                split(0, U_KV, 8, k)
                if k == 0:
                    act.wait_ge(ya_ready, M_HEADS + START)
                    with nc.allow_non_contiguous_dma(reason="sinks, once"):
                        for par in range(2):
                            act.dma_start(sink_col[64 * par:64 * par + 64, :],
                                          sinks[0].rearrange("(j a) -> a j", a=2)[par].partition_broadcast(64)).then_inc(sinks_in, 16)
                        for tok in range(2):
                            act.dma_start(sink_meta[4 * tok:4 * tok + 4, :, :],
                                          sinks[0].rearrange("(g j a) -> j g a", j=4, a=2)).then_inc(sinks_in, 16)
                if k == 5:
                    act.wait_ge(av_turned, 1)
                    for t in range(2):
                        ps = ps_x[t][:, :].rearrange("p (w g d) -> p g w d", w=4, g=2)
                        for g in range(2):
                            nc.scalar.copy(v_win[:, 2 * t + g, :, :], ps[:, g, :, :]).then_inc(v_win_ready, 1)

            def softmax(g, e):
                n = g * STEPS + e + 1
                act.wait_ge(att_nm, n)
                if e < 8:
                    for c in range(2):
                        w = N_META + window(chunks_of(e)[c])[1]
                        nc.scalar.activation(probs_a[:, e % 2, c, 0:w], ps_x[e % 2][:, 144 * c:144 * c + w], ACT.Exp,
                                             bias=att[:, 2 + c:3 + c], accum_out=att[:, 4 + c:5 + c])
                    nc.scalar.activation(att[:, 6:8], att[:, 2:4], ACT.Exp,
                                         bias=sink_col[:, bass.ds(g * 4 + e // 2, 1)]).then_inc(att_exp, 1)
                else:
                    for c in range(2):
                        nc.scalar.activation(probs0[:, c, :], ps_x[0][0:8, 16 * c:16 * c + 16], ACT.Exp,
                                             bias=att0[:, 2 + c:3 + c], accum_out=att0[:, 4 + c:5 + c])
                    nc.scalar.activation(att0[:, 6:8], att0[:, 8:10], ACT.Exp).then_inc(att_exp, 1)

            def turn_out(g, e):
                act.wait_ge(att_turned, g * STEPS + e + 1)
                if e < 8:
                    nc.scalar.copy(prob_t[:], X2[:, 0:256].rearrange("p (c n) -> p c n", c=2))
                    c0 = 1 - e % 2
                    nc.scalar.copy(prob_tm[:, c0:2, :], X2[0:N_META, 256 + P * c0:512].rearrange("p (c n) -> p c n", c=2 - c0)).then_inc(att_prob_t, 1)
                else:
                    nc.scalar.copy(prob_t0[:], X2[0:N_META, 0:16]).then_inc(att_prob_t, 1)

            def mix_out(g, e):
                act.wait_ge(att_mixed, g * STEPS + e + 1 + START)
                if e < 8:
                    c0 = chunks_of(e)[0]
                    dst = yb_hi[:, bass.ds(g * 4 + e // 2, 1), 2 + CHUNK * (c0 - 1):2 + CHUNK * (c0 + 1)]
                    nc.scalar.copy(dst, X3[:, 0:P].rearrange("p (a n) -> p a n", a=1)).then_inc(att_yb_hi, 1)
                else:
                    src = X3[:, 256:264].rearrange("p (t j) -> p j t", t=2)
                    nc.scalar.copy(yb_hi[:, bass.ds(g * 4, 4), 0:2], src).then_inc(att_yb_hi, 1)

            with act.Fori(0, A_KV) as g:
                for k in range(16):
                    split(g, U_AW, 16, k)
                    if 7 <= k <= 15:
                        mix_out(g, k - 7)
                    if 6 <= k <= 14:
                        turn_out(g, k - 6)
                    if 4 <= k <= 12:
                        softmax(g, k - 4)

            with act.Fori(0, 4) as i:
                for k in range(16):
                    split(i, U_P2, 16, k)
                    if k in (3, 7):
                        par = k // 4
                        act.wait_ge(unit_done, i * 16 + U_P2 + k + 1 + RING)
                        act.wait_ge(zt_ready, i * 4 + START)
                        for m in range(2):
                            last = nc.scalar.activation(gate_b[:, 2 * par + m, :], ps_g[:, 2 * par + m, 0:NQ], ACT.Tanh, scale=0.5,
                                                        bias=half_bias[:, bass.ds(i * 4 + B_GB + 2 * par + m, 1)])
                        last.then_inc(gate_b_ready, 1)

            nc.scalar.activation(small[:, 46:47], EPS_C, ACT.Sqrt)
            with act.Fori(0, 4) as i:
                for k in range(8):
                    if k not in (3, 7):
                        split(i, U_WO, 8, k)
                    else:
                        par = k // 4
                        act.wait_ge(unit_done, i * 8 + U_WO + k + 1 + RING)
                        act.wait_ge(y_acc, i * 4 + 2 * par + 1)
                        for m in range(2):
                            nc.scalar.activation(y_sq[:, m, :], ps_g[:, 2 * par + m, 0:NQ], ACT.Square, scale=0.5).then_inc(y_sq_ready, 1)
                        for m in range(2):
                            nc.scalar.activation(z1[:, bass.ds(i * 4 + 2 * par + m, 1), :],
                                                 ps_g[:, 2 * par + m:2 * par + m + 1, 0:NQ], ACT.Copy,
                                                 scale=half_gain[:, bass.ds(i * 4 + 2 * par + m, 1)]).then_inc(y_out, 1)
                        split(i, U_WO, 8, k)

            act.wait_ge(y_ss_done, 1)
            nc.scalar.activation(rs1[:], X0[:, 0:NQ], ACT.Sqrt, scale=1.0 / D, bias=EPS_C).then_inc(y_root, 1)
            for k in range(KT):
                h_added(act, k)
                nc.scalar.activation(xn_hi[:, k, 0:NQ], xt[:, k, QO:T], ACT.Copy,
                                     scale=gains[:, G_PRE_FFN + k:G_PRE_FFN + k + 1]).then_inc(h_hi_ready, 1)
                if k >= 5 and k % 2 == 1 and k < 15:
                    n = (k - 5) // 2 + 3
                    tok, quarter = divmod(n, 4)
                    act.wait_ge(y_turned, n + 1)
                    nc.scalar.copy(y_tok_st[:, tok, quarter * 512:quarter * 512 + 512], ps_x[1 + n % 3][:, :]).then_inc(y_tok_ready[1], 1)
            def up_taps(i, par):
                for m in range(2):
                    t = 2 * par + m
                    act.wait_ge(up_scaled, i * 4 + t + 1 + START)
                    tile = bass.ds(i * 2 + par * FT + m, 1)
                    nc.scalar.activation(c_t[:, t, :], u_t[:, t, 2:NQ], ACT.Identity,
                                         scale=conv_t[:, 2, tile], bias=conv_t[:, 3, tile]).then_inc(up_tap2, 1)

            def up_gelu(i):
                act.wait_ge(g_ready, i + START)
                for m in range(2):
                    act.wait_ge(up_tap0, i * 4 + m + 1)
                    nc.scalar.activation(ge_t[:, m, :], c_t[:, m, :], ACT.Gelu_apprx_tanh).then_inc(gelu_ready, 1)

            for k in range(8):
                if k == 0:
                    act.wait_ge(y_ss_done, 2)
                    nc.scalar.activation(small[:, 40:42], X0[:, 300:302], ACT.Sqrt, scale=1.0 / D, bias=EPS_C).then_inc(y_root, 1)
                    act.wait_ge(h_a_ready, KT)
                    act.wait_ge(y_turned, 8)
                if k < 2:
                    for j in (2 * k, 2 * k + 1):
                        nc.scalar.activation(z1[:, 4 * j:4 * j + 4, :], xt[:, 4 * j:4 * j + 4, QO:T], ACT.Square).then_inc(h_sq_ready, 1)
                split(0, U_UP, 8, k)
                if k == 5:
                    act.wait_ge(h_ss_done, 1)
                    nc.scalar.activation(rs2[:], X0[:, 0:NQ], ACT.Sqrt, scale=1.0 / D, bias=EPS_C).then_inc(h_root, 1)
                if k == 5:
                    up_taps(0, 0)
                if k == 7:
                    up_gelu(0)
                    up_taps(0, 1)
            with act.Fori(1, FT // 2) as i:
                for k in range(8):
                    split(i, U_UP, 8, k)
                    if k == 3:
                        act.wait_ge(g_f_ready, i + START)
                        up_taps(i, 0)
                    if k == 4:
                        up_gelu(i)
                    if k == 7:
                        up_taps(i, 1)

            nc.scalar.activation(small[:, 46:47], EPS_C, ACT.Sqrt)
            for b in range(DN_BLOCKS):
                for k in range(b * DN_U, (b + 1) * DN_U):
                    if k < DN_BLOCKS * DN_U - RING:
                        split(0, U_DN, 0, k)
                if b:
                    act.wait_ge(dn_squared, 2 * b)
                for tok in range(2):
                    if b == DN_BLOCKS - 1 and tok == 0:
                        act.wait_ge(dn_first_done, 1)
                    else:
                        act.wait_ge(unit_done, U_DN + (b + 1) * DN_U + RING)
                    nc.scalar.activation(dn_junk[:, tok, :], ps_g[:, 2 * (b % 2) + tok, :], ACT.Square,
                                         accum_out=small[:, 24 + 4 * tok + b:25 + 4 * tok + b]).then_inc(dn_squared, 1)
                    if b == DN_BLOCKS - 1:
                        act.wait_ge(dn_ss_sum, tok + 1)
                        nc.scalar.activation(small[:, 34 + tok:35 + tok], small[:, 32 + tok:33 + tok], ACT.Sqrt, scale=1.0 / D,
                                             bias=EPS_C).then_inc(dn_root, 1)
            act.wait_ge(dn_rs, 2)
            act.wait_ge(dn_scaled, 8)
            for tok, q in OUT_POOL:
                cols = slice(q * 512, q * 512 + 512)
                nc.scalar.activation(y_dn[:, tok, cols], y_dn[:, tok, cols], ACT.Copy, scale=small[:, 36 + tok:37 + tok]).then_inc(out_normed, 1)

        @block.vector
        def _(dve):
            nc.vector.sem_inc(lo_done, RING)
            def reciprocal_root(n, c, w):
                dve.wait_ge(root_ready, n)
                nc.vector.reciprocal(small[0:w, 20 + c:21 + c], small[0:w, 16 + c:17 + c]).then_inc(rs_ready, 1)

            def x_out(c, j):
                dve.wait_ge(x_turned, c * 4 + j + 1)
                nc.vector.tensor_copy(xt[:, 4 * j:4 * j + 4, c * P:(c + 1) * P],
                                      ps_g[:, j, :].rearrange("p (k n) -> p k n", k=4)).then_inc(xt_ready, 1)

            def norm(c, w, cols, ready):
                nc.vector.tensor_scalar(xn_tok[c][0:w, cols], xs[0:w, c, cols], small[0:w, 20 + c:21 + c], None, ALU.mult).then_inc(ready, 1)

            reciprocal_root(1, 2, N_META)
            dve.wait_ge(rs_ready, 1)
            norm(2, N_META, slice(0, D), xn_first)
            x_out(0, 0)
            reciprocal_root(2, 0, P)
            dve.wait_ge(rs_ready, 2)
            norm(0, P, slice(0, D), xn_first)
            x_out(0, 1)
            x_out(0, 2)
            x_out(0, 3)
            reciprocal_root(3, 1, P)
            dve.wait_ge(rs_ready, 3)
            for q in (0, 2):
                norm(1, P, slice(q * 512, q * 512 + 512), xn_vector)
            x_out(1, 0)
            x_out(1, 1)
            dve.wait_ge(gains_turned, 1)
            nc.vector.tensor_copy(gains[:], X0[:, 0:64]).then_inc(gains_ready, 1)
            x_out(1, 2)
            x_out(1, 3)
            def lo(u, s):
                dve.wait_ge(hi_done, u + 1)
                nc.vector.tensor_tensor(w_lo[:, s, :], raw[:, s, :], w_hi[:, s, :].bitcast(F32), ALU.subtract).then_inc(lo_done, 1)

            def split(i, u0, per, k):
                lo(i * per + u0 + k + RING, k % RING)

            for k in range(KT):
                dve.wait_ge(xn_hi_ready, k + 1)
                nc.vector.scalar_tensor_tensor(xn_lo[:, k, :], ps_g[:, k % 4, 0:T], gains[:, G_PRE_MIX + k:G_PRE_MIX + k + 1],
                                               xn_hi[:, k, :].bitcast(F32), ALU.mult, ALU.subtract).then_inc(xn_lo_ready, 1)
                if k == 3:
                    dve.wait_ge(x_turned, 9)
                    nc.vector.tensor_copy(xt[:, :, 2 * P:T], X1[:, 0:KT * N_META].rearrange("p (k n) -> p k n", k=KT)).then_inc(xt_ready, 1)
                    nc.vector.tensor_scalar(half_gain[:], gains[:, G_POST_MIX:G_POST_MIX + KT], 0.5, None, ALU.mult).then_inc(half_ready, 1)
            dve.wait_ge(par_turned, 1)
            nc.vector.tensor_copy(bias_t[:], X0[:, 128:128 + B_ALL]).then_inc(par_ready, 1)
            nc.vector.tensor_copy(conv_t[:], X1[:, 0:8 * FT].rearrange("p (j m) -> p j m", j=4)).then_inc(par_ready, 1)
            dve.wait_ge(par_ready, 1)
            nc.vector.tensor_scalar(half_bias[:], bias_t[:], 0.5, None, ALU.mult).then_inc(half_ready, 1)
            dve.wait_ge(lo_done, 2 * RING)
            dve.wait_ge(gates_done, 1)
            nc.vector.tensor_scalar(f_pre[:], X3[32:40, 0:T], small[32:40, 0:1], None, ALU.add).then_inc(f_ready, 1)
            dve.wait_ge(f_ready, 1)
            nc.vector.scalar_tensor_tensor(f_neg[:], f_pre[:], -1.0, f_pre[:], ALU.mult, ALU.min).then_inc(f_neg_ready, 1)
            nc.vector.tensor_scalar(i_pre[:], X3[0:8, 0:T], small[0:8, 0:1], None, ALU.add).then_inc(pre_ready, 1)
            dve.wait_ge(f_neg_ready, 1)
            nc.vector.tensor_scalar(f_pre[:], f_pre[:], 0.0, None, ALU.min).then_inc(pre_ready, 1)
            dve.wait_ge(soft_ready, 1)
            dve.wait_ge(pre_ready, 2)
            nc.vector.tensor_tensor_scan(b_cum[:], f_pre[:], f_soft[:], 0.0, ALU.add, ALU.subtract).then_inc(b_cum_ready, 1)
            dve.wait_ge(b_cum_ready, 1)
            nc.vector.tensor_tensor(u_row[:], i_pre[:], b_cum[:], ALU.subtract).then_inc(u_row_ready, 1)
            dve.wait_ge(u_row_ready, 1)
            nc.vector.tensor_tensor_scan(u_max[:], u_row[:], u_row[:], 0.0, ALU.max, ALU.max).then_inc(u_max_ready, 1)
            dve.wait_ge(u_max_ready, 1)
            nc.vector.tensor_tensor(m_row[:], b_cum[:], u_max[:], ALU.add).then_inc(m_row_ready, 1)
            dve.wait_ge(rows_zeroed, 2)
            nc.vector.tensor_scalar(neg_cut[0:8, :], u_max[:], -1.0, None, ALU.mult).then_inc(rows_cut, 1)
            dve.wait_ge(m_row_ready, 1)
            nc.vector.tensor_copy(m_cut[0:8, :], m_row[:]).then_inc(rows_cut, 1)
            dve.wait_ge(rows_cut, 2)
            nc.vector.scalar_tensor_tensor(neg_cut[32:40, :], u_max[:], -1.0, neg_cut[0:8, :].bitcast(F32), ALU.mult, ALU.subtract).then_inc(rows_ready, 1)
            nc.vector.tensor_tensor(m_cut[32:40, :], m_row[:], m_cut[0:8, :].bitcast(F32), ALU.subtract).then_inc(rows_ready, 1)

            with dve.Fori(0, M_HEADS) as h:
                for k in range(16):
                    if k not in (3, 7):
                        split(h, U_M, 16, k)
                    if k == 3:
                        dve.wait_ge(unit_done, h * 16 + U_M + k + 1 + RING)
                        nc.vector.tensor_scalar(q_t[:], ps_g[:, 0, 0:NQ], bias_t[:, bass.ds(h + B_Q, 1)], None, ALU.add)
                        nc.vector.tensor_scalar(k_t[:], ps_g[:, 1, 0:T], bias_t[:, bass.ds(h + B_K, 1)], float(P) ** -0.5,
                                                ALU.add, ALU.mult).then_inc(qk_ready, 1)
                        split(h, U_M, 16, k)
                    if k == 4:
                        dve.wait_ge(scores_done, h + 1 + START)
                        dve.wait_ge(const_ready, 5)
                        nc.vector.tensor_tensor(probs[:, 0:SP1], X1[:, 0:NQ], mask[:, QO:T], ALU.add)
                        nc.vector.tensor_tensor(probs[:, SP1:SP2], X1[:, P - QO:NQ], mask[:, 0:T - P], ALU.add)
                        nc.vector.tensor_tensor(probs[0:N_META, SP2:SP2 + 16], X1[0:N_META, 2 * P - QO:NQ], mask[0:N_META, 0:16],
                                                ALU.add).then_inc(expo_ready, 1)
                        dve.wait_ge(decay_ready, h * 3 + 3)
                        nc.vector.tensor_tensor(probs[:, 0:SP2], probs[:, 0:SP2], X0[:, 0:SP2], ALU.mult)
                        nc.vector.tensor_tensor(probs[0:N_META, SP2:SP2 + 16], probs[0:N_META, SP2:SP2 + 16],
                                                X0[0:N_META, SP2:SP2 + 16], ALU.mult).then_inc(probs_ready, 1)
                    if k == 7:
                        dve.wait_ge(unit_done, h * 16 + U_M + k + 1 + RING)
                        for c in range(2):
                            last = nc.vector.tensor_scalar(v_t[:, c, :], ps_g[:, 2 + c, 0:T], bias_t[:, bass.ds(h * 2 + B_V + c, 1)],
                                                           None, ALU.add)
                        last.then_inc(v_t_ready, 1)
                        split(h, U_M, 16, k)
                    if k == 11:
                        dve.wait_ge(heads_done, h + 1)
                        dve.wait_ge(em_ready, h + 1)
                        nc.vector.scalar_tensor_tensor(den_r[:], X3[:, 0:NQ], -1.0, em[:], ALU.mult, ALU.max).then_inc(den_ready, 1)
                        dve.wait_ge(den_ready, h * 2 + 1)
                        nc.vector.tensor_tensor(den_r[:], X3[:, 0:NQ], den_r[:], ALU.max).then_inc(den_ready, 1)
                        dve.wait_ge(den_ready, h * 2 + 2)
                        nc.vector.reciprocal(den_r[:], den_r[:]).then_inc(rden_ready, 1)
                        dve.wait_ge(rden_ready, h + 1)
                        for c, ps in ((0, X1), (1, X2)):
                            last = nc.vector.tensor_tensor(hm[:, c, :], ps[:, 0:NQ], den_r[:], ALU.mult)
                        last.then_inc(hm_ready, 1)
                    if k == 14:
                        dve.wait_ge(hm_root, h + 1 + START)
                        nc.vector.reciprocal(rs_m[:], rs_m[:]).then_inc(hm_rs, 1)
                        dve.wait_ge(hm_rs, h + 1)
                        for c in range(2):
                            last = nc.vector.scalar_tensor_tensor(hm_sq[:, c, :], hm[:, c, :], gains[:, bass.ds(h * 2 + G_MH + c, 1)],
                                                                  rs_m[:], ALU.mult, ALU.mult)
                        last.then_inc(normed_ready, 1)

            dve.wait_ge(ya_ready, M_HEADS + START)
            for k in range(8):
                split(0, U_KV, 8, k)
                if k == 3:
                    dve.wait_ge(unit_done, U_KV + k + 1 + RING)
                    for c in range(2):
                        last = nc.vector.tensor_scalar(av_t[:, c, :], ps_g[:, c, 0:T], bias_t[:, B_AV + c:B_AV + c + 1], None, ALU.add)
                    last.then_inc(av_t_ready, 1)
                if k == 7:
                    dve.wait_ge(unit_done, U_KV + k + 1 + RING)
                    for c in range(2):
                        for half_in in range(2):
                            for half_out in range(2):
                                pi, po = 64 * half_in, 64 * half_out
                                last = nc.vector.tensor_scalar(k_dup[po:po + 64, 2 * c + half_in, :], ps_g[pi:pi + 64, 2 + c, 0:T],
                                                               bias_t[pi:pi + 64, B_AK + c:B_AK + c + 1], float(DH) ** -0.5,
                                                               ALU.add, ALU.mult)
                    last.then_inc(k_dup_ready, 1)
            dve.wait_ge(sinks_in, 64)

            def softmax(g, e):
                n = g * STEPS + e + 1
                dve.wait_ge(att_scored, n)
                if e < 8:
                    ps = ps_x[e % 2]
                    for c in range(2):
                        w = N_META + window(chunks_of(e)[c])[1]
                        last = nc.vector.tensor_reduce(att[:, c:c + 1], ps[:, 144 * c:144 * c + w], AX_X, ALU.max)
                    last.then_inc(att_max, 1)
                    dve.wait_ge(att_max, n)
                    nc.vector.tensor_scalar(att[:, 2:4], att[:, 0:2], sink_col[:, bass.ds(g * 4 + e // 2, 1)], -1.0,
                                            ALU.max, ALU.mult).then_inc(att_nm, 1)
                    dve.wait_ge(att_exp, n)
                    nc.vector.tensor_tensor(att[:, 8:10], att[:, 4:6], att[:, 6:8], ALU.add).then_inc(att_den, 1)
                    dve.wait_ge(att_den, n)
                    nc.vector.reciprocal(att[:, 10:12], att[:, 8:10]).then_inc(att_rec, 1)
                    dve.wait_ge(att_rec, n)
                    for c in range(2):
                        w = N_META + window(chunks_of(e)[c])[1]
                        pr = probs_a[:, e % 2, c, 0:w]
                        last = nc.vector.tensor_scalar(pr, pr, att[:, 10 + c:11 + c], None, ALU.mult)
                    last.then_inc(att_probs, 1)
                else:
                    nc.vector.tensor_reduce(att0[:, 0:2], ps_x[0][0:8, 0:32].rearrange("p (a n) -> p a n", a=2), AX_X,
                                            ALU.max).then_inc(att_max, 1)
                    dve.wait_ge(att_max, n)
                    sk = sink_meta[:, bass.ds(g, 1), :].rearrange("p g a -> p (g a)")
                    nc.vector.tensor_tensor(att0[:, 10:12], att0[:, 0:2], sk, ALU.max).then_inc(att_maxed, 1)
                    dve.wait_ge(att_maxed, g * 2 + 1)
                    nc.vector.tensor_scalar(att0[:, 2:4], att0[:, 10:12], -1.0, None, ALU.mult).then_inc(att_maxed, 1)
                    dve.wait_ge(att_maxed, g * 2 + 2)
                    nc.vector.tensor_tensor(att0[:, 8:10], att0[:, 2:4], sk, ALU.add).then_inc(att_nm, 1)
                    dve.wait_ge(att_exp, n)
                    nc.vector.tensor_tensor(att0[:, 12:14], att0[:, 4:6], att0[:, 6:8], ALU.add).then_inc(att_den, 1)
                    dve.wait_ge(att_den, n)
                    nc.vector.reciprocal(att0[:, 14:16], att0[:, 12:14]).then_inc(att_rec, 1)
                    dve.wait_ge(att_rec, n)
                    for c in range(2):
                        last = nc.vector.tensor_scalar(probs0[:, c, :], probs0[:, c, :], att0[:, 14 + c:15 + c], None, ALU.mult)
                    last.then_inc(att_probs, 1)

            def mix_out(g, e):
                dve.wait_ge(att_yb_hi, g * STEPS + e + 1)
                if e < 8:
                    c0 = chunks_of(e)[0]
                    at = (slice(None), bass.ds(g * 4 + e // 2, 1), slice(2 + CHUNK * (c0 - 1), 2 + CHUNK * (c0 + 1)))
                    nc.vector.tensor_tensor(yb_lo[at], X3[:, 0:P].rearrange("p (a n) -> p a n", a=1), yb_hi[at].bitcast(F32),
                                            ALU.subtract).then_inc(att_yb, 1)
                else:
                    at = (slice(None), bass.ds(g * 4, 4), slice(0, 2))
                    nc.vector.tensor_tensor(yb_lo[at], X3[:, 256:264].rearrange("p (t j) -> p j t", t=2), yb_hi[at].bitcast(F32),
                                            ALU.subtract).then_inc(att_yb, 1)

            with dve.Fori(0, A_KV) as g:
                for k in range(16):
                    if k - 1 in POOL_STEPS:
                        dve.wait_ge(lo_done, g * 16 + U_AW + k + RING + RING)
                    if k % 4 != 3 and k not in POOL_STEPS:
                        split(g, U_AW, 16, k)
                    if k in (3, 7):
                        par = k // 4
                        dve.wait_ge(unit_done, g * 16 + U_AW + k + 1 + RING)
                        for m in range(2):
                            last = nc.vector.tensor_scalar(q_pairs[:, 2 * par + m, :], ps_g[:, 2 * par + m, 0:NQ],
                                                           bias_t[:, bass.ds(g * 4 + B_AQ + 2 * par + m, 1)], None, ALU.add)
                        last.then_inc(q_pairs_ready, 1)
                    if k in (11, 15):
                        par = k // 4 - 2
                        dve.wait_ge(unit_done, g * 16 + U_AW + k + 1 + RING)
                        for m in range(2):
                            zz = z1[:, bass.ds(g * 4 + 2 * par + m, 1), :]
                            last = nc.vector.scalar_tensor_tensor(zz, zz, 1.0, ps_g[:, 2 * par + m:2 * par + m + 1, 0:NQ],
                                                                  ALU.add, ALU.mult)
                        last.then_inc(wa_gated, 1)
                    if 7 <= k <= 15:
                        mix_out(g, k - 7)
                    if 4 <= k <= 12:
                        softmax(g, k - 4)
                    if k % 4 == 3 and k not in POOL_STEPS:
                        split(g, U_AW, 16, k)

            dve.wait_ge(wa_gated, 8 + START)
            with dve.Fori(0, 4) as i:
                for k in range(16):
                    if k not in (11, 15):
                        split(i, U_P2, 16, k)
                    if k in (11, 15):
                        par = k // 4 - 2
                        dve.wait_ge(unit_done, i * 16 + U_P2 + k + 1 + RING)
                        dve.wait_ge(gate_b_ready, i * 2 + 2)
                        dve.wait_ge(z_ready, i * 4 + START)
                        for m in range(2):
                            t = 2 * par + m
                            last = nc.vector.scalar_tensor_tensor(zt[:, t, :], gate_b[:, t, :], 1.0, ps_g[:, t, 0:NQ],
                                                                  ALU.add, ALU.mult)
                            last.then_inc(zt_ready, 1)
                        split(i, U_P2, 16, k)

            with dve.Fori(0, 4) as i:
                for k in range(8):
                    split(i, U_WO, 8, k)

            for n in range(3):
                dve.wait_ge(y_turned, n + 1)
                nc.vector.tensor_copy(y_tok_st[:, 0, n * 512:n * 512 + 512], ps_x[1 + n % 3][:, :]).then_inc(y_tok_ready[0], 1)
            dve.wait_ge(y_root, 1)
            nc.vector.reciprocal(rs1[:], rs1[:]).then_inc(y_rs, 1)
            dve.wait_ge(y_rs, 1)

            def h_lo_tile(k):
                dve.wait_ge(h_hi_ready, k + 1)
                nc.vector.scalar_tensor_tensor(xn_lo[:, k, 0:NQ], xt[:, k, QO:T], gains[:, G_PRE_FFN + k:G_PRE_FFN + k + 1],
                                               xn_hi[:, k, 0:NQ].bitcast(F32), ALU.mult, ALU.subtract).then_inc(h_lo_ready, 1)

            for k in range(KT):
                if k >= 4:
                    h_added(dve, k - 4)
                nc.vector.tensor_tensor(h_a[:, k % 4, :], z1[:, k, :], rs1[:], ALU.mult).then_inc(h_a_ready, 1)
                if k in H_VECTOR:
                    dve.wait_ge(h_a_ready, k + 1)
                    hk = xt[:, k, QO:T]
                    nc.vector.tensor_tensor(hk, hk, h_a[:, k % 4, :], ALU.add).then_inc(h_vector_ready, 1)
                if k >= 2:
                    h_lo_tile(k - 2)
            h_lo_tile(KT - 2)
            h_lo_tile(KT - 1)
            dve.wait_ge(y_root, 2)
            nc.vector.reciprocal(small[:, 42:44], small[:, 40:42]).then_inc(y_rs, 1)

            def up_scale(i, par):
                dve.wait_ge(unit_done, i * 8 + U_UP + 4 * par + 4 + RING)
                for m in range(2):
                    t = 2 * par + m
                    nc.vector.tensor_tensor(u_t[:, t, :], ps_g[:, t, 0:NQ], rs2[:], ALU.mult).then_inc(up_scaled, 1)

            def up_taps(i, par):
                for j in (1, 0):
                    for m in range(2):
                        t = 2 * par + m
                        dve.wait_ge(up_tap2 if j == 1 else up_tap1, i * 4 + t + 1)
                        nc.vector.scalar_tensor_tensor(c_t[:, t, :], u_t[:, t, j:j + SEQ],
                                                       conv_t[:, j, bass.ds(i * 2 + par * FT + m, 1)], c_t[:, t, :],
                                                       ALU.mult, ALU.add).then_inc(up_tap1 if j == 1 else up_tap0, 1)

            for k in range(8):
                if k == 0:
                    dve.wait_ge(h_sq_ready, 2)
                    nc.vector.tensor_tensor(z1[:, 0:4, :], z1[:, 0:4, :], z1[:, 4:8, :], ALU.add).then_inc(h_sum, 1)
                if k == 5:
                    dve.wait_ge(h_root, 1)
                    nc.vector.reciprocal(rs2[:], rs2[:]).then_inc(h_rs, 1)
                    dve.wait_ge(h_rs, 1)
                    up_scale(0, 0)
                split(0, U_UP, 8, k)
                if k == 2:
                    dve.wait_ge(h_sum_pool, 1)
                    for n in (8, 2, 1):
                        w = min(n, 4)
                        dve.wait_ge(h_sum, (8, 2, 1).index(n) + 1)
                        nc.vector.tensor_tensor(z1[:, 0:w, :], z1[:, 0:w, :], z1[:, n:n + w, :], ALU.add).then_inc(h_sum, 1)
                if k == 5:
                    up_taps(0, 0)
                if k == 7:
                    up_scale(0, 1)
                    up_taps(0, 1)
            with dve.Fori(1, FT // 2) as i:
                for k in range(8):
                    if k in (3, 7):
                        up_scale(i, k // 4)
                    split(i, U_UP, 8, k)
                    if k in (3, 7):
                        up_taps(i, k // 4)

            for b in range(DN_BLOCKS):
                for k in range(b * DN_U, (b + 1) * DN_U):
                    if k < DN_BLOCKS * DN_U - RING:
                        split(0, U_DN, 0, k)
                    if b == 2 and k % 2 == 0 and k // 2 - DN_U < 8:
                        tok, quarter = divmod(k // 2 - DN_U, 4)
                        cols = slice(quarter * 512, quarter * 512 + 512)
                        dve.wait_ge(y_loaded, 16)
                        dve.wait_ge(x_tok_in, 32)
                        dve.wait_ge(y_rs, 2)
                        nc.vector.scalar_tensor_tensor(h_tok[:, tok, cols], h_tok[:, tok, cols], small[:, 42 + tok:43 + tok],
                                                       x_tok[:, tok, cols], ALU.mult, ALU.add).then_inc(h_tok_ready, 1)
                dve.wait_ge(gain_b_in, 16)
                for tok in range(2):
                    dve.wait_ge(dn_squared, 2 * b + tok + 1)
                    if b == DN_BLOCKS - 1:
                        nc.vector.tensor_reduce(small[:, 32 + tok:33 + tok], small[:, 24 + 4 * tok:28 + 4 * tok], AX_X, ALU.add).then_inc(dn_ss_sum, 1)
                    cols = slice(512 * b, 512 * b + 512)
                    nc.vector.tensor_tensor(y_dn[:, tok, cols], ps_g[:, 2 * (b % 2) + tok, :], gain_b[:, cols], ALU.mult).then_inc(dn_scaled, 1)
                    if b == DN_BLOCKS - 1:
                        dve.wait_ge(dn_root, tok + 1)
                        nc.vector.reciprocal(small[:, 36 + tok:37 + tok], small[:, 34 + tok:35 + tok]).then_inc(dn_rs, 1)
                        dve.wait_ge(dn_rs, tok + 1)
                        dve.wait_ge(dn_scaled, 2 * b + tok + 1)
                        dve.wait_ge(h_tok_ready, 8)
                        for quarter in (q for t, q in OUT_VECTOR if t == tok):
                            cols = slice(quarter * 512, quarter * 512 + 512)
                            nc.vector.scalar_tensor_tensor(h_tok[:, tok, cols], y_dn[:, tok, cols], small[:, 36 + tok:37 + tok],
                                                           h_tok[:, tok, cols], ALU.mult, ALU.add).then_inc(out_vector, 1)

        @block.tensor
        def _(pe):
            nc.tensor.sem_inc(unit_done, RING)
            pe.wait_ge(const_ready, 3)
            for c in range(2):
                pe.wait_ge(x_in[c], 32 if c == 0 else 16)
                for j in range(4):
                    if c:
                        pe.wait_ge(xt_ready, j + 1)
                    for k in range(4):
                        last = nc.tensor.transpose(ps_g[:, j, k * P:(k + 1) * P], xs[:, c, (4 * j + k) * P:(4 * j + k + 1) * P], ident[:, :])
                    last.then_inc(x_turned, 1)
            pe.wait_ge(x_in[2], 16)
            for k in range(KT):
                last = nc.tensor.transpose(X1[:, k * N_META:(k + 1) * N_META], xs[0:N_META, 2, k * P:(k + 1) * P], ident[0:N_META, 0:N_META])
            last.then_inc(x_turned, 1)

            pe.wait_ge(gain_in, 4 * 16)
            nc.tensor.transpose(X0[:, 0:64], gain_rows[:, :], ident[0:64, 0:64]).then_inc(gains_turned, 1)

            def gates_tile(k):
                pe.wait_ge(xn_lo_ready, k + 1)
                for a, b in ((wg_hi, xn_hi), (wg_hi, xn_lo), (wg_lo, xn_hi)):
                    last = nc.tensor.matmul(X3[0:GC, 0:T], a[:, k, :], b[:, k, :], start=(k == 0 and a is wg_hi and b is xn_hi),
                                            stop=(k == KT - 1 and a is wg_lo))
                if k == KT - 1:
                    last.then_inc(gates_done, 1)

            pe.wait_ge(xn_first, 2)
            for k in range(KT):
                if k % 4 == 0:
                    if k % 8 == 0:
                        pe.wait_ge(xn_vector, k // 8 + 1)
                    else:
                        pe.wait_ge(xn_scalar, k // 8 + 1)
                if k < 4:
                    pe.wait_ge(xt_ready, 4 + k + 1)
                else:
                    pe.wait_ge(xn_lo_ready, k - 3)
                for c, w in CHUNKS:
                    last = nc.tensor.transpose(ps_g[:, k % 4, c * P:c * P + w], xn_tok[c][0:w, k * P:(k + 1) * P], ident[0:w, 0:w])
                last.then_inc(xn_turned, 1)
                if k == 1:
                    pe.wait_ge(wg_ready, 2)
                if k >= 2:
                    gates_tile(k - 2)
            pe.wait_ge(bias_in, 4 * 16)
            pe.wait_ge(conv_in, 2 * 16)
            pe.wait_ge(gains_ready, 1)
            pe.wait_ge(xt_ready, 9)
            nc.tensor.transpose(X0[:, 128:128 + B_ALL], bias_rows[:, :], ident[0:B_ALL, 0:B_ALL])
            for j in range(4):
                last = nc.tensor.transpose(X1[:, j * 2 * FT:(j + 1) * 2 * FT], conv_rows[:, j, :], ident[0:2 * FT, 0:2 * FT])
            last.then_inc(par_turned, 1)
            gates_tile(KT - 2)
            gates_tile(KT - 1)

            def unit(u, q, par, acts, t0=(0, 0), n=(NQ, NQ), ready=None):
                pe.wait_ge(lo_done, u + 1 + RING)
                wh = w_hi[:, q, :].rearrange("p (t n) -> p t n", t=UK)
                wl = w_lo[:, q, :].rearrange("p (t n) -> p t n", t=UK)
                for m in range(2):
                    dst = ps_g[:, 2 * par + m, 0:n[m]]
                    for t in range(UK):
                        k = q * UK + t
                        if ready is not None and m == 0:
                            pe.wait_ge(ready, k + 1)
                        cols = slice(m * P, (m + 1) * P)
                        mh, ml = (a[:, k, t0[m]:t0[m] + n[m]] for a in acts)
                        nc.tensor.matmul(dst, wh[:, t, cols], mh, start=(k == 0), stop=False)
                        nc.tensor.matmul(dst, wh[:, t, cols], ml, start=False, stop=False)
                        last = nc.tensor.matmul(dst, wl[:, t, cols], mh, start=False, stop=(k == KT - 1))
                last.then_inc(unit_done, 1)

            xn, ya, yb, zz = (xn_hi, xn_lo), (ya_hi, ya_lo), (yb_hi, yb_lo), (z_hi, z_lo)
            Q_TOK = dict(t0=(QO, QO), n=(NQ, NQ))
            ALL_TOK = dict(t0=(0, 0), n=(T, T))

            with pe.Fori(0, M_HEADS) as h:
                for k in range(16):
                    b, q = divmod(k, 4)
                    if q == 0:
                        if b == 0:
                            pe.wait_ge(tanh_o_ready, h + START)
                        elif b == 1:
                            pe.wait_ge(tanh_a_ready, h + START)
                        elif b == 2:
                            pe.wait_ge(qk_ready, h + 1)
                        else:
                            pe.wait_ge(v_t_ready, h + 1)
                    toks = (dict(t0=(QO, 0), n=(NQ, T)), ALL_TOK, Q_TOK, Q_TOK)[b]
                    unit(h * 16 + U_M + k, q, b % 2, xn, **toks)
                    if k == 4:
                        pe.wait_ge(qk_ready, h + 1)
                        pe.wait_ge(sel_ready, h + 1)
                        pe.wait_ge(rows_ready, 2)
                        pe.wait_ge(hm_root, h + START)
                        pe.wait_ge(par_ready, 2)
                        nc.tensor.matmul(X0[:, 0:SP1], k_t[:, 0:P], q_t[:, :], start=True, stop=True)
                        nc.tensor.matmul(X0[:, SP1:SP2], k_t[:, P:2 * P], q_t[:, P - QO:NQ], start=True, stop=True)
                        nc.tensor.matmul(X0[0:N_META, SP2:SP2 + 16], k_t[:, 2 * P:T], q_t[:, 2 * P - QO:NQ], start=True, stop=True)
                        nc.tensor.matmul(X1[:, 0:NQ], sel[:, :], neg_cut[:, QO:T], start=True, stop=True)
                        nc.tensor.matmul(X2[:, 0:NQ], sel[:, :], m_cut[:, QO:T], start=True, stop=True).then_inc(scores_done, 1)
                    if k == 8:
                        pe.wait_ge(v_t_ready, h + 1)
                        pe.wait_ge(em_ready, h + 1)
                        for c in range(2):
                            for st in range(2):
                                nc.tensor.transpose(X3[:, st * BLK + c * P:st * BLK + (c + 1) * P], v_t[:, c, st * P:(st + 1) * P], ident[:, :])
                            last = nc.tensor.transpose(X2[0:N_META, c * P:(c + 1) * P], v_t[:, c, 2 * P:T], ident[:, :])
                        last.then_inc(v_turned, 1)
                    if k == 11:
                        pe.wait_ge(v_tok_ready, h * 2 + 2)
                        pe.wait_ge(probs_ready, h + 1)
                        for c, dst in ((0, X1), (1, X2), (2, X3)):
                            w0 = v_tok[:, 0, c * P:(c + 1) * P] if c < 2 else ones[:, :]
                            w1 = v_tok[:, 1, c * P:(c + 1) * P] if c < 2 else ones[:, :]
                            w2 = v_tok2[:, c * P:(c + 1) * P] if c < 2 else ones[0:N_META, :]
                            nc.tensor.matmul(dst[:, 0:NQ], w0, probs[:, 0:SP1], start=True, stop=False)
                            nc.tensor.matmul(dst[:, P - QO:NQ], w1, probs[:, SP1:SP2], start=False, stop=False)
                            last = nc.tensor.matmul(dst[:, 2 * P - QO:NQ], w2, probs[0:N_META, SP2:SP2 + 16], start=False, stop=True)
                        last.then_inc(heads_done, 1)
                    if k == 14:
                        pe.wait_ge(hm_ss_ready, h + 1)
                        nc.tensor.matmul(X0[:, 0:NQ], ones[:, :], hm_ss[:], start=True, stop=True).then_inc(hm_ss_done, 1)

            for k in range(8):
                b, q = divmod(k, 4)
                if q == 0:
                    pe.wait_ge((tanh_o_ready, tanh_a_ready)[b], M_HEADS + START)
                unit(U_KV + k, q, b, xn, **ALL_TOK)
                if k == 5:
                    pe.wait_ge(av_t_ready, 1)
                    pe.wait_ge(hm_root, M_HEADS + START)
                    for t in range(2):
                        for n, w0 in enumerate((0, *(window(c)[0] for c in (2, 3, 4)))):
                            last = nc.tensor.transpose(ps_x[t][:, n * P:(n + 1) * P], av_t[:, t, w0:w0 + P], ident[:, :])
                    last.then_inc(av_turned, 1)

            def hold():
                nc.tensor.sem_inc(pe_held, 1)

            def scores(g, e):
                pe.wait_ge(q_pairs_ready, g * 2 + (1 if e < 4 else 2))
                pe.wait_ge(v_group_ready, g * 6 + 5)
                if e == 8:
                    pe.wait_ge(q_meta_ready, g + 1)
                hold()
                ps = ps_x[e % 2]
                for par in range(2):
                    rows = slice(64 * par, 64 * par + 64)
                    if e < 8:
                        for c in range(2):
                            ch = chunks_of(e)[c]
                            k0, w = max(ch - 2, 0) * KW, N_META + window(ch)[1]
                            qs = q_pairs[rows, e // 2, 2 + CHUNK * (ch - 1):2 + CHUNK * ch]
                            last = nc.tensor.matmul(ps[rows, 144 * c:144 * c + w], qs, k_group[rows, k0:k0 + w], start=True, stop=True)
                    else:
                        if par:
                            last.then_inc(meta_scored, 1)
                            pe.wait_ge(meta_scored, g + 1)
                            hold()
                        last = nc.tensor.matmul(ps[0:8, 16 * par:16 * par + 16], q_meta[rows, :, :].rearrange("p t j -> p (t j)"),
                                                k_group[rows, 0:N_META], start=True, stop=True)
                last.then_inc(att_scored, 1)

            def turn(g, e):
                pe.wait_ge(att_probs, g * STEPS + e + 1)
                if e == 0:
                    pe.wait_ge(att_prob_t, g * STEPS + START)
                hold()
                if e < 8:
                    for c in range(2):
                        w = window(chunks_of(e)[c])[1]
                        if w < P:
                            last = nc.tensor.transpose(X2[0:N_META + w, c * P:(c + 1) * P], probs_a[:, e % 2, c, 0:N_META + w], ident[:, :])
                            continue
                        nc.tensor.transpose(X2[0:w, c * P:(c + 1) * P], probs_a[:, e % 2, c, N_META:N_META + w], ident[:, :])
                        last = nc.tensor.transpose(X2[0:N_META, 256 + c * P:256 + (c + 1) * P], probs_a[:, e % 2, c, 0:N_META], ident[:, :])
                else:
                    for c in range(2):
                        last = nc.tensor.transpose(X2[0:N_META, 8 * c:8 * c + 8], probs0[:, c, :], ident[0:8, 0:8])
                last.then_inc(att_turned, 1)

            def mix(g, e):
                pe.wait_ge(att_prob_t, g * STEPS + e + 1 + START)
                pe.wait_ge(att_yb, g * STEPS + e + START)
                pe.wait_ge(v_group_ready, g * 6 + 6)
                hold()
                for par in range(2):
                    rows = slice(64 * par, 64 * par + 64)
                    if e < 8:
                        both = e % 2 == 1
                        if both:
                            nc.tensor.matmul(X3[rows, 0:P], v_group[0:N_META, 0, :], prob_tm[:, :, rows], start=True, stop=False)
                        for c in range(2):
                            ch = chunks_of(e)[c]
                            w = window(ch)[1]
                            slot = ch - 1
                            dst = X3[rows, CHUNK * c:CHUNK * (c + 1)]
                            if w < P:
                                nc.tensor.matmul(dst, v_group[0:N_META + w, 0, :], prob_t[0:N_META + w, c, rows], start=True, stop=True)
                                continue
                            if not both:
                                nc.tensor.matmul(dst, v_group[0:N_META, 0, :], prob_tm[:, c, rows], start=True, stop=False)
                            last = nc.tensor.matmul(dst, v_group[0:w, slot, :], prob_t[0:w, c, rows], start=False, stop=(c == 1 or not both))
                    else:
                        last = nc.tensor.matmul(X3[rows, 256:264], v_group[0:N_META, 0, :], prob_t0[:, 8 * par:8 * par + 8],
                                                start=True, stop=True)
                last.then_inc(att_mixed, 1)

            pe.wait_ge(av_t_ready, 1)
            with pe.Fori(0, A_KV) as g:
                for k in range(16):
                    b, q = divmod(k, 4)
                    if q == 0:
                        if b < 2:
                            pe.wait_ge(wa_gated, g * 2 - 1 + b + START)
                            if b == 1:
                                pe.wait_ge(k_dup_ready, 1)
                                pe.wait_ge(v_win_ready, 4)
                        else:
                            pe.wait_ge(q_pairs_ready, g * 2 + b - 1)
                    unit(g * 16 + U_AW + k, q, b % 2, xn if b < 2 else ya, **(Q_TOK if b < 2 else {}))
                    if 7 <= k <= 15:
                        mix(g, k - 7)
                    if 6 <= k <= 14:
                        turn(g, k - 6)
                    if 4 <= k <= 12:
                        scores(g, k - 4)

            with pe.Fori(0, 4) as i:
                for k in range(16):
                    b, q = divmod(k, 4)
                    if q == 0:
                        if b < 2:
                            pe.wait_ge(wa_gated, 7 + b + START)
                            pe.wait_ge(zt_ready, i * 4 - 2 + 2 * b + START)
                        else:
                            pe.wait_ge(gate_b_ready, i * 2 + b - 1)
                            pe.wait_ge(att_yb, A_KV * STEPS + START)
                    unit(i * 16 + U_P2 + k, q, b % 2, xn if b < 2 else yb, **(Q_TOK if b < 2 else {}))

            pe.wait_ge(zt_ready, 14 + START)
            with pe.Fori(0, 4) as i:
                for k in range(8):
                    b, q = divmod(k, 4)
                    if b == 0:
                        pe.wait_ge(z_ready, UK * (q + 1) + START)
                    if q == 0:
                        pe.wait_ge(y_out, i * 4 - 2 + 2 * b + START)
                    unit(i * 8 + U_WO + k, q, b, zz)

            def turn_y(n):
                tok, quarter = divmod(n, 4)
                if n >= 6:
                    pe.wait_ge(y_tok_ready[1], n - 5)
                elif n >= 3:
                    pe.wait_ge(y_tok_ready[0], n - 2)
                if n == 3:
                    pe.wait_ge(y_out, KT + START)
                for j in range(4):
                    k = 4 * quarter + j
                    last = nc.tensor.transpose(ps_x[1 + n % 3][:, j * P:(j + 1) * P], z1[:, k, 2 + tok * P:2 + (tok + 1) * P], ident[:, :])
                last.then_inc(y_turned, 1)

            pe.wait_ge(y_out, KT - 4 + START)
            for n in range(3):
                turn_y(n)
            pe.wait_ge(y_acc, KT - 1)
            for n, part in enumerate((ss_acc[:], y_sq[:, 0, :], y_sq[:, 1, :])):
                if n:
                    pe.wait_ge(y_sq_ready, KT - 2 + n + START)
                last = nc.tensor.matmul(X0[:, 0:NQ], ones[:, :], part, start=(n == 0), stop=(n == 2))
            last.then_inc(y_ss_done, 1)
            for n in range(3, 6):
                turn_y(n)
            pe.wait_ge(y_root, 1)
            for tok in range(2):
                for n, part in enumerate((ss_acc, y_sq[:, 0, :], y_sq[:, 1, :])):
                    last = nc.tensor.matmul(X0[:, 300 + tok:301 + tok], part[:, 2 + tok * P:2 + (tok + 1) * P], ones[:, 0:1],
                                            start=(n == 0), stop=(n == 2))
            last.then_inc(y_ss_done, 1)

            pe.wait_ge(y_out, KT + START)
            for k in range(8):
                unit(U_UP + k, k % 4, k // 4, xn, ready=h_lo_ready if k < 4 else None)
                if k in (0, 1):
                    turn_y(6 + k)
                if k == 5:
                    pe.wait_ge(h_sum, 4)
                    pe.wait_ge(y_root, 2)
                    nc.tensor.matmul(X0[:, 0:NQ], ones[:, :], z1[:, 0, :], start=True, stop=True).then_inc(h_ss_done, 1)
            with pe.Fori(1, FT // 2) as i:
                for k in range(8):
                    b, q = divmod(k, 4)
                    if q == 0:
                        pe.wait_ge(up_scaled, i * 4 - 2 + 2 * b + START)
                    unit(i * 8 + U_UP + k, q, b, xn)

            def down(b, q, tok):
                slot = (b * DN_U + q) % RING
                dst = ps_g[:, 2 * (b % 2) + tok, :]
                for t in range(DN_K):
                    f = q * DN_K + t
                    cols = slice(t * 512, (t + 1) * 512)
                    gh, gl = (a[:, f, tok * P:(tok + 1) * P] for a in (g_hi, g_lo))
                    nc.tensor.matmul(dst, gh, w_hi[:, slot, cols], start=(f == 0), stop=False)
                    nc.tensor.matmul(dst, gl, w_hi[:, slot, cols], start=False, stop=False)
                    last = nc.tensor.matmul(dst, gh, w_lo[:, slot, cols], start=False, stop=(f == FT - 1))
                return last

            for b in range(DN_BLOCKS):
                if b < 2:
                    pe.wait_ge(up_scaled, 2 * FT - 2 + 2 * b + START)
                else:
                    pe.wait_ge(dn_squared, 2 * b - 2)
                    pe.wait_ge(dn_scaled, 2 * b - 2)
                split_from = DN_U - RING if b == DN_BLOCKS - 1 else DN_U
                for q in range(split_from):
                    if b == 0:
                        pe.wait_ge(g_ready, q + 1 + START)
                    pe.wait_ge(lo_done, U_DN + b * DN_U + q + 1 + RING)
                    down(b, q, 0)
                    down(b, q, 1).then_inc(unit_done, 1)
            for q in range(DN_U - RING, DN_U):
                pe.wait_ge(lo_done, U_DN + (DN_BLOCKS - 1) * DN_U + q + 1 + RING)
                last = down(DN_BLOCKS - 1, q, 0)
            last.then_inc(dn_first_done, 1)
            for q in range(DN_U - RING, DN_U):
                down(DN_BLOCKS - 1, q, 1).then_inc(unit_done, 1)


_INS = ['x', 'meta', 'w_in', 'b_in', 'mh_norm', 'sinks', 'w_a', 'w_b', 'w_out', 'g_pre_mix', 'g_post_mix',
        'g_pre_ffn', 'g_post_ffn', 'w_up', 'conv_w', 'conv_b', 'w_down']
_OUTS = [((1, SEQ, D), 'float32')]


def kernel(**inputs):
    import numpy as _np
    import concourse.bacc as _bacc
    from concourse import mybir as _mybir
    from concourse.bass_utils import run_bass_kernel_spmd as _run

    nc = _bacc.Bacc("TRN2", target_bir_lowering=False, num_devices=1)
    arrays, args = {}, []
    for name in _INS:
        a = _np.ascontiguousarray(inputs[name])
        arrays[f"in_{name}_dram"] = a
        args.append(nc.dram_tensor(f"in_{name}_dram", a.shape, _mybir.dt.from_np(a.dtype), kind="ExternalInput").ap())
    for i, (shape, dtype) in enumerate(_OUTS):
        dt = _mybir.dt.from_np(_np.dtype(dtype))
        args.append(nc.dram_tensor(f"out_{i}_dram", shape, dt, kind="ExternalOutput").ap())
    layer(nc, *args)
    r = _run(nc, [arrays], core_ids=[0])
    return r.results[0]["out_0_dram"]
```
